# Optimizing a Trainium2 kernel written in Bass

```python
import jax
import jax.numpy as jnp
from jax import lax
import numpy as np

D_MODEL = 1024
BATCH = 1
SEQ = 128
DEPTH = 2
DEC_BATCH = 1
DEC_SEQ = 512
PAST_LEN = 128

GRID_W = 64
EPS = 1e-6
ADA_CHUNKS = 6
GLA_W = D_MODEL // 4
GLA_DK = 64
GLA_DV = 64
GLA_HEADS = GLA_W // GLA_DV
GLA_RANK = 16
GLA_NORMALIZER = 16.0
GLA_CHUNK = 64
CONV_W = D_MODEL // 4
CONV_GROUPS = 4
CONV_K = 31
HEAD_DIM = 64
ATT_W = D_MODEL // 2
ATT_HEADS = ATT_W // HEAD_DIM
ATT_KV_HEADS = 2
ATT_GROUP = ATT_HEADS // ATT_KV_HEADS
Q_BLOCK = 128
ROPE_THETA = 10000.0
MIX_W = GLA_W + CONV_W + ATT_W
IN_SIZES = (GLA_HEADS * GLA_DK, GLA_HEADS * GLA_DK, GLA_W, GLA_W, GLA_RANK, GLA_RANK,
            CONV_W, CONV_W, ATT_W, ATT_KV_HEADS * HEAD_DIM, ATT_KV_HEADS * HEAD_DIM)
IN_COLS = sum(IN_SIZES)
PEER_HEADS = 8
PEER_NKEYS = 128
PEER_EXPERTS = PEER_NKEYS * PEER_NKEYS
PEER_DKEY = 128
PEER_TOPK = 16
TOKEN_BLOCK = 128

kernel_name = 'hymba_gla_conformer_gqa_peer_diffusion_step'

def rms_norm(x, g):
    xf = x.astype(jnp.float32)
    y = xf * lax.rsqrt(jnp.mean(xf * xf, axis=-1, keepdims=True) + EPS)
    return (y * g.astype(jnp.float32)).astype(x.dtype)

def group_layer_norm(u, g, b):
    bsz, t, ch = u.shape
    uf = u.astype(jnp.float32).reshape(bsz, t, CONV_GROUPS, ch // CONV_GROUPS)
    d = uf - jnp.mean(uf, axis=-1, keepdims=True)
    y = (d * lax.rsqrt(jnp.mean(d * d, axis=-1, keepdims=True) + EPS)).reshape(bsz, t, ch)
    return (y * g.astype(jnp.float32) + b.astype(jnp.float32)).astype(u.dtype)

def rope_axis(x, pos):
    m = x.shape[-1] // 2
    freqs = ROPE_THETA ** (-jnp.arange(m, dtype=jnp.float32) / m)
    ang = pos.astype(jnp.float32)[:, None] * freqs[None, :]
    cos = jnp.cos(ang)[None, :, None, :]
    sin = jnp.sin(ang)[None, :, None, :]
    xf = x.astype(jnp.float32)
    x1, x2 = xf[..., :m], xf[..., m:]
    return jnp.concatenate([x1 * cos - x2 * sin, x1 * sin + x2 * cos], axis=-1).astype(x.dtype)

def rope_2d(x):
    t = x.shape[1]
    rows = t // GRID_W
    pos = jnp.arange(rows * GRID_W)
    half = x.shape[-1] // 2
    return jnp.concatenate([rope_axis(x[..., :half], pos // GRID_W),
                            rope_axis(x[..., half:], pos % GRID_W)], axis=-1)

def attend(q, k, v):
    bsz, t = q.shape[:2]
    nb = t // Q_BLOCK
    qb = q.reshape(bsz, nb, Q_BLOCK, ATT_KV_HEADS, ATT_GROUP, HEAD_DIM).transpose(1, 0, 2, 3, 4, 5)

    def block(qi):
        s = jnp.einsum('bqkgd,bskd->bkgqs', qi, k).astype(jnp.float32)
        p = jax.nn.softmax(s, axis=-1).astype(v.dtype)
        return jnp.einsum('bkgqs,bskd->bqkgd', p, v)

    o = lax.map(block, qb)
    return o.transpose(1, 0, 2, 3, 4, 5).reshape(bsz, t, ATT_W)

def gla_chunk_scan(q, k, v, log_a, s0):
    bsz, t, nh, _ = q.shape
    n = t // GLA_CHUNK

    def chunks(z):
        return z.astype(jnp.float32).reshape(bsz, n, GLA_CHUNK, nh, z.shape[-1]).transpose(1, 0, 3, 2, 4)

    qc, kc, vc = chunks(q), chunks(k), chunks(v)
    bc = jnp.cumsum(chunks(log_a), axis=-2)
    lower = jnp.tril(jnp.ones((GLA_CHUNK, GLA_CHUNK), dtype=bool))

    def step(state, inp):
        qi, ki, vi, bi = inp
        q_dec = qi * jnp.exp(bi)
        k_dec = ki * jnp.exp(-bi)
        a = jnp.where(lower, jnp.einsum('bhid,bhjd->bhij', q_dec, k_dec), 0.0)
        o = jnp.einsum('bhij,bhje->bhie', a, vi) + jnp.einsum('bhid,bhde->bhie', q_dec, state)
        b_last = bi[:, :, -1, :]
        state = state * jnp.exp(b_last)[..., None] + jnp.einsum(
            'bhjd,bhje->bhde', ki * jnp.exp(b_last[:, :, None, :] - bi), vi)
        return state, o

    state, o = lax.scan(step, s0.astype(jnp.float32), (qc, kc, vc, bc))
    o = o.transpose(1, 0, 3, 2, 4).reshape(bsz, t, nh, v.shape[-1])
    return o.astype(q.dtype), state

def dwconv(u, w, b):
    ch = u.shape[-1]
    y = lax.conv_general_dilated(u, w[:, None, :].astype(u.dtype), (1,), [(CONV_K // 2, CONV_K // 2)],
                                 dimension_numbers=('NWC', 'WIO', 'NWC'), feature_group_count=ch)
    return y + b

def peer(h, wq, sub_keys, peer_u, peer_v):
    bsz, t, d = h.shape
    flat = h.reshape(-1, TOKEN_BLOCK, d)

    def block(xb):
        n = xb.shape[0]
        qry = (xb @ wq).reshape(n, PEER_HEADS, 2, PEER_DKEY // 2)
        s1 = jnp.einsum('nhd,hkd->nhk', qry[:, :, 0], sub_keys[:, 0]).astype(jnp.float32)
        s2 = jnp.einsum('nhd,hkd->nhk', qry[:, :, 1], sub_keys[:, 1]).astype(jnp.float32)
        v1, i1 = lax.top_k(s1, PEER_TOPK)
        v2, i2 = lax.top_k(s2, PEER_TOPK)
        cand = (v1[..., :, None] + v2[..., None, :]).reshape(n, PEER_HEADS, PEER_TOPK * PEER_TOPK)
        cidx = (i1[..., :, None] * PEER_NKEYS + i2[..., None, :]).reshape(n, PEER_HEADS, PEER_TOPK * PEER_TOPK)
        sc, pos = lax.top_k(cand, PEER_TOPK)
        idx = jnp.take_along_axis(cidx, pos, axis=-1)
        g = jax.nn.softmax(sc, axis=-1)
        act = jax.nn.gelu(jnp.einsum('nd,nhkd->nhk', xb, peer_u[idx]).astype(jnp.float32), approximate=False)
        w = (g * act).astype(xb.dtype)
        return jnp.einsum('nhk,nhkd->nd', w, peer_v[idx])

    return lax.map(block, flat).reshape(bsz, t, d)

def trunk_layer(x, cvec, p, l, ctx):
    bsz, t, _ = x.shape
    m = jax.nn.silu(cvec) @ p['ada_w'][l] + p['ada_b'][l]
    m = m.reshape(m.shape[:-1] + (1, ADA_CHUNKS, D_MODEL))
    shift1, scale1, gate1, shift2, scale2, gate2 = [m[..., i, :] for i in range(ADA_CHUNKS)]

    h = rms_norm(x, p['norm1_g'][l]) * (1 + scale1) + shift1
    proj = h @ p['w_in'][l]
    gq, gk, gv, gg, gaf, gab, cval, cgate, aq, ak, av = jnp.split(
        proj, np.cumsum(IN_SIZES)[:-1].tolist(), axis=-1)

    def heads(z, dh):
        return z.reshape(bsz, t, -1, dh)

    la_f = jax.nn.log_sigmoid((gaf @ p['gla_a_w_f'][l] + p['gla_a_b_f'][l]).astype(jnp.float32)) / GLA_NORMALIZER
    la_b = jax.nn.log_sigmoid((gab @ p['gla_a_w_b'][l] + p['gla_a_b_b'][l]).astype(jnp.float32)) / GLA_NORMALIZER
    qg = heads(gq, GLA_DK) * (GLA_DK ** -0.5)
    kg = heads(gk, GLA_DK)
    vg = heads(gv, GLA_DV)
    if ctx is None:
        s0_f = jnp.zeros((bsz, GLA_HEADS, GLA_DK, GLA_DV), jnp.float32)
        s0_b = s0_f
    else:
        s0_f, s0_b = ctx[2], ctx[3]
    o_f, s_f = gla_chunk_scan(qg, kg, vg, heads(la_f, GLA_DK), s0_f)
    o_b, s_b = gla_chunk_scan(jnp.flip(qg, 1), jnp.flip(kg, 1), jnp.flip(vg, 1),
                              jnp.flip(heads(la_b, GLA_DK), 1), s0_b)
    o_gla = rms_norm(o_f + jnp.flip(o_b, 1), p['gla_norm_g'][l]) * jax.nn.silu(heads(gg, GLA_DV))
    o_gla = o_gla.reshape(bsz, t, GLA_W)

    u = cval * jax.nn.sigmoid(cgate)
    u = dwconv(u, p['conv_w'][l], p['conv_b'][l])
    u = jax.nn.silu(group_layer_norm(u, p['conv_norm_g'][l], p['conv_norm_b'][l]))

    qa = rms_norm(heads(aq, HEAD_DIM), p['q_norm_g'][l])
    ka = rms_norm(heads(ak, HEAD_DIM), p['k_norm_g'][l])
    va = heads(av, HEAD_DIM)
    if ctx is None:
        keys, vals = ka, va
    else:
        qa = rope_2d(qa)
        keys = jnp.concatenate([ctx[0], rope_2d(ka)], axis=1)
        vals = jnp.concatenate([ctx[1], va], axis=1)
    qa = (qa * (HEAD_DIM ** -0.5)).reshape(bsz, t, ATT_KV_HEADS, ATT_GROUP, HEAD_DIM)
    o_att = attend(qa, keys, vals)

    mix = jnp.concatenate([o_gla, u, o_att], axis=-1) @ p['w_out'][l]
    x = x + gate1 * mix
    h2 = rms_norm(x, p['norm2_g'][l]) * (1 + scale2) + shift2
    x = x + gate2 * peer(h2, p['peer_wq'][l], p['peer_keys'][l], p['peer_u'][l], p['peer_v'][l])
    return x, ka, va, s_f.astype(x.dtype), s_b.astype(x.dtype)

def setup_inputs(seed: int = 0) -> dict:
    key = jax.random.key(seed)
    ks = jax.random.split(key, 32)

    def nrm(k, shape, s):
        return jax.random.normal(k, shape, jnp.float32) * s

    def gain(k, shape):
        return 1.0 + 0.02 * jax.random.normal(k, shape, jnp.float32)

    return {
        'x_prompt': nrm(ks[0], (BATCH, SEQ, D_MODEL), 1.0),
        'x_sample': nrm(ks[1], (DEC_BATCH, DEC_SEQ, D_MODEL), 1.0),
        'c': nrm(ks[2], (DEC_BATCH, D_MODEL), 1.0),
        'cache_k': nrm(ks[3], (DEC_BATCH, DEPTH, PAST_LEN, ATT_KV_HEADS, HEAD_DIM), 1.0),
        'cache_v': nrm(ks[4], (DEC_BATCH, DEPTH, PAST_LEN, ATT_KV_HEADS, HEAD_DIM), 1.0),
        'state_gla': nrm(ks[5], (DEC_BATCH, DEPTH, 2, GLA_HEADS, GLA_DK, GLA_DV), 1.0),
        'c_ctx': nrm(ks[6], (D_MODEL,), 1.0),
        'ada_w': nrm(ks[7], (DEPTH, D_MODEL, ADA_CHUNKS * D_MODEL), 0.5 * D_MODEL ** -0.5),
        'ada_b': nrm(ks[8], (DEPTH, ADA_CHUNKS * D_MODEL), 0.02),
        'norm1_g': gain(ks[9], (DEPTH, D_MODEL)),
        'norm2_g': gain(ks[10], (DEPTH, D_MODEL)),
        'w_in': nrm(ks[11], (DEPTH, D_MODEL, IN_COLS), D_MODEL ** -0.5),
        'gla_a_w_f': nrm(ks[12], (DEPTH, GLA_RANK, GLA_HEADS * GLA_DK), GLA_RANK ** -0.5),
        'gla_a_b_f': nrm(ks[13], (DEPTH, GLA_HEADS * GLA_DK), 0.02),
        'gla_a_w_b': nrm(ks[14], (DEPTH, GLA_RANK, GLA_HEADS * GLA_DK), GLA_RANK ** -0.5),
        'gla_a_b_b': nrm(ks[15], (DEPTH, GLA_HEADS * GLA_DK), 0.02),
        'gla_norm_g': gain(ks[16], (DEPTH, GLA_HEADS, GLA_DV)),
        'conv_w': nrm(ks[17], (DEPTH, CONV_K, CONV_W), CONV_K ** -0.5),
        'conv_b': nrm(ks[18], (DEPTH, CONV_W), 0.02),
        'conv_norm_g': gain(ks[19], (DEPTH, CONV_W)),
        'conv_norm_b': nrm(ks[20], (DEPTH, CONV_W), 0.02),
        'q_norm_g': gain(ks[21], (DEPTH, HEAD_DIM)),
        'k_norm_g': gain(ks[22], (DEPTH, HEAD_DIM)),
        'w_out': nrm(ks[23], (DEPTH, MIX_W, D_MODEL), MIX_W ** -0.5),
        'peer_wq': nrm(ks[24], (DEPTH, D_MODEL, PEER_HEADS * PEER_DKEY), D_MODEL ** -0.5),
        'peer_keys': nrm(ks[25], (DEPTH, PEER_HEADS, 2, PEER_NKEYS, PEER_DKEY // 2), (PEER_DKEY // 2) ** -0.5),
        'peer_u': nrm(ks[26], (DEPTH, PEER_EXPERTS, D_MODEL), D_MODEL ** -0.5),
        'peer_v': nrm(ks[27], (DEPTH, PEER_EXPERTS, D_MODEL), 0.5),
    }

def reference(x_prompt, x_sample, c, cache_k, cache_v, state_gla, c_ctx, ada_w, ada_b, norm1_g, norm2_g,
              w_in, gla_a_w_f, gla_a_b_f, gla_a_w_b, gla_a_b_b, gla_norm_g, conv_w, conv_b,
              conv_norm_g, conv_norm_b, q_norm_g, k_norm_g, w_out, peer_wq, peer_keys, peer_u, peer_v):
    p = {'ada_w': ada_w, 'ada_b': ada_b, 'norm1_g': norm1_g, 'norm2_g': norm2_g, 'w_in': w_in,
         'gla_a_w_f': gla_a_w_f, 'gla_a_b_f': gla_a_b_f, 'gla_a_w_b': gla_a_w_b, 'gla_a_b_b': gla_a_b_b,
         'gla_norm_g': gla_norm_g, 'conv_w': conv_w, 'conv_b': conv_b, 'conv_norm_g': conv_norm_g,
         'conv_norm_b': conv_norm_b, 'q_norm_g': q_norm_g, 'k_norm_g': k_norm_g, 'w_out': w_out,
         'peer_wq': peer_wq, 'peer_keys': peer_keys, 'peer_u': peer_u, 'peer_v': peer_v}

    x = x_prompt
    ks_, vs_, sts_ = [], [], []
    for l in range(DEPTH):
        x, k_l, v_l, sf_l, sb_l = trunk_layer(x, c_ctx, p, l, None)
        ks_.append(k_l)
        vs_.append(v_l)
        sts_.append(jnp.stack([sf_l, sb_l], axis=1))
    y_prompt = x
    new_cache_k = jnp.stack(ks_, axis=1)
    new_cache_v = jnp.stack(vs_, axis=1)
    new_state_gla = jnp.stack(sts_, axis=1)

    x = x_sample
    for l in range(DEPTH):
        ctx = (cache_k[:, l], cache_v[:, l], state_gla[:, l, 0], state_gla[:, l, 1])
        x, _, _, _, _ = trunk_layer(x, c, p, l, ctx)
    y_sample = x

    return (y_prompt, y_sample, new_cache_k, new_cache_v, new_state_gla)


_drawn_inputs = setup_inputs


def setup_inputs(seed=0):
    import zlib

    import numpy as np

    out = dict(_drawn_inputs(seed))
    spreads = {}
    factors = {'cache_k': 4.191,
     'cache_v': 3.635,
     'state_gla': 7.217,
     'norm2_g': 3.152,
     'gla_a_b_f': 8.0,
     'gla_a_b_b': 7.613,
     'gla_norm_g': 7.266,
     'conv_b': 5.72,
     'conv_norm_g': 7.351,
     'conv_norm_b': 7.608,
     'q_norm_g': 8.0,
     'k_norm_g': 3.31}
    for name, (base, spread) in spreads.items():
        noise = np.random.default_rng([zlib.crc32(name.encode()), seed]).standard_normal(out[name].shape)
        drawn = base * np.exp(spread * noise) if base else spread * noise
        out[name] = jnp.asarray(drawn.astype(out[name].dtype))
    for name, factor in factors.items():
        out[name] = (out[name] * factor).astype(out[name].dtype)
    return out
```

```python
import numpy as np
import concourse.bass as bass
from concourse import mybir
from contextlib import ExitStack

F32 = mybir.dt.float32
U32 = mybir.dt.uint32
BF16 = mybir.dt.bfloat16
ALU = mybir.AluOpType
ACT = mybir.ActivationFunctionType
AX = mybir.AxisListType

P = 128
D = 1024
KT = D // P
DEPTH = 2
N_SAMPLE, N_PROMPT = 512, 128
NTOK = N_SAMPLE + N_PROMPT
NT = NTOK // P
NT_S = N_SAMPLE // P
CHUNK = 64
NCH = NTOK // CHUNK
TAPS = 31
PAD = TAPS // 2
EPS = 1e-6
NCOLS = 2336
GQ0, GK0, GV0, GG0, GA0, CV0, CG0, AQ0, AK0, AV0 = 0, 256, 512, 768, 1024, 1056, 1312, 1568, 2080, 2208
HEADS, TOPK, NKEYS = 8, 16, 128
EXPERTS = NKEYS * NKEYS
RING = 8
DIAGS = 4

C_ID, C_MEAN, C_ROT, C_DUP, C_MASK, C_COS, C_SIN, C_SCAN, C_SEL, C_IOTA = (
    0, 128, 256, 384, 640, 896, 1408, 1920, 2560, 2816)
C_END = 2832
R_CB, R_CNG, R_CNB, R_GLG, R_ABF, R_ABB, R_QG, R_KG, R_END = 62, 64, 66, 68, 70, 72, 74, 75, 76


def group_of(t):
    return 0 if t < NT_S else 1


def build(nc, x_prompt, x_sample, c, cache_k, cache_v, state_gla, c_ctx, ada_w, ada_b, norm1_g, norm2_g,
          w_in, gla_a_w_f, gla_a_b_f, gla_a_w_b, gla_a_b_b, gla_norm_g, conv_w, conv_b,
          conv_norm_g, conv_norm_b, q_norm_g, k_norm_g, w_out, peer_wq, peer_keys, peer_u, peer_v,
          consts, y_prompt, y_sample, new_k, new_v, new_state):
    ctx = ExitStack()
    with ctx:
        def sb(name, shape, dt=F32):
            return ctx.enter_context(nc.sbuf_tensor(name, shape, dt))

        def sem(name):
            return ctx.enter_context(nc.semaphore(name))

        CST = sb("constants", [P, C_END])
        X = sb("residual", [P, NT, D])
        MOD2 = sb("peer_modulation", [P, 2, 3, D])
        ident = CST[:, C_ID:C_ID + P]
        mean_mat = CST[:, C_MEAN:C_MEAN + P]
        rot_mat = CST[:, C_ROT:C_ROT + P]
        masks = CST[:, C_MASK:C_MASK + 256].rearrange("p (a b) -> p a b", a=2)
        cos_t = CST[:, C_COS:C_COS + N_SAMPLE]
        sin_t = CST[:, C_SIN:C_SIN + N_SAMPLE]
        scan_keep = CST[:, C_SCAN:C_SCAN + NTOK]
        iota16 = CST[:, C_IOTA:C_IOTA + 16]

        cond = sb("cond", [P, 2, KT])
        cond_s = sb("cond_silu", [P, KT, 2])
        sumsq = sb("sumsq", [P, 8])
        rms = sb("rms", [P, 8])
        rstd = sb("rstd", [P, 8])
        vec = sb("vec_columns", [P, R_END])
        eps_c = sb("eps_column", [P, 1])
        gla_w = sb("gla_gate_w", [32, 2, 256])
        e_last = sb("gla_chunk_decay", [P, 4, NCH])
        smax = sb("score_max", [P, 4])
        nmax = sb("score_neg_max", [P, 4])
        psum_p = sb("softmax_sum", [P, 2, 8])
        prec = sb("softmax_rec", [P, 8])
        top_v = sb("top_values", [P, 2, 16])
        top_i = sb("top_indices", [P, 2, 16], U32)
        top_if = sb("top_indices_f", [P, 2, 16])
        best = sb("best_scores", [P, 16])
        pos = sb("best_positions", [P, 16], U32)
        pos2 = sb("best_pos_split", [P, 2, 16], U32)
        pos_f = sb("best_pos_f", [P, 2, 16])
        chosen = sb("chosen_pair", [P, 2, 16])
        chosen_e = sb("chosen_expert", [P, 16])
        idx_u = sb("rows_for_u", [P, 16], U32)
        idx_v = sb("rows_for_v", [P, 16], U32)
        centred = sb("centred_scores", [P, 16])
        gexp = sb("gate_exp", [P, 16])
        gsum = sb("gate_sum", [P, 1])
        grec = sb("gate_rec", [P, 1])
        act_h = sb("expert_act", [P, 16])
        gelu_h = sb("expert_gelu", [P, 16])
        w_h = sb("expert_weight", [P, 16])
        zero_l = sb("zero_lhs", [P, P], BF16)
        zero_r = sb("zero_rhs", [P, 512], BF16)
        A = sb("arena", [P, 37680])

        def at(start, n):
            return A[:, start:start + n]

        def at3(start, a, b):
            return A[:, start:start + a * b].rearrange("p (a b) -> p a b", a=a)

        MOD1 = A[:, 0:6144].rearrange("p (g r d) -> p g r d", g=2, r=3)
        m_row = A[0:2, 6144:12288]
        ada_bias = A[0:2, 12288:18432]
        ada_slab = [at3(18432 + 4096 * i, KT, 512) for i in range(2)]
        gain_row = at3(26624, 2, D)
        HT = at3(6144, KT, NTOK)
        hbuf = at3(11264, 2, D)
        win = [at3(13312 + 1024 * i, KT, P) for i in range(5)]
        w_v = at3(18432, KT, 384)
        CV = at3(21504, 2, NTOK)
        CG = at3(22784, 2, NTOK)
        AQ = at3(24064, 4, NTOK)
        AK = at(26624, NTOK)
        GA = A[0:32, 27264:27904]
        GK = at3(27904, 2, NTOK)
        GQ = at3(29184, 2, NTOK)
        GG = at3(30464, 2, NTOK)
        UPW = N_SAMPLE + N_PROMPT + 4 * PAD
        UP = at3(31744, 2, UPW)
        VT = at3(33144, NT, 384)
        vec_rows = A[0:R_END, 35064:35192]
        MIX = at3(6144, KT, NTOK)
        CX = at3(11264, 2, NTOK)
        SQ = at3(13312, 2, NTOK)
        SD = at3(14592, 2, NTOK)
        RT = at(15872, NTOK)
        KTD = at3(16512, 2, 768)
        KC = at(18048, P)
        CK = at(18176, P)
        CVAL = at(18304, P)
        PR = at3(18432, 2, NTOK)
        PRT = at3(19712, 2, NTOK)
        OTOK = at(20992, 512)
        KOUT = at(12544, P)
        ST = A[:, 11264:16896].rearrange("p (i s e) -> p i s e", i=4, s=11)
        LA = at3(16896, 4, NTOK)
        KK = at3(19456, 4, NTOK)
        QD = at3(22016, 4, NTOK)
        KD = at3(24576, 4, NTOK)
        KKT = A[:, 35064:37624].rearrange("p (i t f) -> p i t f", i=4, t=NT)
        ATM = A[:, 31744:32768].rearrange("p (r h d i) -> p r h d i", r=2, h=2, d=2)
        OG = at3(16896, 2, NTOK)
        OSQ = at3(18176, 2, NTOK)
        OSD = at3(19456, 2, NTOK)
        WOUT = at3(19456, KT, D)
        TMP1 = at(31744, D)
        UR = at3(0, RING, D)
        VR = at3(8192, RING, D)
        WQ = at3(16384, KT, D)
        KEYS = at3(24576, HEADS, 256)
        H2 = at3(26624, 2, D)
        H2T = at3(28672, KT, P)
        QTOK = at(29696, P)
        QT = at(29824, P)
        SCC = at3(29952, 2, NKEYS)
        SC2 = at3(30208, 2, NKEYS)
        CAND = at(30464, 256)
        CAND2 = at(30720, 256)
        OH = at(30976, 512)
        DG = at3(31488, DIAGS, P)
        TMP2 = at(32768, D)
        KRAW = at3(33792, HEADS, P)

        PS = ctx.enter_context(nc.psum_tensor("ps", [P, 8, 512], F32))
        PSF = PS[:, :, :].rearrange("p b n -> p (b n)")

        def pair(i):
            return PSF[:, 1024 * i:1024 * i + 1024]

        S = {n: sem(n) for n in (
            "const_in", "cond_in", "x_in", "adab_in", "gain_in", "vec_in", "wv_in", "misc_in", "st_in", "wout_in",
            "keys_in", "wq_in",
            "cond_ready", "m_ps", "m_row_done", "bc_ps", "bc_act", "bc_dve",
            "ss_done", "ms_done", "sd_done", "h_ready", "ht_ps", "ht_ready", "vec_ps", "vec_ready", "proj_ps",
            "proj_ev", "vt_ps", "vt_ready", "pad_ready",
            "kc_ps", "kc_ready", "cx_mean", "cx_cent", "sq_ready", "var_ps", "sd_ready", "n_ready", "rot_ps",
            "rope_done", "kout_ps", "kout_ready", "silu_done", "dup_ps", "dup_ready",
            "s_ps", "nmax_ready", "p_ready", "pt_ps", "pt_act", "pt_dve", "o_ps", "o_ready", "ot_ps", "ot_ready",
            "z_ps", "abs_done", "ln_done", "b_ready", "ex_done", "el_ready", "qk_ready", "kk_ps", "kk_ready",
            "st_zero", "dS_ps", "st_ready", "a_ps", "atm_ready", "og_ps", "og_sq", "og_var", "og_sd", "og_done",
            "mix_ps", "res_read",
            "keys_zero", "keys_ps", "keys_ready", "ss2_done", "ms2_done", "sd2_done", "h2_ready", "h2t_ps", "h2t_ready",
            "q_ps", "q_ready", "qt_ps", "qt_ready", "sc_ps", "sc_now", "sc_taken", "idx_ready", "idxv_ready", "u_free",
            "v_free", "gelu_done", "w_ready", "diag_ready", "acc_done", "acc_out", "y_ready", "zeros_ready",
            "pool_turn", "dve_turn",
            "out_done", "phase")}
        adaw_in = [sem(f"adaw_in{i}") for i in range(2)]
        win_in = [sem(f"win_in{i}") for i in range(5)]
        u_in = [sem(f"u_in{i}") for i in range(RING)]
        v_in = [sem(f"v_in{i}") for i in range(RING)]
        step_sem = {e: sem(f"{e}_step") for e in ("dve", "act")}

        class Steps:
            def __init__(self, eng, which):
                self.eng, self.sem, self.n = eng, step_sem[which], 0

            def do(self, ins):
                self.n += 1
                ins.then_inc(self.sem, 1)

            def after(self, n):
                self.eng.wait_ge(self.sem, n)

            def link(self, ins):
                self.do(ins)
                self.after(self.n)

        PH = 7

        def phase_end(eng, n):
            eng.drain().then_inc(S["phase"], 1)
            eng.wait_ge(S["phase"], 4 * n)

        BLOCKS = ([(CG[:, 0, :], P, CG0), (CV[:, 0, :], P, CV0), (CG[:, 1, :], P, CG0 + P), (CV[:, 1, :], P, CV0 + P)]
                  + [(AQ[:, j, :], P, AQ0 + P * j) for j in range(4)]
                  + [(AK, P, AK0), (GA, 32, GA0)]
                  + [(GK[:, j, :], P, GK0 + P * j) for j in range(2)]
                  + [(GQ[:, j, :], P, GQ0 + P * j) for j in range(2)]
                  + [(GG[:, j, :], P, GG0 + P * j) for j in range(2)])
        NB = len(BLOCKS)
        BCAST = [(r, g, hf) for r in range(6) for g in range(2) for hf in range(2)]
        NBC = len(BCAST)

        def is_scale(j):
            return BCAST[j][0] in (1, 4)

        N_SC = sum(is_scale(j) for j in range(NBC))
        N_PL = NBC - N_SC

        def mod_dst(j):
            r, g, hf = BCAST[j]
            return (MOD1 if r < 3 else MOD2)[:, g, r % 3, 512 * hf:512 * hf + 512]

        UNITS = ([("q", AQ[:, j, :], R_QG) for j in range(4)] + [("k", AK, R_KG)]
                 + [("c", CX[:, j, :], R_CNG + j) for j in range(2)])
        NU = len(UNITS)
        STEPS = [(t, h) for t in range(NT) for h in range(8)]
        NS = len(STEPS)

        def keys_of(t):
            return (0, NTOK) if t < NT_S else (NTOK, P)

        def vals_of(t):
            return [VT[:, s, 256:384] for s in range(NT_S)] + [CVAL] if t < NT_S else [VT[:, NT_S, 256:384]]

        def updates():
            out = []
            for n in range(9):
                for i in range(4):
                    if i < 2:
                        ch = n if n < 7 else n + 1
                        out.append((i, ch, 10 if ch == 9 else ch + 1))
                    else:
                        ch = 7 - n if n < 7 else 16 - n
                        out.append((i, ch, 10 if ch == 8 else ch - 1))
            return out

        UPD = updates()
        NUPD = len(UPD)
        N_OUT = 10

        block = ctx.enter_context(nc.Block())

        @block.sync
        def _(sp):
            sp.dma_start(CST[:, :], consts).then_inc(S["const_in"], 16)
            sp.dma_start(cond[:, 0, :], c[0].rearrange("(p k) -> p k", p=P)).then_inc(S["cond_in"], 16)
            sp.dma_start(cond[:, 1, :], c_ctx.rearrange("(p k) -> p k", p=P)).then_inc(S["cond_in"], 16)
            sp.dma_start(X[:, 0:NT_S, :], x_sample[0].rearrange("(t p) d -> p t d", p=P)).then_inc(S["x_in"], 16)
            sp.dma_start(X[:, NT_S, :], x_prompt[0]).then_inc(S["x_in"], 16)
            for l in range(DEPTH):
                if l:
                    sp.wait_ge(S["phase"], 4 * PH * l)
                sp.dma_start(ada_bias, ada_b[l:l + 1, :].to_broadcast([2, 6 * D])).then_inc(S["adab_in"], 16)
                for i, g in enumerate((norm1_g, norm2_g)):
                    sp.dma_start(gain_row[:, i, :], g[l:l + 1, :].to_broadcast([P, D])).then_inc(S["gain_in"], 16)
                aw = ada_w[l].rearrange("(p k) n -> p k n", p=P)
                for n in range(12):
                    if n >= 2:
                        sp.wait_ge(S["m_ps"], 12 * l + n - 1)
                    sp.dma_start(ada_slab[n % 2], aw[:, :, 512 * n:512 * n + 512]).then_inc(adaw_in[n % 2], 16)
                sp.wait_ge(S["phase"], 4 * (PH * l + 1))
                for ct in range(2):
                    sp.dma_start(vec_rows[TAPS * ct:TAPS * ct + TAPS, :],
                                 conv_w[l, :, P * ct:P * ct + P]).then_inc(S["vec_in"], 16)
                for r, v in ((R_CB, conv_b[l]), (R_CNG, conv_norm_g[l]), (R_CNB, conv_norm_b[l]),
                             (R_GLG, gla_norm_g[l].rearrange("h e -> (h e)")), (R_ABF, gla_a_b_f[l]),
                             (R_ABB, gla_a_b_b[l])):
                    sp.dma_start(vec_rows[r:r + 2, :], v.rearrange("(a b) -> a b", a=2)).then_inc(S["vec_in"], 16)
                for r, v in ((R_QG, q_norm_g), (R_KG, k_norm_g)):
                    for half in range(2):
                        sp.dma_start(vec_rows[r:r + 1, 64 * half:64 * half + 64],
                                     v[l:l + 1, :]).then_inc(S["vec_in"], 16)
                wi = w_in[l].rearrange("(k p) n -> p k n", p=P)
                for b, (_, w, c0) in enumerate(BLOCKS):
                    if b >= 5:
                        sp.wait_ge(S["proj_ps"], NB * l + b - 4)
                    sp.dma_start(win[b % 5][:, :, 0:w], wi[:, :, c0:c0 + w]).then_inc(win_in[b % 5], 16)
                sp.dma_start(w_v[:, :, 0:256], wi[:, :, GV0:GV0 + 256]).then_inc(S["wv_in"], 16)
                sp.dma_start(w_v[:, :, 256:384], wi[:, :, AV0:AV0 + P]).then_inc(S["wv_in"], 16)
                sp.wait_ge(S["phase"], 4 * (PH * l + 2))
                sp.dma_start(CK, cache_k[0, l].rearrange("s h d -> s (h d)")).then_inc(S["misc_in"], 16)
                sp.dma_start(CVAL, cache_v[0, l].rearrange("s h d -> s (h d)")).then_inc(S["misc_in"], 16)
                for dr, w in enumerate((gla_a_w_f, gla_a_w_b)):
                    sp.dma_start(gla_w[16 * dr:16 * dr + 16, dr, :], w[l]).then_inc(S["misc_in"], 16)
                sp.dma_start(new_v[0, l].rearrange("s h d -> s (h d)"), VT[:, NT_S, 256:384]).then_inc(S["out_done"], 16)
                sp.wait_ge(S["kout_ready"], l + 1)
                sp.dma_start(new_k[0, l].rearrange("s h d -> s (h d)"), KOUT).then_inc(S["out_done"], 16)
                sp.wait_ge(S["st_zero"], l + 1)
                for i in range(4):
                    for hb in range(2):
                        q = slice(64 * hb, 64 * hb + 64)
                        sp.dma_start(ST[q, i, 0 if i < 2 else 7, q],
                                     state_gla[0, l, i // 2, 2 * (i % 2) + hb]).then_inc(S["st_in"], 16)
                sp.wait_ge(S["st_ready"], NUPD * (l + 1))
                for i in range(4):
                    for hb in range(2):
                        q = slice(64 * hb, 64 * hb + 64)
                        sp.dma_start(new_state[0, l, i // 2, 2 * (i % 2) + hb],
                                     ST[q, i, 10, q]).then_inc(S["out_done"], 16)
                sp.wait_ge(S["phase"], 4 * (PH * l + 5))
                sp.dma_start(WOUT, w_out[l].rearrange("(k p) n -> p k n", p=P)).then_inc(S["wout_in"], 16)
                sp.wait_ge(S["out_done"], 16 * N_OUT * (l + 1))
                sp.wait_ge(S["phase"], 4 * (PH * l + 6))
                for s in range(2):
                    sp.dma_start(KRAW[:, :, 64 * s:64 * s + 64],
                                 peer_keys[l, :, s].rearrange("h k d -> k h d")).then_inc(S["keys_in"], 16)
                sp.dma_start(WQ, peer_wq[l].rearrange("(k p) n -> p k n", p=P)).then_inc(S["wq_in"], 16)
            for t in range(NT):
                sp.wait_ge(S["y_ready"], NT * (DEPTH - 1) + t + 1)
                dst = y_sample[0, P * t:P * t + P, :] if t < NT_S else y_prompt[0]
                sp.dma_start(dst, X[:, t, :]).then_inc(S["out_done"], 16)
            sp.wait_ge(S["out_done"], 16 * (N_OUT * DEPTH + NT))

        @block.gpsimd
        def _(pool):
            u_rows = peer_u.rearrange("l e d -> (l e) d")
            v_rows = peer_v.rearrange("l e d -> (l e) d")
            pool.memset(gla_w[:, :, :], 0.0)
            pool.memset(zero_l[:, :], 0.0)
            pool.memset(zero_r[:, :], 0.0).then_inc(S["zeros_ready"], 1)
            for l in range(DEPTH):
                phase_end(pool, PH * l + 1)
                pool.memset(UP[:, :, :], 0.0).then_inc(S["pad_ready"], 1)
                for n in (2, 3, 4):
                    phase_end(pool, PH * l + n)
                pool.wait_ge(S["out_done"], 16 * (N_OUT * l + 2))
                pool.memset(A[:, 11264:16896], 0.0).then_inc(S["st_zero"], 1)
                for n in (5, 6):
                    phase_end(pool, PH * l + n)
                pool.memset(KEYS[:, :, :], 0.0).then_inc(S["keys_zero"], 1)
                with pool.Fori(0, NT * HEADS) as i:
                    head = NT * HEADS * l + i
                    pool.wait_ge(S["idx_ready"], head + 1)
                    pool.sem_inc(S["pool_turn"], 1)
                    for k in range(TOPK):
                        pool.wait_ge(S["u_free"], head * TOPK + k + 1)
                        pool.sem_inc(S["pool_turn"], 1)
                        pool.indirect_dma_start(UR[:, k % RING, :], None, u_rows,
                                                bass.IndirectOffsetOnAxis(ap=idx_u[:, k:k + 1], axis=0))\
                            .then_inc(u_in[k % RING], 16)
                    pool.wait_ge(S["idxv_ready"], head + 1)
                    pool.sem_inc(S["pool_turn"], 1)
                    for k in range(TOPK):
                        pool.wait_ge(S["v_free"], head * TOPK + k + 1)
                        pool.sem_inc(S["pool_turn"], 1)
                        pool.indirect_dma_start(VR[:, k % RING, :], None, v_rows,
                                                bass.IndirectOffsetOnAxis(ap=idx_v[:, k:k + 1], axis=0))\
                            .then_inc(v_in[k % RING], 16)
                phase_end(pool, PH * l + 7)

        @block.tensor
        def _(pe):
            def mm(out, lhsT, rhs, start=True, stop=True):
                return pe.matmul(out, lhsT, rhs, start=start, stop=stop)

            def wide(out, lhsT, rhs, start=True, stop=True):
                mm(out[:, 0:512], lhsT, rhs[:, 0:512], start, stop)
                return mm(out[:, 512:NTOK], lhsT, rhs[:, 512:NTOK], start, stop)

            def ada(l):
                if l == 0:
                    pe.wait_ge(S["cond_ready"], 2)
                    pe.wait_ge(S["const_in"], 16)
                for n in range(12):
                    pe.wait_ge(adaw_in[n % 2], 16 * (6 * l + n // 2 + 1))
                    if n >= 2:
                        pe.wait_ge(S["m_row_done"], 12 * l + n - 1)
                    for k in range(KT):
                        m = mm(PS[0:2, n % 2, :], cond_s[:, k, :], ada_slab[n % 2][:, k, :], k == 0, k == KT - 1)
                    m.then_inc(S["m_ps"], 1)
                pe.wait_ge(S["m_row_done"], 12 * l + 12)
                for j, (r, g, hf) in enumerate(BCAST):
                    if j >= 4:
                        if is_scale(j - 4):
                            pe.wait_ge(S["bc_dve"], N_SC * l + sum(is_scale(q) for q in range(j - 3)))
                        else:
                            pe.wait_ge(S["bc_act"], N_PL * l + sum(not is_scale(q) for q in range(j - 3)))
                    mm(PS[:, 4 + j % 4, :], CST[0:2, C_SEL + P * g:C_SEL + P * g + P],
                       m_row[:, D * r + 512 * hf:D * r + 512 * hf + 512]).then_inc(S["bc_ps"], 1)

            def project(l):
                pe.wait_ge(S["vec_in"], 16 * 12 * (l + 1))
                pe.transpose(PS[:, 4, 0:R_END], vec_rows, CST[0:R_END, C_ID:C_ID + R_END]).then_inc(S["vec_ps"], 1)
                for t in range(NT):
                    pe.wait_ge(S["h_ready"], NT * l + t + 1)
                    if t >= 2:
                        pe.wait_ge(S["ht_ready"], NT * l + t - 1)
                    for k in range(KT):
                        m = pe.transpose(pair(t % 2)[:, P * k:P * k + P], hbuf[:, t % 2, P * k:P * k + P], ident)
                    m.then_inc(S["ht_ps"], 1)
                pe.wait_ge(S["ht_ready"], NT * l + NT)
                pe.wait_ge(S["vec_ready"], l + 1)
                for b, (_, w, _c) in enumerate(BLOCKS):
                    pe.wait_ge(win_in[b % 5], 16 * (len(range(b % 5, NB, 5)) * l + b // 5 + 1))
                    if b >= 2:
                        pe.wait_ge(S["proj_ev"], NB * l + b - 1)
                    for k in range(KT):
                        m = wide(pair(2 + b % 2)[0:w], win[b % 5][:, k, 0:w], HT[:, k, :], k == 0, k == KT - 1)
                    m.then_inc(S["proj_ps"], 1)
                pe.wait_ge(S["wv_in"], 32 * (l + 1))
                for t in range(NT):
                    if t >= 2:
                        pe.wait_ge(S["vt_ready"], NT * l + t - 1)
                    for k in range(KT):
                        m = mm(PS[:, t % 2, 0:384], HT[:, k, P * t:P * t + P], w_v[:, k, :], k == 0, k == KT - 1)
                    m.then_inc(S["vt_ps"], 1)

            def feature_norms(l):
                pe.wait_ge(S["misc_in"], 64 * (l + 1))
                pe.transpose(PS[:, 7, 0:P], CK, ident).then_inc(S["kc_ps"], 1)
                for i, (kind, src, _g) in enumerate(UNITS):
                    if kind == "c":
                        wide(pair(2), mean_mat, src).then_inc(S["cx_mean"], 1)
                        pe.wait_ge(S["cx_cent"], 2 * l + i - 4)
                    pe.wait_ge(S["sq_ready"], NU * l + i + 1)
                    if i >= 2:
                        pe.wait_ge(S["sd_ready"], NU * l + i - 1)
                    wide(pair(i % 2), mean_mat, SQ[:, i % 2, :]).then_inc(S["var_ps"], 1)
                    if kind != "c":
                        pe.wait_ge(S["n_ready"], NU * l + i + 1)
                        if kind == "k":
                            pe.transpose(PS[:, 6, 0:P], src[:, N_SAMPLE:NTOK], ident).then_inc(S["kout_ps"], 1)
                        if i >= 2:
                            pe.wait_ge(S["rope_done"], 5 * l + i - 1)
                        mm(PS[:, 4 + i % 2, :], rot_mat, src[:, 0:N_SAMPLE]).then_inc(S["rot_ps"], 1)
                        if kind == "k":
                            pe.wait_ge(S["rope_done"], 5 * l + 5)
                pe.wait_ge(S["kc_ready"], l + 1)
                pe.wait_ge(S["sd_ready"], NU * l + NU)
                for kv in range(2):
                    dup = CST[:, C_DUP + P * kv:C_DUP + P * kv + P]
                    o = pair(kv)
                    mm(o[:, 0:512], dup, AK[:, 0:512])
                    mm(o[:, 512:640], dup, KC)
                    mm(o[:, 640:768], dup, AK[:, N_SAMPLE:NTOK]).then_inc(S["dup_ps"], 1)

            def attention(l):
                def scores(i):
                    t, h = STEPS[i]
                    if i >= 2:
                        pe.wait_ge(S["p_ready"], NS * l + i - 1)
                    q = slice(64 * (h % 2), 64 * (h % 2) + 64)
                    k0, nk = keys_of(t)
                    for a in range(0, nk, 512):
                        b = min(nk, a + 512)
                        m = mm(pair(i % 2)[:, a:b], AQ[q, h // 2, P * t:P * t + P], KTD[q, h // 4, k0 + a:k0 + b])
                    m.then_inc(S["s_ps"], 1)

                def evacuated(i):
                    pe.wait_ge(S["pt_dve" if i % 2 else "pt_act"], NS // 2 * l + i // 2 + 1)

                def transposes(i):
                    pe.wait_ge(S["p_ready"], NS * l + i + 1)
                    if i >= 1:
                        evacuated(i - 1)
                    for s in range(keys_of(STEPS[i][0])[1] // P):
                        m = pe.transpose(pair(2)[:, P * s:P * s + P], PR[:, i % 2, P * s:P * s + P], ident)
                    m.then_inc(S["pt_ps"], 1)

                def values(i):
                    t, h = STEPS[i]
                    evacuated(i)
                    if h == 0 and t:
                        pe.wait_ge(S["o_ready"], NT * l + t)
                    v = vals_of(t)
                    for s, vt in enumerate(v):
                        m = mm(PS[:, 6, 64 * h:64 * h + 64], PRT[:, i % 2, P * s:P * s + P],
                               vt[:, 64 * (h // 4):64 * (h // 4) + 64], s == 0, s == len(v) - 1)
                    m.then_inc(S["o_ps"], 1)

                def out_transposes(t):
                    pe.wait_ge(S["o_ready"], NT * l + t + 1)
                    if t:
                        pe.wait_ge(S["ot_ready"], NT * l + t)
                    for j in range(4):
                        m = pe.transpose(PS[:, 7, P * j:P * j + P], OTOK[:, P * j:P * j + P], ident)
                    m.then_inc(S["ot_ps"], 1)

                for i in range(NS + 2):
                    if i < NS:
                        scores(i)
                    if 1 <= i <= NS:
                        transposes(i - 1)
                    if i >= 2:
                        values(i - 2)
                        if STEPS[i - 2][1] == 7:
                            out_transposes(STEPS[i - 2][0])

            def gla_out(l, s):
                hp, t = s // NT, s % NT
                pe.wait_ge(S["atm_ready"], 2 * NT * l + s + 1)
                o = pair(hp)
                for n, (dr, ch) in enumerate(((0, 2 * t), (0, 2 * t + 1), (1, 2 * t), (1, 2 * t + 1))):
                    i = 2 * dr + hp
                    cols = slice(64 * ch, 64 * ch + 64)
                    mm(o[:, cols], ST[:, i, ch, :], QD[:, i, cols], n == 0, False)
                for hb in range(2):
                    head = 2 * hp + hb
                    for dr in range(2):
                        m = mm(o[64 * hb:64 * hb + 64, P * t:P * t + P], VT[:, t, 64 * head:64 * head + 64],
                               ATM[:, s % 2, hb, dr, :], False, dr == 1)
                m.then_inc(S["og_ps"], 1)

            def gla(l):
                for i in range(4):
                    wide(pair(i), gla_w[:, i // 2, P * (i % 2):P * (i % 2) + P], GA).then_inc(S["z_ps"], 1)
                for i in range(4):
                    pe.wait_ge(S["qk_ready"], 4 * l + i + 1)
                    for t in range(NT):
                        m = pe.transpose(pair(i)[:, P * t:P * t + P], KK[:, i, P * t:P * t + P], ident)
                    m.then_inc(S["kk_ps"], 1)
                pe.wait_ge(S["kk_ready"], 4 * l + 4)
                for u, (i, ch, _n) in enumerate(UPD):
                    if u >= 8:
                        pe.wait_ge(S["st_ready"], NUPD * l + u - 7)
                    q = slice(64 * (ch % 2), 64 * (ch % 2) + 64)
                    mm(PS[:, u % 8, 0:P], KKT[q, i, ch // 2, :],
                       VT[q, ch // 2, P * (i % 2):P * (i % 2) + P]).then_inc(S["dS_ps"], 1)
                pe.wait_ge(S["st_ready"], NUPD * (l + 1))
                for s in range(2 * NT):
                    hp, t = s // NT, s % NT
                    if s >= 2:
                        pe.wait_ge(S["atm_ready"], 2 * NT * l + s - 1)
                    cols = slice(P * t, P * t + P)
                    for hb in range(2):
                        q = slice(64 * hb, 64 * hb + 64)
                        for dr in range(2):
                            i = 2 * dr + hp
                            m = mm(PS[:, 4 + 2 * (s % 2) + hb, P * dr:P * dr + P], KD[q, i, cols], QD[q, i, cols])
                    m.then_inc(S["a_ps"], 1)
                    if s >= 1:
                        gla_out(l, s - 1)
                gla_out(l, 2 * NT - 1)
                for hp in range(2):
                    pe.wait_ge(S["og_sq"], 2 * l + hp + 1)
                    wide(pair(2 + hp), mean_mat, OSQ[:, hp, :]).then_inc(S["og_var"], 1)

            def out_project(l):
                pe.wait_ge(S["wout_in"], 16 * (l + 1))
                for t in range(NT):
                    if t >= 2:
                        pe.wait_ge(S["res_read"], NT * l + t - 1)
                    for hf in range(2):
                        for k in range(KT):
                            m = mm(pair(t % 2)[:, 512 * hf:512 * hf + 512], MIX[:, k, P * t:P * t + P],
                                   WOUT[:, k, 512 * hf:512 * hf + 512], k == 0, k == KT - 1)
                    m.then_inc(S["mix_ps"], 1)

            def tile_transposes(l, t):
                n = NT * l + t
                pe.wait_ge(S["h2_ready"], n + 1)
                if t:
                    pe.wait_ge(S["sc_now"], HEADS * n)
                for k in range(KT):
                    m = pe.transpose(pair(2)[:, P * k:P * k + P], H2[:, t % 2, P * k:P * k + P], ident)
                m.then_inc(S["h2t_ps"], 1)
                pe.wait_ge(S["h2t_ready"], n + 1)

            def query(g, h):
                if not isinstance(g, int) or g:
                    pe.wait_ge(S["q_ready"], g)
                for k in range(KT):
                    m = mm(PS[:, 6, 0:P], H2T[:, k, :], WQ[:, k, bass.ds(h * P, P)], k == 0, k == KT - 1)
                m.then_inc(S["q_ps"], 1)

            def query_transpose(g):
                pe.wait_ge(S["q_ready"], g + 1)
                pe.transpose(PS[:, 7, 0:P], QTOK, ident).then_inc(S["qt_ps"], 1)

            def key_scores(g, h):
                pe.wait_ge(S["qt_ready"], g + 1)
                mm(PS[:, 4, 0:256], QT, KEYS[:, :, :].rearrange("p h k -> p (h k)")[:, bass.ds(h * 256, 256)])\
                    .then_inc(S["sc_ps"], 1)

            def head_sum(head, ahead):
                for k in range(TOPK):
                    if ahead is not None:
                        if k == 0:
                            query(head + 2, ahead)
                        if k == 5:
                            query_transpose(head + 2)
                        if k == 10:
                            key_scores(head + 2, ahead)
                    pe.wait_ge(v_in[k % RING], head * 32 + 16 * (k // RING + 1))
                    pe.wait_ge(S["diag_ready"], head * TOPK + k + 1)
                    for cc in range(2):
                        m = mm(PS[:, cc, :], DG[:, k % DIAGS, :], VR[:, k % RING, 512 * cc:512 * cc + 512],
                               False, False)
                    m.then_inc(S["v_free"], 1)

            def peer(l):
                pe.wait_ge(S["keys_in"], 32 * (l + 1))
                for h in range(HEADS):
                    m = pe.transpose(pair(2)[:, P * h:P * h + P], KRAW[:, h, :], ident)
                m.then_inc(S["keys_ps"], 1)
                pe.wait_ge(S["keys_ready"], l + 1)
                tile_transposes(l, 0)
                pe.wait_ge(S["wq_in"], 16 * (l + 1))
                for h in range(2):
                    g = HEADS * NT * l + h
                    query(g, h)
                    query_transpose(g)
                    if h:
                        pe.wait_ge(S["sc_now"], g)
                    key_scores(g, h)
                if l == 0:
                    pe.wait_ge(S["zeros_ready"], 1)
                    pe.sem_inc(S["v_free"], RING)
                for t in range(NT):
                    n = NT * l + t
                    if n:
                        pe.wait_ge(S["acc_out"], n)
                    for cc in range(2):
                        mm(PS[:, cc, :], zero_l[:, :], zero_r[:, :], True, False)
                    with pe.Fori(0, HEADS - 2) as i:
                        head_sum(HEADS * n + i, i + 2)
                    if t + 1 < NT:
                        tile_transposes(l, t + 1)
                        with pe.Fori(0, 2) as i:
                            head_sum(HEADS * n + HEADS - 2 + i, i)
                    else:
                        with pe.Fori(0, 2) as i:
                            head_sum(HEADS * n + HEADS - 2 + i, None)
                    for cc in range(2):
                        m = mm(PS[:, cc, :], zero_l[:, :], zero_r[:, :], False, True)
                    m.then_inc(S["acc_done"], 1)

            for l in range(DEPTH):
                for n, stage in enumerate((ada, project, feature_norms, attention, gla, out_project, peer)):
                    stage(l)
                    phase_end(pe, PH * l + n + 1)

        @block.scalar
        def _(act):
            st = Steps(act, "act")

            def ada(l):
                if l == 0:
                    act.wait_ge(S["cond_in"], 32)
                    for group in range(2):
                        act.activation(cond_s[:, :, group], cond[:, group, :], ACT.Silu).then_inc(S["cond_ready"], 1)
                for j in range(NBC):
                    if not is_scale(j):
                        act.wait_ge(S["bc_ps"], NBC * l + j + 1)
                        act.activation(mod_dst(j), PS[:, 4 + j % 4, :], ACT.Copy).then_inc(S["bc_act"], 1)

            def project(l):
                if l == 0:
                    act.wait_ge(S["x_in"], 32)
                for t in range(NT):
                    st.link(act.activation(hbuf[:, t % 2, :], X[:, t, :], ACT.Square, accum_out=sumsq[:, t:t + 1]))
                act.sem_inc(S["ss_done"], 1)
                act.wait_ge(S["ms_done"], l + 1)
                act.activation(rms[:, 0:NT], rstd[:, 0:NT], ACT.Sqrt).then_inc(S["sd_done"], 1)
                act.wait_ge(S["vec_ps"], l + 1)
                act.activation(vec[:, :], PS[:, 4, 0:R_END], ACT.Copy).then_inc(S["vec_ready"], 1)
                for t in range(NT):
                    act.wait_ge(S["ht_ps"], NT * l + t + 1)
                    act.activation(HT[:, :, P * t:P * t + P], pair(t % 2).rearrange("p (k n) -> p k n", k=KT),
                                   ACT.Copy).then_inc(S["ht_ready"], 1)
                for b, (dst, w, _c) in enumerate(BLOCKS):
                    act.wait_ge(S["proj_ps"], NB * l + b + 1)
                    f = ACT.Sigmoid if b in (0, 2) else ACT.Silu if b >= NB - 2 else ACT.Copy
                    act.activation(dst, pair(2 + b % 2)[0:w, 0:NTOK], f).then_inc(S["proj_ev"], 1)
                for t in range(NT):
                    act.wait_ge(S["vt_ps"], NT * l + t + 1)
                    act.activation(VT[:, t, :], PS[:, t % 2, 0:384], ACT.Copy).then_inc(S["vt_ready"], 1)

            def feature_norms(l):
                act.wait_ge(S["kc_ps"], l + 1)
                act.activation(KC, PS[:, 7, 0:P], ACT.Copy).then_inc(S["kc_ready"], 1)

                def square(i):
                    if i >= 2:
                        act.wait_ge(S["var_ps"], NU * l + i - 1)
                    if UNITS[i][0] == "c":
                        act.wait_ge(S["cx_cent"], 2 * l + i - 4)
                    act.activation(SQ[:, i % 2, :], UNITS[i][1], ACT.Square).then_inc(S["sq_ready"], 1)

                square(0)
                for i in range(NU):
                    if i + 1 < 5:
                        square(i + 1)
                    act.wait_ge(S["var_ps"], NU * l + i + 1)
                    if i >= 2:
                        act.wait_ge(S["n_ready"], NU * l + i - 1)
                    act.activation(SD[:, i % 2, :], pair(i % 2)[:, 0:NTOK], ACT.Sqrt, bias=eps_c[:, 0:1])\
                        .then_inc(S["sd_ready"], 1)
                    if i == 4:
                        act.wait_ge(S["kout_ps"], l + 1)
                        act.activation(KOUT, PS[:, 6, 0:P], ACT.Copy).then_inc(S["kout_ready"], 1)
                    if 5 <= i + 1 < NU:
                        square(i + 1)
                for j in range(2):
                    act.wait_ge(S["n_ready"], NU * l + 6 + j)
                    act.activation(MIX[:, 2 + j, :], CX[:, j, :], ACT.Silu, bias=vec[:, R_CNB + j:R_CNB + j + 1])\
                        .then_inc(S["silu_done"], 1)
                for kv in range(2):
                    act.wait_ge(S["dup_ps"], 2 * l + kv + 1)
                    act.activation(KTD[:, kv, :], pair(kv)[:, 0:768], ACT.Copy).then_inc(S["dup_ready"], 1)

            def attention(l):
                def softmax(i):
                    t, h = STEPS[i]
                    act.wait_ge(S["nmax_ready"], NS * l + i + 1)
                    if i >= 2:
                        act.wait_ge(S["pt_ps"], NS * l + i - 1)
                    if h == 0 and t >= 2:
                        act.wait_ge(S["o_ready"], NT * l + t - 1)
                    nk = keys_of(t)[1]
                    act.activation(PR[:, i % 2, 0:nk], pair(i % 2)[:, 0:nk], ACT.Exp, bias=nmax[:, i % 4:i % 4 + 1],
                                   scale=0.125, accum_out=psum_p[:, t % 2, h:h + 1]).then_inc(S["p_ready"], 1)

                def evacuate(i):
                    act.wait_ge(S["pt_ps"], NS * l + i + 1)
                    if i >= 2:
                        act.wait_ge(S["o_ps"], NS * l + i - 1)
                    nk = keys_of(STEPS[i][0])[1]
                    act.activation(PRT[:, i % 2, 0:nk], pair(2)[:, 0:nk], ACT.Copy).then_inc(S["pt_act"], 1)

                def out_evacuate(t):
                    act.wait_ge(S["ot_ps"], NT * l + t + 1)
                    act.activation(MIX[:, 4:8, P * t:P * t + P], PS[:, 7, :].rearrange("p (j n) -> p j n", j=4),
                                   ACT.Copy).then_inc(S["ot_ready"], 1)

                for i in range(NS + 3):
                    if i < NS:
                        softmax(i)
                    if 1 <= i <= NS and (i - 1) % 2 == 0:
                        evacuate(i - 1)
                    if i >= 3 and STEPS[i - 3][1] == 7:
                        out_evacuate(STEPS[i - 3][0])

            def gla(l):
                for i in range(4):
                    act.wait_ge(S["z_ps"], 4 * l + i + 1)
                    col = (R_ABF if i < 2 else R_ABB) + i % 2
                    act.activation(KK[:, i, :], pair(i)[:, 0:NTOK], ACT.Abs, bias=vec[:, col:col + 1])\
                        .then_inc(S["abs_done"], 1)
                act.wait_ge(S["abs_done"], 4 * l + 4)
                st.link(act.activation(KK[:, :, :], KK[:, :, :], ACT.Exp, scale=-1.0))
                act.activation(KK[:, :, :], KK[:, :, :], ACT.Ln, bias=1.0).then_inc(S["ln_done"], 1)
                for i in range(4):
                    act.wait_ge(S["b_ready"], 4 * l + i + 1)
                    act.activation(QD[:, i, :], LA[:, i, :], ACT.Exp, scale=1 / 16)
                    act.activation(KD[:, i, :], LA[:, i, :], ACT.Exp, scale=-1 / 16)
                    act.activation(KK[:, i, :], KK[:, i, :], ACT.Exp, scale=1 / 16).then_inc(S["ex_done"], 1)
                act.activation(e_last[:, :, :], e_last[:, :, :], ACT.Exp, scale=1 / 16).then_inc(S["el_ready"], 1)
                for i in range(4):
                    act.wait_ge(S["kk_ps"], 4 * l + i + 1)
                    act.activation(KKT[:, i, :, :], pair(i)[:, 0:NTOK].rearrange("p (t f) -> p t f", t=NT), ACT.Copy)\
                        .then_inc(S["kk_ready"], 1)
                for hp in range(2):
                    act.wait_ge(S["og_ps"], 2 * NT * l + NT * (hp + 1))
                    act.activation(OG[:, hp, :], pair(hp)[:, 0:NTOK], ACT.Copy)
                    act.activation(OSQ[:, hp, :], pair(hp)[:, 0:NTOK], ACT.Square).then_inc(S["og_sq"], 1)
                for hp in range(2):
                    act.wait_ge(S["og_var"], 2 * l + hp + 1)
                    act.activation(OSD[:, hp, :], pair(2 + hp)[:, 0:NTOK], ACT.Sqrt, bias=eps_c[:, 0:1])\
                        .then_inc(S["og_sd"], 1)

            def out_project(l):
                pass

            def query_out(g):
                act.wait_ge(S["q_ps"], g + 1)
                act.activation(QTOK, PS[:, 6, 0:P], ACT.Copy).then_inc(S["q_ready"], 1)

            def query_transpose_out(g):
                act.wait_ge(S["qt_ps"], g + 1)
                act.activation(QT, PS[:, 7, 0:P], ACT.Copy).then_inc(S["qt_ready"], 1)

            def scores_out(g):
                act.wait_ge(S["sc_ps"], g + 1)
                if not isinstance(g, int) or g:
                    act.wait_ge(S["sc_taken"], g)
                act.activation(SCC[:, :, :].rearrange("p a b -> p (a b)"), PS[:, 4, 0:256], ACT.Copy)\
                    .then_inc(S["sc_now"], 1)

            def head_weights(head, ahead):
                act.wait_ge(S["idx_ready"], head + 1)
                act.activation(gexp[:, :], centred[:, :], ACT.Exp, accum_out=gsum[:, 0:1])
                act.wait_ge(S["u_free"], head * TOPK + TOPK + RING)
                act.activation(gelu_h[:, :], act_h[:, :], ACT.Gelu).then_inc(S["gelu_done"], 1)
                act.wait_ge(S["w_ready"], head + 1)
                for k in range(TOPK):
                    if ahead:
                        if k == 2:
                            query_out(head + 2)
                        if k == 7:
                            query_transpose_out(head + 2)
                        if k == 12:
                            scores_out(head + 2)
                    act.wait_ge(S["v_free"], head * TOPK + k + 1 + RING - DIAGS)
                    act.activation(DG[:, k % DIAGS, :], ident, ACT.Copy, scale=w_h[:, k:k + 1])\
                        .then_inc(S["diag_ready"], 1)

            def tile_out(l, t):
                act.wait_ge(S["h2t_ps"], NT * l + t + 1)
                act.activation(H2T[:, :, :], pair(2).rearrange("p (k n) -> p k n", k=KT), ACT.Copy)\
                    .then_inc(S["h2t_ready"], 1)

            def peer(l):
                for t in range(NT):
                    st.link(act.activation(H2[:, t % 2, :], X[:, t, :], ACT.Square, accum_out=sumsq[:, t:t + 1]))
                act.sem_inc(S["ss2_done"], 1)
                act.wait_ge(S["ms2_done"], l + 1)
                act.activation(rms[:, 0:NT], rstd[:, 0:NT], ACT.Sqrt).then_inc(S["sd2_done"], 1)
                act.wait_ge(S["keys_ps"], l + 1)
                act.wait_ge(S["keys_zero"], l + 1)
                kv = pair(2).rearrange("p (h k) -> p h k", h=HEADS)
                act.activation(KEYS[0:64, :, 0:128], kv[0:64], ACT.Copy)
                act.activation(KEYS[64:128, :, 128:256], kv[64:128], ACT.Copy).then_inc(S["keys_ready"], 1)
                tile_out(l, 0)
                for h in range(2):
                    g = HEADS * NT * l + h
                    query_out(g)
                    query_transpose_out(g)
                    scores_out(g)
                for t in range(NT):
                    n = NT * l + t
                    with act.Fori(0, HEADS - 2) as i:
                        head_weights(HEADS * n + i, True)
                    if t + 1 < NT:
                        tile_out(l, t + 1)
                    with act.Fori(0, 2) as i:
                        head_weights(HEADS * n + HEADS - 2 + i, t + 1 < NT)
                    act.wait_ge(S["acc_done"], n + 1)
                    if n:
                        act.wait_ge(S["y_ready"], n)
                    act.activation(TMP2, pair(0), ACT.Copy).then_inc(S["acc_out"], 1)

            for l in range(DEPTH):
                for n, stage in enumerate((ada, project, feature_norms, attention, gla, out_project, peer)):
                    stage(l)
                    phase_end(act, PH * l + n + 1)

        @block.vector
        def _(dve):
            st = Steps(dve, "dve")
            tt, stt, ts = dve.tensor_tensor, dve.scalar_tensor_tensor, dve.tensor_scalar

            def ada(l):
                if l == 0:
                    dve.memset(eps_c[:, :], EPS)
                dve.wait_ge(S["adab_in"], 16 * (l + 1))
                for n in range(12):
                    dve.wait_ge(S["m_ps"], 12 * l + n + 1)
                    w = slice(512 * n, 512 * n + 512)
                    tt(m_row[:, w], PS[0:2, n % 2, :], ada_bias[:, w], ALU.add).then_inc(S["m_row_done"], 1)
                dve.wait_ge(S["gain_in"], 32 * (l + 1))
                for j, (r, g, hf) in enumerate(BCAST):
                    if is_scale(j):
                        dve.wait_ge(S["bc_ps"], NBC * l + j + 1)
                        stt(mod_dst(j), PS[:, 4 + j % 4, :], 1.0, gain_row[:, r // 3, 512 * hf:512 * hf + 512],
                            ALU.add, ALU.mult).then_inc(S["bc_dve"], 1)

            def project(l):
                dve.wait_ge(S["ss_done"], l + 1)
                ts(rstd[:, 0:NT], sumsq[:, 0:NT], 1.0 / D, EPS, ALU.mult, ALU.add).then_inc(S["ms_done"], 1)
                dve.wait_ge(S["sd_done"], l + 1)
                st.link(dve.reciprocal(rstd[:, 0:NT], rms[:, 0:NT]))
                for t in range(NT):
                    if t >= 2:
                        dve.wait_ge(S["ht_ps"], NT * l + t - 1)
                    g = group_of(t)
                    st.link(stt(hbuf[:, t % 2, :], X[:, t, :], rstd[:, t:t + 1], MOD1[:, g, 1, :], ALU.mult, ALU.mult))
                    tt(hbuf[:, t % 2, :], hbuf[:, t % 2, :], MOD1[:, g, 0, :], ALU.add).then_inc(S["h_ready"], 1)
                dve.wait_ge(S["vec_ready"], l + 1)
                dve.wait_ge(S["pad_ready"], l + 1)
                dve.wait_ge(S["ht_ps"], NT * l + NT)
                segs = ((0, N_SAMPLE, 0), (N_SAMPLE, N_PROMPT, N_SAMPLE + 2 * PAD))
                for ct in range(2):
                    dve.wait_ge(S["proj_ev"], NB * l + 2 * ct + 2)
                    for o, n, q in segs:
                        st.do(tt(UP[:, ct, q + PAD:q + PAD + n], CV[:, ct, o:o + n], CG[:, ct, o:o + n], ALU.mult))
                    for j in range(TAPS):
                        w = vec[:, TAPS * ct + j:TAPS * ct + j + 1]
                        for o, n, q in segs:
                            st.after(st.n - 1)
                            src, dst = UP[:, ct, q + j:q + j + n], CX[:, ct, o:o + n]
                            if j == 0:
                                st.do(ts(dst, src, w, vec[:, R_CB + ct:R_CB + ct + 1], ALU.mult, ALU.add))
                            else:
                                st.do(stt(dst, src, w, dst, ALU.mult, ALU.add))
                st.after(st.n)

            def feature_norms(l):
                for i, (kind, src, g) in enumerate(UNITS):
                    if kind == "c":
                        dve.wait_ge(S["cx_mean"], 2 * l + i - 4)
                        tt(src, src, pair(2)[:, 0:NTOK], ALU.subtract).then_inc(S["cx_cent"], 1)
                        dve.wait_ge(S["cx_cent"], 2 * l + i - 4)
                    dve.wait_ge(S["sd_ready"], NU * l + i + 1)
                    r = SD[:, i % 2, :]
                    st.link(dve.reciprocal(r, r))
                    stt(src, src, vec[:, g:g + 1], r, ALU.mult, ALU.mult).then_inc(S["n_ready"], 1)
                    if kind != "c":
                        dve.wait_ge(S["rot_ps"], 5 * l + i + 1)
                        s5 = src[:, 0:N_SAMPLE]
                        st.do(tt(RT[:, 0:N_SAMPLE], PS[:, 4 + i % 2, :], sin_t, ALU.mult))
                        st.link(tt(s5, s5, cos_t, ALU.mult))
                        tt(s5, s5, RT[:, 0:N_SAMPLE], ALU.add).then_inc(S["rope_done"], 1)
                        dve.wait_ge(S["rope_done"], 5 * l + i + 1)

            def attention(l):
                def maxima(i):
                    t, h = STEPS[i]
                    dve.wait_ge(S["s_ps"], NS * l + i + 1)
                    if i >= 4:
                        dve.wait_ge(S["p_ready"], NS * l + i - 3)
                    st.link(dve.reduce_max(smax[:, i % 4:i % 4 + 1], pair(i % 2)[:, 0:keys_of(t)[1]], AX.X))
                    ts(nmax[:, i % 4:i % 4 + 1], smax[:, i % 4:i % 4 + 1], -0.125, None, ALU.mult)\
                        .then_inc(S["nmax_ready"], 1)

                def evacuate(i):
                    dve.wait_ge(S["pt_ps"], NS * l + i + 1)
                    if i >= 2:
                        dve.wait_ge(S["o_ps"], NS * l + i - 1)
                    nk = keys_of(STEPS[i][0])[1]
                    dve.tensor_copy(PRT[:, i % 2, 0:nk], pair(2)[:, 0:nk]).then_inc(S["pt_dve"], 1)

                def normalise(t):
                    dve.wait_ge(S["o_ps"], NS * l + 8 * t + 8)
                    if t:
                        dve.wait_ge(S["ot_ps"], NT * l + t)
                    st.link(dve.reciprocal(prec[:, :], psum_p[:, t % 2, :]))
                    tt(OTOK.rearrange("p (h e) -> p h e", h=8), PS[:, 6, :].rearrange("p (h e) -> p h e", h=8),
                       prec[:, :].unsqueeze(2).to_broadcast([P, 8, 64]), ALU.mult).then_inc(S["o_ready"], 1)

                for i in range(NS + 2):
                    if i < NS:
                        maxima(i)
                    if 1 <= i <= NS and (i - 1) % 2:
                        evacuate(i - 1)
                    if i >= 2 and STEPS[i - 2][1] == 7:
                        normalise(STEPS[i - 2][0])

            def gla(l):
                for i in range(4):
                    dve.wait_ge(S["abs_done"], 4 * l + i + 1)
                    col = (R_ABF if i < 2 else R_ABB) + i % 2
                    st.do(ts(LA[:, i, :], pair(i)[:, 0:NTOK], vec[:, col:col + 1], 0.0, ALU.add, ALU.min))
                st.after(st.n)
                dve.wait_ge(S["ln_done"], l + 1)
                st.link(tt(LA[:, :, :], LA[:, :, :], KK[:, :, :], ALU.subtract))
                for i in range(4):
                    b = QD[:, i, :]
                    st.link(dve.tensor_tensor_scan(b, scan_keep, LA[:, i, :], 0.0, ALU.mult, ALU.add))
                    bch = b.rearrange("p (c s) -> p c s", c=NCH)
                    lch = LA[:, i, :].rearrange("p (c s) -> p c s", c=NCH)
                    kch = KK[:, i, :].rearrange("p (c s) -> p c s", c=NCH)
                    total = bch[:, :, CHUNK - 1:CHUNK].to_broadcast([P, NCH, CHUNK])
                    st.do(dve.tensor_copy(e_last[:, i, :].unsqueeze(2), bch[:, :, CHUNK - 1:CHUNK]))
                    if i < 2:
                        st.do(tt(kch, total, bch, ALU.subtract))
                        st.link(dve.tensor_copy(LA[:, i, :], b))
                    else:
                        st.link(tt(kch, bch, lch, ALU.subtract))
                        st.link(tt(lch, total, kch, ALU.subtract))
                    dve.sem_inc(S["b_ready"], 1)
                for i in range(4):
                    hp = i % 2
                    dve.wait_ge(S["ex_done"], 4 * l + i + 1)
                    st.do(stt(QD[:, i, :], GQ[:, hp, :], 0.125, QD[:, i, :], ALU.mult, ALU.mult))
                    st.do(tt(KD[:, i, :], GK[:, hp, :], KD[:, i, :], ALU.mult))
                    tt(KK[:, i, :], GK[:, hp, :], KK[:, i, :], ALU.mult).then_inc(S["qk_ready"], 1)
                dve.wait_ge(S["el_ready"], l + 1)
                dve.wait_ge(S["st_in"], 16 * 8 * (l + 1))
                for u, (i, ch, nxt) in enumerate(UPD):
                    dve.wait_ge(S["dS_ps"], NUPD * l + u + 1)
                    if u >= 4:
                        dve.wait_ge(S["st_ready"], NUPD * l + u - 3)
                    for hb in range(2):
                        q = slice(64 * hb, 64 * hb + 64)
                        ins = stt(ST[q, i, nxt, q], ST[q, i, ch, q], e_last[q, i, ch:ch + 1],
                                  PS[q, u % 8, q], ALU.mult, ALU.add)
                    ins.then_inc(S["st_ready"], 1)
                for s in range(2 * NT):
                    dve.wait_ge(S["a_ps"], 2 * NT * l + s + 1)
                    if s >= 2:
                        dve.wait_ge(S["og_ps"], 2 * NT * l + s - 1)
                    for hb in range(2):
                        ins = tt(ATM[:, s % 2, hb, :, :],
                                 PS[:, 4 + 2 * (s % 2) + hb, 0:256].rearrange("p (d i) -> p d i", d=2), masks, ALU.mult)
                    ins.then_inc(S["atm_ready"], 1)
                for hp in range(2):
                    dve.wait_ge(S["og_sd"], 2 * l + hp + 1)
                    st.link(dve.reciprocal(OSD[:, hp, :], OSD[:, hp, :]))
                    st.link(stt(OG[:, hp, :], OG[:, hp, :], vec[:, R_GLG + hp:R_GLG + hp + 1], OSD[:, hp, :],
                                ALU.mult, ALU.mult))
                    tt(MIX[:, hp, :], OG[:, hp, :], GG[:, hp, :], ALU.mult).then_inc(S["og_done"], 1)

            def out_project(l):
                for t in range(NT):
                    dve.wait_ge(S["mix_ps"], NT * l + t + 1)
                    tt(TMP1, pair(t % 2), MOD1[:, group_of(t), 2, :], ALU.mult).then_inc(S["res_read"], 1)
                    dve.wait_ge(S["res_read"], NT * l + t + 1)
                    st.link(tt(X[:, t, :], X[:, t, :], TMP1, ALU.add))

            def normed(l, t):
                if t >= 2:
                    dve.wait_ge(S["h2t_ps"], NT * l + t - 1)
                h, g = H2[:, t % 2, :], group_of(t)
                st.link(stt(h, X[:, t, :], rstd[:, t:t + 1], MOD2[:, g, 1, :], ALU.mult, ALU.mult))
                tt(h, h, MOD2[:, g, 0, :], ALU.add).then_inc(S["h2_ready"], 1)

            def top16(vals, inds, src, spare):
                dve.max(vals[:, 0:8], src)
                dve.drain()
                dve.max_index(inds[:, 0:8], vals[:, 0:8], src)
                dve.match_replace(spare, vals[:, 0:8], src, -3.0e38)
                dve.drain()
                dve.max(vals[:, 8:16], spare)
                dve.drain()
                dve.max_index(inds[:, 8:16], vals[:, 8:16], spare)

            def route(l, head):
                dve.wait_ge(S["sc_now"], head + 1)
                dve.sem_inc(S["dve_turn"], 1)
                for s in range(2):
                    top16(top_v[:, s, :], top_i[:, s, :], SCC[:, s, :], SC2[:, s, :])
                dve.drain().then_inc(S["sc_taken"], 1)
                tt(CAND.rearrange("p (a b) -> p a b", a=16), top_v[:, 0, :].unsqueeze(2).to_broadcast([P, 16, 16]),
                   top_v[:, 1, :].unsqueeze(1).to_broadcast([P, 16, 16]), ALU.add)
                dve.tensor_copy(top_if[:, :, :], top_i[:, :, :])
                dve.drain()
                top16(best[:, :], pos[:, :], CAND, CAND2)
                dve.drain()
                ts(centred[:, :], best[:, :], best[:, 0:1], None, ALU.subtract)
                ts(pos2[:, 0, :], pos[:, :], 4, None, ALU.logical_shift_right)
                ts(pos2[:, 1, :], pos[:, :], 15, None, ALU.bitwise_and)
                dve.drain()
                dve.tensor_copy(pos_f[:, :, :], pos2[:, :, :])
                dve.drain()
                oh = OH.rearrange("p (a b) -> p a b", a=32)
                oh4 = OH.rearrange("p (s a b) -> p s a b", s=2, a=16)
                tt(oh, pos_f[:, :, :].rearrange("p s k -> p (s k)").unsqueeze(2).to_broadcast([P, 32, 16]),
                   iota16.unsqueeze(1).to_broadcast([P, 32, 16]), ALU.is_equal)
                dve.drain()
                tt(oh4, oh4, top_if[:, :, :].unsqueeze(2).to_broadcast([P, 2, 16, 16]), ALU.mult)
                dve.drain()
                dve.reduce_sum(chosen[:, :, :].rearrange("p s k -> p (s k)"), oh, AX.X)
                dve.drain()
                stt(chosen_e[:, :], chosen[:, 0, :], float(NKEYS), chosen[:, 1, :], ALU.mult, ALU.add)
                dve.drain()
                ts(idx_u[:, :], chosen_e[:, :], float(EXPERTS * l), None, ALU.add).then_inc(S["idx_ready"], 1)

            def head_dots(head):
                for k in range(TOPK):
                    if k == 9:
                        dve.wait_ge(S["v_free"], head * TOPK + RING)
                        dve.tensor_copy(idx_v[:, :], idx_u[:, :]).then_inc(S["idxv_ready"], 1)
                    dve.wait_ge(u_in[k % RING], head * 32 + 16 * (k // RING + 1))
                    dve.tensor_tensor_reduce(out=UR[:, k % RING, :], in0=UR[:, k % RING, :], in1=pair(1),
                                             scale=1.0, scalar=0.0, op0=ALU.mult, op1=ALU.add,
                                             accum_out=act_h[:, k:k + 1]).then_inc(S["u_free"], 1)
                dve.wait_ge(S["gelu_done"], head + 1)
                dve.sem_inc(S["dve_turn"], 1)
                dve.reciprocal(grec[:, :], gsum[:, :])
                dve.drain()
                stt(w_h[:, :], gelu_h[:, :], grec[:, 0:1], gexp[:, :], ALU.mult, ALU.mult).then_inc(S["w_ready"], 1)

            def residual(l, t):
                dve.wait_ge(S["acc_out"], NT * l + t + 1)
                st.link(tt(TMP2, TMP2, MOD2[:, group_of(t), 2, :], ALU.mult))
                tt(X[:, t, :], X[:, t, :], TMP2, ALU.add).then_inc(S["y_ready"], 1)

            def peer(l):
                dve.wait_ge(S["ss2_done"], l + 1)
                ts(rstd[:, 0:NT], sumsq[:, 0:NT], 1.0 / D, EPS, ALU.mult, ALU.add).then_inc(S["ms2_done"], 1)
                dve.wait_ge(S["sd2_done"], l + 1)
                st.link(dve.reciprocal(rstd[:, 0:NT], rms[:, 0:NT]))
                normed(l, 0)
                route(l, HEADS * NT * l)
                if l == 0:
                    dve.sem_inc(S["u_free"], RING)
                for t in range(NT):
                    n = NT * l + t
                    dve.drain()
                    dve.tensor_copy(pair(1), H2[:, t % 2, :])
                    if t + 1 < NT:
                        normed(l, t + 1)
                    dve.drain()
                    with dve.Fori(0, HEADS if t + 1 < NT else HEADS - 1) as i:
                        head_dots(HEADS * n + i)
                        route(l, HEADS * n + 1 + i)
                        dve.drain()
                    if t + 1 == NT:
                        head_dots(HEADS * n + HEADS - 1)
                    if t:
                        residual(l, t - 1)
                residual(l, NT - 1)

            for l in range(DEPTH):
                for n, stage in enumerate((ada, project, feature_norms, attention, gla, out_project, peer)):
                    stage(l)
                    phase_end(dve, PH * l + n + 1)


def shape_constants():
    t = np.zeros((P, C_END), np.float32)
    p = np.arange(P)
    t[:, C_ID:C_ID + P] = np.eye(P)
    t[:, C_MEAN:C_MEAN + P] = (p[:, None] // 64 == p[None, :] // 64) / 64.0
    low = p % 32 < 16
    t[np.where(low, p + 16, p - 16), C_ROT + p] = np.where(low, -1.0, 1.0)
    for kv in range(2):
        t[kv * 64 + p % 64, C_DUP + P * kv + p] = 1.0
    same = p[:, None] // CHUNK == p[None, :] // CHUNK
    t[:, C_MASK:C_MASK + P] = same & (p[:, None] <= p[None, :])
    t[:, C_MASK + P:C_MASK + 2 * P] = same & (p[:, None] >= p[None, :])
    tok = np.arange(N_SAMPLE)
    freq = np.float32(10000.0) ** (-np.arange(16, dtype=np.float32) / np.float32(16))
    where = np.where((p % 64 < 32)[:, None], (tok // 64)[None, :], (tok % 64)[None, :]).astype(np.float32)
    angle = where * freq[p % 16][:, None]
    t[:, C_COS:C_COS + N_SAMPLE] = np.cos(angle)
    t[:, C_SIN:C_SIN + N_SAMPLE] = np.sin(angle)
    t[:, C_SCAN:C_SCAN + NTOK] = np.arange(NTOK) % CHUNK != 0
    for g in range(2):
        t[g, C_SEL + P * g:C_SEL + P * g + P] = 1.0
    t[:, C_IOTA:C_IOTA + 16] = np.arange(16)
    return t


_INS = ['x_prompt', 'x_sample', 'c', 'cache_k', 'cache_v', 'state_gla', 'c_ctx', 'ada_w', 'ada_b', 'norm1_g',
        'norm2_g', 'w_in', 'gla_a_w_f', 'gla_a_b_f', 'gla_a_w_b', 'gla_a_b_b', 'gla_norm_g', 'conv_w', 'conv_b',
        'conv_norm_g', 'conv_norm_b', 'q_norm_g', 'k_norm_g', 'w_out', 'peer_wq', 'peer_keys', 'peer_u', 'peer_v']
_OUTS = [(1, 128, 1024), (1, 512, 1024), (1, 2, 128, 2, 64), (1, 2, 128, 2, 64), (1, 2, 2, 4, 64, 64)]


def kernel(**inputs):
    import numpy as _np
    import concourse.bacc as _bacc
    from concourse import mybir as _mybir
    from concourse.bass_utils import run_bass_kernel_spmd as _run

    nc = _bacc.Bacc("TRN2", target_bir_lowering=False, num_devices=1)
    arrays, args = {}, []
    for name in _INS:
        a = _np.ascontiguousarray(inputs[name])
        arrays[f"in_{name}"] = a
        args.append(nc.dram_tensor(f"in_{name}", a.shape, _mybir.dt.from_np(a.dtype), kind="ExternalInput").ap())
    arrays["in_consts"] = shape_constants()
    args.append(nc.dram_tensor("in_consts", (P, C_END), F32, kind="ExternalInput").ap())
    for i, shape in enumerate(_OUTS):
        args.append(nc.dram_tensor(f"out_{i}", shape, F32, kind="ExternalOutput").ap())
    build(nc, *args)
    r = _run(nc, [arrays], core_ids=[0])
    return tuple(r.results[0][f"out_{i}"] for i in range(len(_OUTS)))
```

```python
import numpy as np
import concourse.bass as bass
from concourse import mybir
from contextlib import ExitStack

F32 = mybir.dt.float32
U32 = mybir.dt.uint32
BF16 = mybir.dt.bfloat16
ALU = mybir.AluOpType
ACT = mybir.ActivationFunctionType
AX = mybir.AxisListType

P = 128
D = 1024
KT = D // P
DEPTH = 2
N_SAMPLE, N_PROMPT = 512, 128
NTOK = N_SAMPLE + N_PROMPT
NT = NTOK // P
NT_S = N_SAMPLE // P
CHUNK = 64
NCH = NTOK // CHUNK
TAPS = 31
PAD = TAPS // 2
EPS = 1e-6
NCOLS = 2336
GQ0, GK0, GV0, GG0, GA0, CV0, CG0, AQ0, AK0, AV0 = 0, 256, 512, 768, 1024, 1056, 1312, 1568, 2080, 2208
HEADS, TOPK, NKEYS = 8, 16, 128
EXPERTS = NKEYS * NKEYS
WRING = 3
RING = 8
DIAGS = 4

C_ID, C_MEAN, C_ROT, C_DUP, C_MASK, C_COS, C_SIN, C_SCAN, C_IOTA, C_ONE = (
    0, 128, 256, 384, 640, 896, 1408, 1920, 2560, 2576)
C_END = 2578
R_CB, R_CNG, R_CNB, R_GLG, R_ABF, R_ABB, R_QG, R_KG, R_END = 62, 64, 66, 68, 70, 72, 74, 75, 76


def group_of(t):
    return 0 if t < NT_S else 1


def build(nc, x_prompt, x_sample, c, cache_k, cache_v, state_gla, c_ctx, ada_w, ada_b, norm1_g, norm2_g,
          w_in, gla_a_w_f, gla_a_b_f, gla_a_w_b, gla_a_b_b, gla_norm_g, conv_w, conv_b,
          conv_norm_g, conv_norm_b, q_norm_g, k_norm_g, w_out, peer_wq, peer_keys, peer_u, peer_v,
          consts, y_prompt, y_sample, new_k, new_v, new_state):
    ctx = ExitStack()
    with ctx:
        def sb(name, shape, dt=F32):
            return ctx.enter_context(nc.sbuf_tensor(name, shape, dt))

        def sem(name):
            return ctx.enter_context(nc.semaphore(name))

        CST = sb("constants", [P, C_END])
        X = sb("residual", [P, NT, D])
        MOD2 = sb("peer_modulation", [P, 3, 2, D])
        ident = CST[:, C_ID:C_ID + P]
        mean_mat = CST[:, C_MEAN:C_MEAN + P]
        rot_mat = CST[:, C_ROT:C_ROT + P]
        masks = CST[:, C_MASK:C_MASK + 256].rearrange("p (a b) -> p a b", a=2)
        cos_t = CST[:, C_COS:C_COS + N_SAMPLE]
        sin_t = CST[:, C_SIN:C_SIN + N_SAMPLE]
        scan_keep = CST[:, C_SCAN:C_SCAN + NTOK]
        iota16 = CST[:, C_IOTA:C_IOTA + 16]

        cond = sb("cond", [P, 2, KT])
        cond_s = sb("cond_silu", [P, KT, 2])
        sumsq = sb("sumsq", [P, 2, 8])
        rms = sb("rms", [P, 8])
        rstd = sb("rstd", [P, 8])
        vec = sb("vec_columns", [P, R_END])
        eps_c = sb("eps_column", [P, 1])
        gla_w = sb("gla_gate_w", [32, 2, 256])
        e_last = sb("gla_chunk_decay", [P, 4, NCH])
        smax = sb("score_max", [P, 4])
        nmax = sb("score_neg_max", [P, 4])
        psum_p = sb("softmax_sum", [P, 2, 8])
        prec = sb("softmax_rec", [P, 8])
        top_v = sb("top_values", [P, 2, 16])
        top_i = sb("top_indices", [P, 2, 16], U32)
        top_if = sb("top_indices_f", [P, 2, 16])
        best = sb("best_scores", [P, 16])
        pos = sb("best_positions", [P, 16], U32)
        pos2 = sb("best_pos_split", [P, 2, 16], U32)
        pos_f = sb("best_pos_f", [P, 2, 16])
        chosen = sb("chosen_pair", [P, 2, 16])
        chosen_e = sb("chosen_expert", [P, 16])
        idx_u = sb("rows_for_u", [P, 16], U32)
        idx_v = sb("rows_for_v", [P, 16], U32)
        centred = sb("centred_scores", [P, 16])
        gexp = sb("gate_exp", [P, 16])
        gsum = sb("gate_sum", [P, 1])
        grec = sb("gate_rec", [P, 1])
        act_h = sb("expert_act", [P, 16])
        gelu_h = sb("expert_gelu", [P, 16])
        w_h = sb("expert_weight", [P, 16])
        zero_l = sb("zero_lhs", [P, P], BF16)
        zero_r = sb("zero_rhs", [P, 512], BF16)
        A = sb("arena", [P, 37680])

        def at(start, n):
            return A[:, start:start + n]

        def at3(start, a, b):
            return A[:, start:start + a * b].rearrange("p (a b) -> p a b", a=a)

        MOD1 = A[:, 0:6144].rearrange("p (r g d) -> p r g d", r=3, g=2)
        wide_slab = [at3(21504 + 4096 * i, KT, 512) for i in range(2)]
        m_row = A[0:2, 29696:31744]
        ada_bias = A[0:2, 31744:33792]
        ada_slab = [at3(35192 + 1152 * i, KT + 1, P) for i in range(2)]
        m_chunk = A[0:2, 37496:37624]
        HT = at3(6144, KT, NTOK)
        hbuf = at3(11264, 2, D)
        w_v = at3(13312, KT, 384)
        win = [at3(16384 + 1024 * i, KT, P) for i in range(WRING)]
        SQ = at(19456, NTOK)
        SD = at(20096, NTOK)
        RT = at(20736, N_SAMPLE)
        CK = at(21248, P)
        KC = at(21376, P)
        CV = at3(21504, 2, NTOK)
        CG = at3(22784, 2, NTOK)
        AQ = at3(24064, 4, NTOK)
        gain1 = at(33144, D)
        AK = at(26624, NTOK)
        GA = A[0:32, 27264:27904]
        GK = at3(27904, 2, NTOK)
        GQ = at3(29184, 2, NTOK)
        GG = at3(30464, 2, NTOK)
        UPW = N_SAMPLE + N_PROMPT + 4 * PAD
        UP = at3(31744, 2, UPW)
        VT = at3(33144, NT, 384)
        vec_rows = A[0:R_END, 24064:24192]
        CX = at3(11264, 2, NTOK)
        CVAL = at(12544, P)
        KOUT = at(12672, P)
        MIX = at3(6144, KT, NTOK)
        KTD = at3(16512, 2, 768)
        PR = at3(18432, 2, NTOK)
        PRT = at3(19712, 2, NTOK)
        OTOK = at(20992, 512)
        ST = A[:, 12544:18176].rearrange("p (i s e) -> p i s e", i=4, s=11)
        LA = at3(18176, 4, NTOK)
        KK = at3(20736, 4, NTOK)
        QD = at3(0, 4, NTOK)
        KD = at3(23296, 4, NTOK)
        KKT = A[:, 35064:37624].rearrange("p (i t f) -> p i t f", i=4, t=NT)
        ATM = A[:, 31744:32768].rearrange("p (r h d i) -> p r h d i", r=2, h=2, d=2)
        OG = at3(18176, 2, NTOK)
        OSQ = at3(19456, 2, NTOK)
        OSD = at3(20736, 2, NTOK)
        CSQ = at3(22016, 2, NTOK)
        WOUT = [at3(24576, 4, D), at3(28672, 4, D)]
        TMP = at(34168, D)
        gain2 = at(35192, D)
        xsq = at(11264, D)
        UR = at3(0, RING, D)
        VR = at3(8192, RING, D)
        WQ = at3(16384, KT, D)
        H2 = at3(26624, 2, D)
        H2T = at3(28672, KT, P)
        KRAW = at3(0, HEADS, P)
        QTOK = at(29696, P)
        QT = at(29824, P)
        SCC = at3(29952, 2, NKEYS)
        SC2 = at3(30208, 2, NKEYS)
        CAND = at(30464, 256)
        CAND2 = at(30720, 256)
        OH = at(30976, 512)
        DG = at3(31488, DIAGS, P)
        KEYS = at3(24576, HEADS, 256)

        PS = ctx.enter_context(nc.psum_tensor("ps", [P, 8, 512], F32))
        PSF = PS[:, :, :].rearrange("p b n -> p (b n)")

        def pair(i):
            return PSF[:, 1024 * i:1024 * i + 1024]

        def zp(i):
            return pair((i + 2) % 4)

        S = {n: sem(n) for n in (
            "const_in", "cond_in", "x_in", "adab_in", "gain1_in", "gain2_in", "mod_in", "gate_in", "mod2_in", "vec_in",
            "wv_in", "ck_in", "misc_in", "st_in", "keys_in", "wq_in",
            "cond_ready", "m_ps", "m_row_done", "mod_out",
            "ss_done", "ms_done", "sd_done", "h_ready", "ht_ps", "ht_ready", "vec_ps", "vec_ready", "proj_ps",
            "proj_ev", "vt_ps", "vt_ready", "kc_ps", "kc_ready", "sq_ready", "var_ps", "sd_ready", "n_ready",
            "rot_ps", "rope_done", "kout_ps", "kout_ready", "pad_ready",
            "dup_ps", "dup_ready", "s_ps", "nmax_ready", "p_ready", "pt_ps", "pt_act", "pt_dve", "o_ps", "o_ready",
            "ot_ps", "ot_ready",
            "cx_mean", "cx_cent", "cx_sq", "cx_var", "cx_sd", "cx_ready", "silu_done",
            "z_ps", "abs_done", "ln_done", "b_ready", "ex_done", "el_ready", "qk_ready", "kk_ps", "kk_ready",
            "st_zero", "dS_ps", "st_ready", "a_ps", "atm_ready", "og_ps", "og_sq", "og_var", "og_sd", "og_done",
            "mix_ps", "res_read", "res_done",
            "keys_zero", "keys_ps", "keys_ready", "ss2_done", "ms2_done", "sd2_done", "h2_ready", "h2t_ps", "h2t_ready",
            "q_ps", "q_ready", "qt_ps", "qt_ready", "sc_ps", "sc_now", "sc_taken", "idx_ready", "idxv_ready", "u_free",
            "v_free", "gelu_done", "w_ready", "diag_ready", "acc_done", "acc_out", "y_ready", "zeros_ready",
            "pool_turn", "dve_turn", "act_turn", "pe_turn",
            "out_done", "phase")}
        wide_in = [sem(f"wide_in{i}") for i in range(2)]
        slab_in = [sem(f"slab_in{i}") for i in range(2)]
        win_in = [sem(f"win_in{i}") for i in range(WRING)]
        wout_in = [sem(f"wout_in{i}") for i in range(2)]
        u_in = [sem(f"u_in{i}") for i in range(RING)]
        v_in = [sem(f"v_in{i}") for i in range(RING)]
        step_sem = {e: sem(f"{e}_step") for e in ("dve", "act")}

        class Steps:
            def __init__(self, eng, which):
                self.eng, self.sem, self.n = eng, step_sem[which], 0

            def do(self, ins):
                self.n += 1
                ins.then_inc(self.sem, 1)

            def after(self, n):
                self.eng.wait_ge(self.sem, n)

            def link(self, ins):
                self.do(ins)
                self.after(self.n)

        PH = 5

        def phase_end(eng, n):
            eng.drain().then_inc(S["phase"], 1)
            eng.wait_ge(S["phase"], 4 * n)

        BLOCKS = ([(CG[:, 0, :], P, CG0), (CV[:, 0, :], P, CV0), (CG[:, 1, :], P, CG0 + P), (CV[:, 1, :], P, CV0 + P)]
                  + [(AK, P, AK0)] + [(AQ[:, j, :], P, AQ0 + P * j) for j in range(4)]
                  + [(GA, 32, GA0)]
                  + [(GK[:, j, :], P, GK0 + P * j) for j in range(2)]
                  + [(GQ[:, j, :], P, GQ0 + P * j) for j in range(2)]
                  + [(GG[:, j, :], P, GG0 + P * j) for j in range(2)])
        NB = len(BLOCKS)
        WIDE = 4
        LATE = 48 - 4 * WIDE
        M_EXPERTS = WIDE + LATE
        scratch = nc.dram_tensor("modulation_rows", (DEPTH, 2, 6 * D), F32, kind="Internal").ap()

        UNITS = [(AK, R_KG)] + [(AQ[:, j, :], R_QG) for j in range(4)]
        NU = len(UNITS)
        STEPS = [(t, h) for t in range(NT) for h in range(8)]
        NS = len(STEPS)

        def keys_of(t):
            return (0, NTOK) if t < NT_S else (NTOK, P)

        def vals_of(t):
            return [VT[:, s, 256:384] for s in range(NT_S)] + [CVAL] if t < NT_S else [VT[:, NT_S, 256:384]]

        def updates():
            out = []
            for n in range(9):
                for i in range(4):
                    if i < 2:
                        ch = n if n < 7 else n + 1
                        out.append((i, ch, 10 if ch == 9 else ch + 1))
                    else:
                        ch = 7 - n if n < 7 else 16 - n
                        out.append((i, ch, 10 if ch == 8 else ch - 1))
            return out

        UPD = updates()
        NUPD = len(UPD)
        SEGS = ((0, N_SAMPLE, 0), (N_SAMPLE, N_PROMPT, N_SAMPLE + 2 * PAD))
        N_OUT = 10
        GROUPS = range(2)

        block = ctx.enter_context(nc.Block())

        @block.sync
        def _(sp):
            def load_slab(l, n, c0, slot):
                aw = ada_w[l].rearrange("(p k) n -> p k n", p=P)
                sp.dma_start(ada_slab[slot][:, 0:KT, :], aw[:, :, bass.ds(c0, P)]).then_inc(slab_in[slot], 16)
                sp.dma_start(ada_slab[slot][0:1, KT, :], ada_b[l:l + 1, bass.ds(c0, P)]).then_inc(slab_in[slot], 16)

            def store_rows(l, done, c0):
                sp.wait_ge(S["m_row_done"], done)
                sp.dma_start(scratch[l, :, bass.ds(c0, P)], m_chunk).then_inc(S["mod_out"], 16)

            def load_block(l, b):
                _, w, c0 = BLOCKS[b]
                wi = w_in[l].rearrange("(k p) n -> p k n", p=P)
                sp.dma_start(win[b % WRING][:, :, 0:w], wi[:, :, c0:c0 + w]).then_inc(win_in[b % WRING], 16)

            def load_vectors(l):
                for ct in range(2):
                    sp.dma_start(vec_rows[TAPS * ct:TAPS * ct + TAPS, :],
                                 conv_w[l, :, P * ct:P * ct + P]).then_inc(S["vec_in"], 16)
                for r, v in ((R_CB, conv_b[l]), (R_CNG, conv_norm_g[l]), (R_CNB, conv_norm_b[l]),
                             (R_GLG, gla_norm_g[l].rearrange("h e -> (h e)")), (R_ABF, gla_a_b_f[l]),
                             (R_ABB, gla_a_b_b[l])):
                    sp.dma_start(vec_rows[r:r + 2, :], v.rearrange("(a b) -> a b", a=2)).then_inc(S["vec_in"], 16)
                for r, v in ((R_QG, q_norm_g), (R_KG, k_norm_g)):
                    for half in range(2):
                        sp.dma_start(vec_rows[r:r + 1, 64 * half:64 * half + 64],
                                     v[l:l + 1, :]).then_inc(S["vec_in"], 16)
                sp.dma_start(CK, cache_k[0, l].rearrange("s h d -> s (h d)")).then_inc(S["ck_in"], 16)

            def load_rows(l, dst, first, rows, name):
                for g in GROUPS:
                    src = scratch[l, g, D * first:D * (first + rows)].rearrange("(r d) -> r d", r=rows)
                    sp.dma_start(dst[:, :, g, :], src.unsqueeze(0).to_broadcast([P, rows, D])).then_inc(S[name], 16)

            def start():
                for g, v in enumerate((c[0], c_ctx)):
                    sp.dma_start(cond[:, g, :], v.rearrange("(p k) -> p k", p=P)).then_inc(S["cond_in"], 16)
                aw = ada_w[0].rearrange("(p k) n -> p k n", p=P)
                for n in range(WIDE):
                    if n >= 2:
                        sp.wait_ge(S["m_ps"], n - 1)
                    sp.dma_start(wide_slab[n % 2], aw[:, :, 512 * n:512 * n + 512]).then_inc(wide_in[n % 2], 16)
                    if n == 0:
                        sp.dma_start(ada_bias, ada_b[0:1, 0:2 * D].to_broadcast([2, 2 * D])).then_inc(S["adab_in"], 16)
                        sp.dma_start(X[:, 0:NT_S, :], x_sample[0].rearrange("(t p) d -> p t d", p=P))\
                            .then_inc(S["x_in"], 16)
                        sp.dma_start(X[:, NT_S, :], x_prompt[0]).then_inc(S["x_in"], 16)
                        sp.dma_start(CST[:, :], consts).then_inc(S["const_in"], 16)
                for b in range(WRING):
                    load_block(0, b)
                sp.wait_ge(S["m_row_done"], WIDE)
                sp.dma_start(scratch[0, :, 0:2 * D], m_row).then_inc(S["mod_out"], 16)
                load_vectors(0)
                sp.dma_start(gain1, norm1_g[0:1, :].to_broadcast([P, D])).then_inc(S["gain1_in"], 16)
                sp.wait_ge(S["mod_out"], 16)
                load_rows(0, MOD1[:, 0:2], 0, 2, "mod_in")

            def project(l):
                if l == 0:
                    for n in range(2):
                        load_slab(0, n, 512 * WIDE + P * n, n)
                else:
                    sp.wait_ge(S["phase"], 4 * PH * l)
                wi = w_in[l].rearrange("(k p) n -> p k n", p=P)
                sp.dma_start(w_v[:, :, 0:256], wi[:, :, GV0:GV0 + 256]).then_inc(S["wv_in"], 16)
                sp.dma_start(w_v[:, :, 256:384], wi[:, :, AV0:AV0 + P]).then_inc(S["wv_in"], 16)
                for b in range(NB):
                    if l == 0:
                        for n in (2 * b, 2 * b + 1):
                            store_rows(0, WIDE + n + 1, 512 * WIDE + P * n)
                            if n + 2 < LATE:
                                load_slab(0, n + 2, 512 * WIDE + P * (n + 2), n % 2)
                    if b + WRING < NB:
                        sp.wait_ge(S["proj_ps"], NB * l + b + 1)
                        load_block(l, b + WRING)
                    if b == 0:
                        sp.wait_ge(S["ht_ps"], NT * l + NT)
                        sp.dma_start(CVAL, cache_v[0, l].rearrange("s h d -> s (h d)")).then_inc(S["misc_in"], 16)
                        sp.wait_ge(S["zeros_ready"], 1)
                        for dr, w in enumerate((gla_a_w_f, gla_a_w_b)):
                            sp.dma_start(gla_w[16 * dr:16 * dr + 16, dr, :], w[l]).then_inc(S["misc_in"], 16)
                sp.wait_ge(S["kout_ready"], l + 1)
                sp.dma_start(new_k[0, l].rearrange("s h d -> s (h d)"), KOUT).then_inc(S["out_done"], 16)
                sp.wait_ge(S["vt_ready"], NT * (l + 1))
                sp.dma_start(new_v[0, l].rearrange("s h d -> s (h d)"), VT[:, NT_S, 256:384]).then_inc(S["out_done"], 16)
                if l == 0:
                    sp.wait_ge(S["mod_out"], 16 * (1 + LATE))
                load_rows(l, MOD1[:, 2:3], 2, 1, "gate_in")
                load_rows(l, MOD2[:, :, :, :], 3, 3, "mod2_in")

            def gla(l):
                sp.wait_ge(S["st_zero"], l + 1)
                for i in range(4):
                    for hb in range(2):
                        q = slice(64 * hb, 64 * hb + 64)
                        sp.dma_start(ST[q, i, 0 if i < 2 else 7, q],
                                     state_gla[0, l, i // 2, 2 * (i % 2) + hb]).then_inc(S["st_in"], 16)
                sp.wait_ge(S["st_ready"], NUPD * (l + 1))
                for i in range(4):
                    for hb in range(2):
                        q = slice(64 * hb, 64 * hb + 64)
                        sp.dma_start(new_state[0, l, i // 2, 2 * (i % 2) + hb],
                                     ST[q, i, 10, q]).then_inc(S["out_done"], 16)

            def out_project(l):
                sp.wait_ge(S["phase"], 4 * (PH * l + 3))
                wo = w_out[l].rearrange("(k p) n -> p k n", p=P)
                for i in range(2):
                    sp.dma_start(WOUT[i], wo[:, 4 * i:4 * i + 4, :]).then_inc(wout_in[i], 16)
                sp.dma_start(gain2, norm2_g[l:l + 1, :].to_broadcast([P, D])).then_inc(S["gain2_in"], 16)
                for s in range(2):
                    sp.dma_start(KRAW[:, :, 64 * s:64 * s + 64],
                                 peer_keys[l, :, s].rearrange("h k d -> k h d")).then_inc(S["keys_in"], 16)
                sp.wait_ge(S["out_done"], 16 * N_OUT * (l + 1))
                sp.dma_start(WQ, peer_wq[l].rearrange("(k p) n -> p k n", p=P)).then_inc(S["wq_in"], 16)

            def peer(l):
                if l + 1 == DEPTH:
                    return
                sp.wait_ge(S["phase"], 4 * (PH * l + 4))
                for n in range(2):
                    load_slab(l + 1, n, P * n, n)
                with sp.Fori(0, 23) as i:
                    for j in range(2):
                        store_rows(l + 1, M_EXPERTS + 2 * i + j + 1, i * (2 * P) + P * j)
                        load_slab(l + 1, None, i * (2 * P) + P * (j + 2), j)
                for n in (46, 47):
                    store_rows(l + 1, M_EXPERTS + n + 1, P * n)
                sp.wait_ge(S["keys_ready"], l + 1)
                sp.dma_start(gain1, norm1_g[l + 1:l + 2, :].to_broadcast([P, D])).then_inc(S["gain1_in"], 16)
                sp.wait_ge(S["q_ps"], HEADS * NT * (l + 1))
                for b in range(WRING):
                    load_block(l + 1, b)
                load_vectors(l + 1)
                sp.wait_ge(S["mod_out"], 16 * (1 + LATE + 48))
                sp.wait_ge(S["u_free"], RING + TOPK * HEADS * NT * (l + 1))
                load_rows(l + 1, MOD1[:, 0:2], 0, 2, "mod_in")

            start()
            for l in range(DEPTH):
                for stage in (project, gla, out_project, peer):
                    stage(l)
            for t in range(NT):
                sp.wait_ge(S["y_ready"], NT * (DEPTH - 1) + t + 1)
                dst = y_sample[0, P * t:P * t + P, :] if t < NT_S else y_prompt[0]
                sp.dma_start(dst, X[:, t, :]).then_inc(S["out_done"], 16)
            sp.wait_ge(S["out_done"], 16 * (N_OUT * DEPTH + NT))

        @block.gpsimd
        def _(pool):
            u_rows = peer_u.rearrange("l e d -> (l e) d")
            v_rows = peer_v.rearrange("l e d -> (l e) d")
            pool.memset(gla_w[:, :, :], 0.0)
            pool.memset(zero_l[:, :], 0.0)
            pool.memset(zero_r[:, :], 0.0).then_inc(S["zeros_ready"], 1)
            for l in range(DEPTH):
                if l == 0:
                    pool.wait_ge(S["m_row_done"], WIDE)
                pool.memset(UP[:, :, :], 0.0)
                pool.wait_ge(S["vec_ready"], l + 1)
                pool.wait_ge(S["ht_ps"], NT * l + NT)
                pool.drain().then_inc(S["pad_ready"], 1)
                pool.wait_ge(S["proj_ev"], NB * l + 2)
                for o, n, q in SEGS:
                    pool.tensor_tensor(UP[:, 0, q + PAD:q + PAD + n], CV[:, 0, o:o + n], CG[:, 0, o:o + n], ALU.mult)
                for j in range(TAPS):
                    pool.drain()
                    w = vec[:, j:j + 1]
                    for o, n, q in SEGS:
                        src = UP[:, 0, q + j:q + j + n]
                        if j == 0:
                            pool.tensor_scalar(CX[:, 0, o:o + n], src, w, vec[:, R_CB:R_CB + 1], ALU.mult, ALU.add)
                        else:
                            pool.tensor_scalar(CV[:, 0, o:o + n], src, w, None, ALU.mult)
                    if j:
                        pool.drain()
                        pool.tensor_tensor(CX[:, 0, :], CX[:, 0, :], CV[:, 0, :], ALU.add)
                for n in (1, 2):
                    phase_end(pool, PH * l + n)
                pool.wait_ge(S["out_done"], 16 * (N_OUT * l + 2))
                pool.memset(ST[:, :, :, :], 0.0).then_inc(S["st_zero"], 1)
                for n in (3, 4):
                    phase_end(pool, PH * l + n)
                pool.memset(KEYS[:, :, :], 0.0).then_inc(S["keys_zero"], 1)
                with pool.Fori(0, NT * HEADS) as i:
                    head = NT * HEADS * l + i
                    pool.wait_ge(S["idx_ready"], head + 1)
                    pool.sem_inc(S["pool_turn"], 1)
                    for k in range(TOPK):
                        pool.wait_ge(S["u_free"], head * TOPK + k + 1)
                        pool.sem_inc(S["pool_turn"], 1)
                        pool.indirect_dma_start(UR[:, k % RING, :], None, u_rows,
                                                bass.IndirectOffsetOnAxis(ap=idx_u[:, k:k + 1], axis=0))\
                            .then_inc(u_in[k % RING], 16)
                    pool.wait_ge(S["idxv_ready"], head + 1)
                    pool.sem_inc(S["pool_turn"], 1)
                    for k in range(TOPK):
                        pool.wait_ge(S["v_free"], head * TOPK + k + 1)
                        pool.sem_inc(S["pool_turn"], 1)
                        pool.indirect_dma_start(VR[:, k % RING, :], None, v_rows,
                                                bass.IndirectOffsetOnAxis(ap=idx_v[:, k:k + 1], axis=0))\
                            .then_inc(v_in[k % RING], 16)
                phase_end(pool, PH * l + 5)

        @block.tensor
        def _(pe):
            def mm(out, lhsT, rhs, start=True, stop=True):
                return pe.matmul(out, lhsT, rhs, start=start, stop=stop)

            def wide(out, lhsT, rhs, start=True, stop=True):
                mm(out[:, 0:512], lhsT, rhs[:, 0:512], start, stop)
                return mm(out[:, 512:NTOK], lhsT, rhs[:, 512:NTOK], start, stop)

            def start():
                pe.wait_ge(S["cond_ready"], 2)
                for n in range(WIDE):
                    pe.wait_ge(wide_in[n % 2], 16 * (n // 2 + 1))
                    if n >= 2:
                        pe.wait_ge(S["m_row_done"], n - 1)
                    for k in range(KT):
                        m = mm(PS[0:2, n % 2, :], cond_s[:, k, :], wide_slab[n % 2][:, k, :], k == 0, k == KT - 1)
                    m.then_inc(S["m_ps"], 1)
                pe.wait_ge(S["m_row_done"], WIDE)
                pe.wait_ge(S["const_in"], 16)

            def mod_block(bank, slot, loads, done):
                pe.wait_ge(slab_in[slot], loads)
                pe.wait_ge(S["m_row_done"], done)
                for k in range(KT):
                    mm(PS[0:2, bank, 0:P], cond_s[:, k, :], ada_slab[slot][:, k, :], k == 0, False)
                mm(PS[0:2, bank, 0:P], CST[0:1, C_ONE:C_ONE + 2], ada_slab[slot][0:1, KT, :], False, True)\
                    .then_inc(S["m_ps"], 1)

            def project(l):
                pe.wait_ge(S["vec_in"], 16 * 12 * (l + 1))
                pe.transpose(PS[:, 4, 0:R_END], vec_rows, CST[0:R_END, C_ID:C_ID + R_END]).then_inc(S["vec_ps"], 1)
                pe.wait_ge(S["ck_in"], 16 * (l + 1))
                pe.transpose(PS[:, 5, 0:P], CK, ident).then_inc(S["kc_ps"], 1)
                for t in range(NT):
                    pe.wait_ge(S["h_ready"], NT * l + t + 1)
                    if t >= 2:
                        pe.wait_ge(S["ht_ready"], NT * l + t - 1)
                    for k in range(KT):
                        m = pe.transpose(pair(t % 2)[:, P * k:P * k + P], hbuf[:, t % 2, P * k:P * k + P], ident)
                    m.then_inc(S["ht_ps"], 1)
                pe.wait_ge(S["ht_ready"], NT * l + NT)
                pe.wait_ge(S["vec_ready"], l + 1)
                pe.wait_ge(S["kc_ready"], l + 1)

                def variance(u):
                    pe.wait_ge(S["sq_ready"], NU * l + u + 1)
                    if u:
                        pe.wait_ge(S["sd_ready"], NU * l + u)
                    wide(pair(0), mean_mat, SQ).then_inc(S["var_ps"], 1)

                def rotated(u):
                    pe.wait_ge(S["n_ready"], NU * l + u + 1)
                    if u:
                        pe.wait_ge(S["rope_done"], NU * l + u)
                    mm(PS[:, 2, :], rot_mat, UNITS[u][0][:, 0:N_SAMPLE]).then_inc(S["rot_ps"], 1)

                for b, (_, w, _c) in enumerate(BLOCKS):
                    pe.wait_ge(win_in[b % WRING], 16 * (len(range(b % WRING, NB, WRING)) * l + b // WRING + 1))
                    if b >= 2:
                        pe.wait_ge(S["proj_ev"], NB * l + b - 1)
                    for k in range(KT):
                        m = wide(pair(2 + b % 2)[0:w], win[b % WRING][:, k, 0:w], HT[:, k, :], k == 0, k == KT - 1)
                        if l == 0 and k == 3:
                            mod_block(3, 0, 32 * (b + 1), WIDE + 2 * b)
                    m.then_inc(S["proj_ps"], 1)
                    if l == 0:
                        mod_block(3, 1, 32 * (b + 1), WIDE + 2 * b + 1)
                    if 0 <= b - 5 < NU:
                        variance(b - 5)
                    if 0 <= b - 7 < NU:
                        rotated(b - 7)
                    if b == 13:
                        pe.wait_ge(S["rope_done"], NU * (l + 1))
                        pe.transpose(PS[:, 2, 0:P], AK[:, N_SAMPLE:NTOK], ident).then_inc(S["kout_ps"], 1)
                pe.wait_ge(S["wv_in"], 32 * (l + 1))
                for t in range(NT):
                    if t >= 2:
                        pe.wait_ge(S["vt_ready"], NT * l + t - 1)
                    for k in range(KT):
                        m = mm(PS[:, t % 2, 0:384], HT[:, k, P * t:P * t + P], w_v[:, k, :], k == 0, k == KT - 1)
                    m.then_inc(S["vt_ps"], 1)

            def attention(l):
                def scores(i):
                    t, h = STEPS[i]
                    if i >= 2:
                        pe.wait_ge(S["p_ready"], NS * l + i - 1)
                    q = slice(64 * (h % 2), 64 * (h % 2) + 64)
                    k0, nk = keys_of(t)
                    for a in range(0, nk, 512):
                        b = min(nk, a + 512)
                        m = mm(pair(i % 2)[:, a:b], AQ[q, h // 2, P * t:P * t + P], KTD[q, h // 4, k0 + a:k0 + b])
                    m.then_inc(S["s_ps"], 1)

                def evacuated(i):
                    pe.wait_ge(S["pt_dve" if i % 2 else "pt_act"], NS // 2 * l + i // 2 + 1)

                def transposes(i):
                    pe.wait_ge(S["p_ready"], NS * l + i + 1)
                    if i >= 1:
                        evacuated(i - 1)
                    for s in range(keys_of(STEPS[i][0])[1] // P):
                        m = pe.transpose(pair(2)[:, P * s:P * s + P], PR[:, i % 2, P * s:P * s + P], ident)
                    m.then_inc(S["pt_ps"], 1)

                def values(i):
                    t, h = STEPS[i]
                    evacuated(i)
                    if h == 0 and t:
                        pe.wait_ge(S["o_ready"], NT * l + t)
                    v = vals_of(t)
                    for s, vt in enumerate(v):
                        m = mm(PS[:, 6, 64 * h:64 * h + 64], PRT[:, i % 2, P * s:P * s + P],
                               vt[:, 64 * (h // 4):64 * (h // 4) + 64], s == 0, s == len(v) - 1)
                    m.then_inc(S["o_ps"], 1)

                def out_transposes(t):
                    pe.wait_ge(S["o_ready"], NT * l + t + 1)
                    if t:
                        pe.wait_ge(S["ot_ready"], NT * l + t)
                    for j in range(4):
                        m = pe.transpose(PS[:, 7, P * j:P * j + P], OTOK[:, P * j:P * j + P], ident)
                    m.then_inc(S["ot_ps"], 1)

                pe.wait_ge(S["kc_ready"], l + 1)
                for kv in range(2):
                    dup = CST[:, C_DUP + P * kv:C_DUP + P * kv + P]
                    o = pair(kv)
                    mm(o[:, 0:512], dup, AK[:, 0:512])
                    mm(o[:, 512:640], dup, KC)
                    mm(o[:, 640:768], dup, AK[:, N_SAMPLE:NTOK]).then_inc(S["dup_ps"], 1)
                pe.wait_ge(S["dup_ready"], 2 * (l + 1))
                pe.wait_ge(S["misc_in"], 48 * (l + 1))
                for i in range(NS + 2):
                    if i < NS:
                        scores(i)
                    if 1 <= i <= NS:
                        transposes(i - 1)
                    if i >= 2:
                        values(i - 2)
                        if STEPS[i - 2][1] == 7:
                            out_transposes(STEPS[i - 2][0])

            def gla_out(l, s):
                hp, t = s // NT, s % NT
                pe.wait_ge(S["atm_ready"], 2 * NT * l + s + 1)
                o = pair(hp)
                for n, (dr, ch) in enumerate(((0, 2 * t), (0, 2 * t + 1), (1, 2 * t), (1, 2 * t + 1))):
                    i = 2 * dr + hp
                    cols = slice(64 * ch, 64 * ch + 64)
                    mm(o[:, cols], ST[:, i, ch, :], QD[:, i, cols], n == 0, False)
                for hb in range(2):
                    head = 2 * hp + hb
                    for dr in range(2):
                        m = mm(o[64 * hb:64 * hb + 64, P * t:P * t + P], VT[:, t, 64 * head:64 * head + 64],
                               ATM[:, s % 2, hb, dr, :], False, dr == 1)
                m.then_inc(S["og_ps"], 1)

            def gla(l):
                for ct in range(2):
                    wide(pair(ct), mean_mat, CX[:, ct, :]).then_inc(S["cx_mean"], 1)
                for i in range(4):
                    if i == 2:
                        pe.wait_ge(S["cx_cent"], 2 * (l + 1))
                    wide(zp(i), gla_w[:, i // 2, P * (i % 2):P * (i % 2) + P], GA).then_inc(S["z_ps"], 1)
                for i in range(4):
                    pe.wait_ge(S["qk_ready"], 4 * l + i + 1)
                    for t in range(NT):
                        m = pe.transpose(zp(i)[:, P * t:P * t + P], KK[:, i, P * t:P * t + P], ident)
                    m.then_inc(S["kk_ps"], 1)
                pe.wait_ge(S["kk_ready"], 4 * l + 4)
                for u, (i, ch, _n) in enumerate(UPD):
                    if u >= 8:
                        pe.wait_ge(S["st_ready"], NUPD * l + u - 7)
                    q = slice(64 * (ch % 2), 64 * (ch % 2) + 64)
                    mm(PS[:, u % 8, 0:P], KKT[q, i, ch // 2, :],
                       VT[q, ch // 2, P * (i % 2):P * (i % 2) + P]).then_inc(S["dS_ps"], 1)
                pe.wait_ge(S["st_ready"], NUPD * (l + 1))
                for s in range(2 * NT):
                    hp, t = s // NT, s % NT
                    if s >= 2:
                        pe.wait_ge(S["atm_ready"], 2 * NT * l + s - 1)
                    cols = slice(P * t, P * t + P)
                    for hb in range(2):
                        q = slice(64 * hb, 64 * hb + 64)
                        for dr in range(2):
                            i = 2 * dr + hp
                            m = mm(PS[:, 4 + 2 * (s % 2) + hb, P * dr:P * dr + P], KD[q, i, cols], QD[q, i, cols])
                    m.then_inc(S["a_ps"], 1)
                    if s >= 1:
                        gla_out(l, s - 1)
                gla_out(l, 2 * NT - 1)
                for ct in range(2):
                    pe.wait_ge(S["cx_sq"], 2 * l + ct + 1)
                    wide(pair(2 + ct), mean_mat, CSQ[:, ct, :]).then_inc(S["cx_var"], 1)
                for hp in range(2):
                    pe.wait_ge(S["og_sq"], 2 * l + hp + 1)
                    wide(pair(hp), mean_mat, OSQ[:, hp, :]).then_inc(S["og_var"], 1)

            def out_project(l):
                for t in range(NT):
                    if t >= 2:
                        pe.wait_ge(S["res_read"], NT * l + t - 1)
                    for k in range(KT):
                        if t == 0 and k % 4 == 0:
                            pe.wait_ge(wout_in[k // 4], 16 * (l + 1))
                        for hf in range(2):
                            m = mm(pair(t % 2)[:, 512 * hf:512 * hf + 512], MIX[:, k, P * t:P * t + P],
                                   WOUT[k // 4][:, k % 4, 512 * hf:512 * hf + 512], k == 0, k == KT - 1)
                    m.then_inc(S["mix_ps"], 1)

            def tile_transposes(l, t):
                n = NT * l + t
                pe.wait_ge(S["h2_ready"], n + 1)
                if t:
                    pe.wait_ge(S["sc_now"], HEADS * n)
                    if l == 0:
                        pe.wait_ge(S["m_row_done"], M_EXPERTS + 12 * t)
                for k in range(KT):
                    m = pe.transpose(pair(2)[:, P * k:P * k + P], H2[:, t % 2, P * k:P * k + P], ident)
                m.then_inc(S["h2t_ps"], 1)
                pe.wait_ge(S["h2t_ready"], n + 1)

            def query(g, h):
                if not isinstance(g, int) or g:
                    pe.wait_ge(S["q_ready"], g)
                for k in range(KT):
                    m = mm(PS[:, 6, 0:P], H2T[:, k, :], WQ[:, k, bass.ds(h * P, P)], k == 0, k == KT - 1)
                m.then_inc(S["q_ps"], 1)

            def query_transpose(g):
                pe.wait_ge(S["q_ready"], g + 1)
                pe.transpose(PS[:, 7, 0:P], QTOK, ident).then_inc(S["qt_ps"], 1)

            def key_scores(g, h):
                pe.wait_ge(S["qt_ready"], g + 1)
                mm(PS[:, 4, 0:256], QT, KEYS[:, :, :].rearrange("p h k -> p (h k)")[:, bass.ds(h * 256, 256)])\
                    .then_inc(S["sc_ps"], 1)

            def head_sum(head, ahead, block=None):
                for k in range(TOPK):
                    if block is not None and k in (4, 14):
                        j = k // 10
                        mod_block(5, j, 32 * LATE // 2 + 16 * block + 32, M_EXPERTS + block + j)
                    if ahead is not None:
                        if k == 0:
                            query(head + 2, ahead)
                        if k == 5:
                            query_transpose(head + 2)
                        if k == 10:
                            key_scores(head + 2, ahead)
                    pe.wait_ge(v_in[k % RING], head * 32 + 16 * (k // RING + 1))
                    pe.wait_ge(S["diag_ready"], head * TOPK + k + 1)
                    for cc in range(2):
                        m = mm(PS[:, cc, :], DG[:, k % DIAGS, :], VR[:, k % RING, 512 * cc:512 * cc + 512],
                               False, False)
                    m.then_inc(S["v_free"], 1)

            def peer(l):
                pe.wait_ge(S["keys_in"], 32 * (l + 1))
                for h in range(HEADS):
                    m = pe.transpose(pair(2)[:, P * h:P * h + P], KRAW[:, h, :], ident)
                m.then_inc(S["keys_ps"], 1)
                pe.wait_ge(S["keys_ready"], l + 1)
                tile_transposes(l, 0)
                pe.wait_ge(S["wq_in"], 16 * (l + 1))
                for h in range(2):
                    g = HEADS * NT * l + h
                    query(g, h)
                    query_transpose(g)
                    if h:
                        pe.wait_ge(S["sc_now"], g)
                    key_scores(g, h)
                if l == 0:
                    pe.wait_ge(S["zeros_ready"], 1)
                    pe.sem_inc(S["v_free"], RING)
                for t in range(NT):
                    n = NT * l + t
                    if n:
                        pe.wait_ge(S["acc_out"], n)
                    for cc in range(2):
                        mm(PS[:, cc, :], zero_l[:, :], zero_r[:, :], True, False)
                    with pe.Fori(0, HEADS - 2) as i:
                        head_sum(HEADS * n + i, i + 2, 12 * t + i * 2 if l == 0 and t < 4 else None)
                    if t + 1 < NT:
                        tile_transposes(l, t + 1)
                        with pe.Fori(0, 2) as i:
                            head_sum(HEADS * n + HEADS - 2 + i, i)
                    else:
                        with pe.Fori(0, 2) as i:
                            head_sum(HEADS * n + HEADS - 2 + i, None)
                    for cc in range(2):
                        m = mm(PS[:, cc, :], zero_l[:, :], zero_r[:, :], False, True)
                    m.then_inc(S["acc_done"], 1)

            start()
            for l in range(DEPTH):
                for n, stage in enumerate((project, attention, gla, out_project, peer)):
                    stage(l)
                    phase_end(pe, PH * l + n + 1)

        @block.scalar
        def _(act):
            st = Steps(act, "act")

            def start():
                act.wait_ge(S["cond_in"], 32)
                for group in GROUPS:
                    act.activation(cond_s[:, :, group], cond[:, group, :], ACT.Silu).then_inc(S["cond_ready"], 1)
                act.wait_ge(S["x_in"], 32)

            def mod_rows(bank, done, stored):
                act.wait_ge(S["m_ps"], done + 1)
                act.wait_ge(S["mod_out"], stored)
                act.activation(m_chunk, PS[0:2, bank, 0:P], ACT.Copy).then_inc(S["m_row_done"], 1)

            def project(l):
                for t in range(NT):
                    st.link(act.activation(hbuf[:, t % 2, :], X[:, t, :], ACT.Square, accum_out=sumsq[:, 0, t:t + 1]))
                act.sem_inc(S["ss_done"], 1)
                act.wait_ge(S["ms_done"], l + 1)
                act.activation(rms[:, 0:NT], rstd[:, 0:NT], ACT.Sqrt).then_inc(S["sd_done"], 1)
                act.wait_ge(S["vec_ps"], l + 1)
                act.activation(vec[:, :], PS[:, 4, 0:R_END], ACT.Copy).then_inc(S["vec_ready"], 1)
                act.wait_ge(S["kc_ps"], l + 1)
                act.activation(KC, PS[:, 5, 0:P], ACT.Copy).then_inc(S["kc_ready"], 1)
                for t in range(NT):
                    act.wait_ge(S["ht_ps"], NT * l + t + 1)
                    act.activation(HT[:, :, P * t:P * t + P], pair(t % 2).rearrange("p (k n) -> p k n", k=KT),
                                   ACT.Copy).then_inc(S["ht_ready"], 1)

                def square(u):
                    if u:
                        act.wait_ge(S["var_ps"], NU * l + u)
                    act.wait_ge(S["proj_ev"], NB * l + 4 + u + 1)
                    act.activation(SQ, UNITS[u][0], ACT.Square).then_inc(S["sq_ready"], 1)

                def deviation(u):
                    act.wait_ge(S["var_ps"], NU * l + u + 1)
                    if u:
                        act.wait_ge(S["n_ready"], NU * l + u)
                    act.activation(SD, pair(0)[:, 0:NTOK], ACT.Sqrt, bias=eps_c[:, 0:1]).then_inc(S["sd_ready"], 1)

                for b, (dst, w, _c) in enumerate(BLOCKS):
                    if l == 0:
                        mod_rows(3, WIDE + 2 * b, 16 * (2 * b + 1))
                    act.wait_ge(S["proj_ps"], NB * l + b + 1)
                    f = ACT.Sigmoid if b in (0, 2) else ACT.Silu if b >= NB - 2 else ACT.Copy
                    act.activation(dst, pair(2 + b % 2)[0:w, 0:NTOK], f).then_inc(S["proj_ev"], 1)
                    if l == 0:
                        mod_rows(3, WIDE + 2 * b + 1, 16 * (2 * b + 2))
                    if 0 <= b - 6 < NU:
                        deviation(b - 6)
                    if 0 <= b - 4 < NU:
                        square(b - 4)
                    if b == 14:
                        act.wait_ge(S["kout_ps"], l + 1)
                        act.activation(KOUT, PS[:, 2, 0:P], ACT.Copy).then_inc(S["kout_ready"], 1)
                for t in range(NT):
                    act.wait_ge(S["vt_ps"], NT * l + t + 1)
                    act.activation(VT[:, t, :], PS[:, t % 2, 0:384], ACT.Copy).then_inc(S["vt_ready"], 1)

            def attention(l):
                def softmax(i):
                    t, h = STEPS[i]
                    act.wait_ge(S["nmax_ready"], NS * l + i + 1)
                    if i >= 2:
                        act.wait_ge(S["pt_ps"], NS * l + i - 1)
                    if h == 0 and t >= 2:
                        act.wait_ge(S["o_ready"], NT * l + t - 1)
                    nk = keys_of(t)[1]
                    act.activation(PR[:, i % 2, 0:nk], pair(i % 2)[:, 0:nk], ACT.Exp, bias=nmax[:, i % 4:i % 4 + 1],
                                   scale=0.125, accum_out=psum_p[:, t % 2, h:h + 1]).then_inc(S["p_ready"], 1)

                def evacuate(i):
                    act.wait_ge(S["pt_ps"], NS * l + i + 1)
                    if i >= 2:
                        act.wait_ge(S["o_ps"], NS * l + i - 1)
                    nk = keys_of(STEPS[i][0])[1]
                    act.activation(PRT[:, i % 2, 0:nk], pair(2)[:, 0:nk], ACT.Copy).then_inc(S["pt_act"], 1)

                def out_evacuate(t):
                    act.wait_ge(S["ot_ps"], NT * l + t + 1)
                    act.activation(MIX[:, 4:8, P * t:P * t + P], PS[:, 7, :].rearrange("p (j n) -> p j n", j=4),
                                   ACT.Copy).then_inc(S["ot_ready"], 1)

                for kv in range(2):
                    act.wait_ge(S["dup_ps"], 2 * l + kv + 1)
                    act.activation(KTD[:, kv, :], pair(kv)[:, 0:768], ACT.Copy).then_inc(S["dup_ready"], 1)
                for i in range(NS + 3):
                    if i < NS:
                        softmax(i)
                    if 1 <= i <= NS and (i - 1) % 2 == 0:
                        evacuate(i - 1)
                    if i >= 3 and STEPS[i - 3][1] == 7:
                        out_evacuate(STEPS[i - 3][0])

            def gla(l):
                for i in range(4):
                    act.wait_ge(S["z_ps"], 4 * l + i + 1)
                    col = (R_ABF if i < 2 else R_ABB) + i % 2
                    act.activation(KK[:, i, :], zp(i)[:, 0:NTOK], ACT.Abs, bias=vec[:, col:col + 1])\
                        .then_inc(S["abs_done"], 1)
                act.wait_ge(S["abs_done"], 4 * l + 4)
                st.link(act.activation(KK[:, :, :], KK[:, :, :], ACT.Exp, scale=-1.0))
                act.activation(KK[:, :, :], KK[:, :, :], ACT.Ln, bias=1.0).then_inc(S["ln_done"], 1)
                for i in range(4):
                    act.wait_ge(S["b_ready"], 4 * l + i + 1)
                    act.activation(QD[:, i, :], LA[:, i, :], ACT.Exp, scale=1 / 16)
                    act.activation(KD[:, i, :], LA[:, i, :], ACT.Exp, scale=-1 / 16)
                    act.activation(KK[:, i, :], KK[:, i, :], ACT.Exp, scale=1 / 16).then_inc(S["ex_done"], 1)
                act.activation(e_last[:, :, :], e_last[:, :, :], ACT.Exp, scale=1 / 16).then_inc(S["el_ready"], 1)
                act.wait_ge(S["mod_out"], 16 * (1 + LATE))
                for i in range(4):
                    act.wait_ge(S["kk_ps"], 4 * l + i + 1)
                    act.activation(KKT[:, i, :, :], zp(i)[:, 0:NTOK].rearrange("p (t f) -> p t f", t=NT), ACT.Copy)\
                        .then_inc(S["kk_ready"], 1)
                for ct in range(2):
                    act.activation(CSQ[:, ct, :], CX[:, ct, :], ACT.Square).then_inc(S["cx_sq"], 1)
                for hp in range(2):
                    act.wait_ge(S["og_ps"], 2 * NT * l + NT * (hp + 1))
                    act.activation(OG[:, hp, :], pair(hp)[:, 0:NTOK], ACT.Copy)
                    act.activation(OSQ[:, hp, :], pair(hp)[:, 0:NTOK], ACT.Square).then_inc(S["og_sq"], 1)
                for ct in range(2):
                    act.wait_ge(S["cx_var"], 2 * l + ct + 1)
                    act.activation(CSQ[:, ct, :], pair(2 + ct)[:, 0:NTOK], ACT.Sqrt, bias=eps_c[:, 0:1])\
                        .then_inc(S["cx_sd"], 1)
                for hp in range(2):
                    act.wait_ge(S["og_var"], 2 * l + hp + 1)
                    act.activation(OSD[:, hp, :], pair(hp)[:, 0:NTOK], ACT.Sqrt, bias=eps_c[:, 0:1])\
                        .then_inc(S["og_sd"], 1)
                for ct in range(2):
                    act.wait_ge(S["cx_ready"], 2 * l + ct + 1)
                    act.activation(MIX[:, 2 + ct, :], CX[:, ct, :], ACT.Silu, bias=vec[:, R_CNB + ct:R_CNB + ct + 1])\
                        .then_inc(S["silu_done"], 1)

            def out_project(l):
                act.wait_ge(S["out_done"], 16 * N_OUT * (l + 1))
                for t in range(NT):
                    act.wait_ge(S["res_done"], NT * l + t + 1)
                    st.link(act.activation(xsq, X[:, t, :], ACT.Square, accum_out=sumsq[:, 1, t:t + 1]))
                act.sem_inc(S["ss2_done"], 1)
                act.wait_ge(S["ms2_done"], l + 1)
                act.activation(rms[:, 0:NT], rstd[:, 0:NT], ACT.Sqrt).then_inc(S["sd2_done"], 1)

            def query_out(g):
                act.wait_ge(S["q_ps"], g + 1)
                act.activation(QTOK, PS[:, 6, 0:P], ACT.Copy).then_inc(S["q_ready"], 1)

            def query_transpose_out(g):
                act.wait_ge(S["qt_ps"], g + 1)
                act.activation(QT, PS[:, 7, 0:P], ACT.Copy).then_inc(S["qt_ready"], 1)

            def scores_out(g):
                act.wait_ge(S["sc_ps"], g + 1)
                if not isinstance(g, int) or g:
                    act.wait_ge(S["sc_taken"], g)
                act.activation(SCC[:, :, :].rearrange("p a b -> p (a b)"), PS[:, 4, 0:256], ACT.Copy)\
                    .then_inc(S["sc_now"], 1)

            def head_weights(head, ahead, block=None):
                act.wait_ge(S["idx_ready"], head + 1)
                act.activation(gexp[:, :], centred[:, :], ACT.Exp, accum_out=gsum[:, 0:1])
                act.wait_ge(S["u_free"], head * TOPK + TOPK + RING)
                act.activation(gelu_h[:, :], act_h[:, :], ACT.Gelu).then_inc(S["gelu_done"], 1)
                act.wait_ge(S["w_ready"], head + 1)
                for k in range(TOPK):
                    if ahead:
                        if k == 2:
                            query_out(head + 2)
                        if k == 7:
                            query_transpose_out(head + 2)
                        if k == 12:
                            scores_out(head + 2)
                    if block is not None and k in (6, 15):
                        mod_rows(5, M_EXPERTS + block + k // 10, 16 * (1 + LATE) + block * 16 + 16 * (k // 10))
                    act.wait_ge(S["v_free"], head * TOPK + k + 1 + RING - DIAGS)
                    act.activation(DG[:, k % DIAGS, :], ident, ACT.Copy, scale=w_h[:, k:k + 1])\
                        .then_inc(S["diag_ready"], 1)

            def tile_out(l, t):
                act.wait_ge(S["h2t_ps"], NT * l + t + 1)
                act.activation(H2T[:, :, :], pair(2).rearrange("p (k n) -> p k n", k=KT), ACT.Copy)\
                    .then_inc(S["h2t_ready"], 1)

            def peer(l):
                act.wait_ge(S["keys_ps"], l + 1)
                act.wait_ge(S["keys_zero"], l + 1)
                kv = pair(2).rearrange("p (h k) -> p h k", h=HEADS)
                act.activation(KEYS[0:64, :, 0:128], kv[0:64], ACT.Copy)
                act.activation(KEYS[64:128, :, 128:256], kv[64:128], ACT.Copy).then_inc(S["keys_ready"], 1)
                tile_out(l, 0)
                for h in range(2):
                    g = HEADS * NT * l + h
                    query_out(g)
                    query_transpose_out(g)
                    scores_out(g)
                for t in range(NT):
                    n = NT * l + t
                    with act.Fori(0, HEADS - 2) as i:
                        head_weights(HEADS * n + i, True, 12 * t + i * 2 if l == 0 and t < 4 else None)
                    if t + 1 < NT:
                        tile_out(l, t + 1)
                    with act.Fori(0, 2) as i:
                        head_weights(HEADS * n + HEADS - 2 + i, t + 1 < NT)
                    act.wait_ge(S["acc_done"], n + 1)
                    if n:
                        act.wait_ge(S["y_ready"], n)
                    act.activation(TMP, pair(0), ACT.Copy).then_inc(S["acc_out"], 1)

            start()
            for l in range(DEPTH):
                for n, stage in enumerate((project, attention, gla, out_project, peer)):
                    stage(l)
                    phase_end(act, PH * l + n + 1)

        @block.vector
        def _(dve):
            st = Steps(dve, "dve")
            tt, stt, ts = dve.tensor_tensor, dve.scalar_tensor_tensor, dve.tensor_scalar

            def start():
                dve.memset(eps_c[:, :], EPS)
                dve.wait_ge(S["adab_in"], 16)
                for n in range(WIDE):
                    dve.wait_ge(S["m_ps"], n + 1)
                    w = slice(512 * n, 512 * n + 512)
                    tt(m_row[:, w], PS[0:2, n % 2, :], ada_bias[:, w], ALU.add).then_inc(S["m_row_done"], 1)

            def scale_gain(mod, gain):
                for g in GROUPS:
                    st.do(stt(mod[:, 1, g, :], mod[:, 1, g, :], 1.0, gain, ALU.add, ALU.mult))
                st.after(st.n)

            def project(l):
                dve.wait_ge(S["ss_done"], l + 1)
                ts(rstd[:, 0:NT], sumsq[:, 0, 0:NT], 1.0 / D, EPS, ALU.mult, ALU.add).then_inc(S["ms_done"], 1)
                dve.wait_ge(S["sd_done"], l + 1)
                st.link(dve.reciprocal(rstd[:, 0:NT], rms[:, 0:NT]))
                dve.wait_ge(S["gain1_in"], 16 * (l + 1))
                dve.wait_ge(S["mod_in"], 32 * (l + 1))
                scale_gain(MOD1, gain1)
                for t in range(NT):
                    if t >= 2:
                        dve.wait_ge(S["ht_ps"], NT * l + t - 1)
                    g = group_of(t)
                    st.link(stt(hbuf[:, t % 2, :], X[:, t, :], rstd[:, t:t + 1], MOD1[:, 1, g, :], ALU.mult, ALU.mult))
                    tt(hbuf[:, t % 2, :], hbuf[:, t % 2, :], MOD1[:, 0, g, :], ALU.add).then_inc(S["h_ready"], 1)
                for u, (src, g) in enumerate(UNITS):
                    dve.wait_ge(S["sd_ready"], NU * l + u + 1)
                    st.link(dve.reciprocal(SD, SD))
                    stt(src, src, vec[:, g:g + 1], SD, ALU.mult, ALU.mult).then_inc(S["n_ready"], 1)
                    dve.wait_ge(S["rot_ps"], NU * l + u + 1)
                    s5 = src[:, 0:N_SAMPLE]
                    st.do(tt(RT, PS[:, 2, :], sin_t, ALU.mult))
                    st.link(tt(s5, s5, cos_t, ALU.mult))
                    tt(s5, s5, RT, ALU.add).then_inc(S["rope_done"], 1)
                    dve.wait_ge(S["rope_done"], NU * l + u + 1)
                dve.wait_ge(S["pad_ready"], l + 1)
                dve.wait_ge(S["proj_ev"], NB * l + 4)
                for o, n, q in SEGS:
                    st.do(tt(UP[:, 1, q + PAD:q + PAD + n], CV[:, 1, o:o + n], CG[:, 1, o:o + n], ALU.mult))
                for j in range(TAPS):
                    w = vec[:, TAPS + j:TAPS + j + 1]
                    for o, n, q in SEGS:
                        st.after(st.n - 1)
                        src, dst = UP[:, 1, q + j:q + j + n], CX[:, 1, o:o + n]
                        if j == 0:
                            st.do(ts(dst, src, w, vec[:, R_CB + 1:R_CB + 2], ALU.mult, ALU.add))
                        else:
                            st.do(stt(dst, src, w, dst, ALU.mult, ALU.add))
                st.after(st.n)

            def attention(l):
                def maxima(i):
                    t, h = STEPS[i]
                    dve.wait_ge(S["s_ps"], NS * l + i + 1)
                    if i >= 4:
                        dve.wait_ge(S["p_ready"], NS * l + i - 3)
                    st.link(dve.reduce_max(smax[:, i % 4:i % 4 + 1], pair(i % 2)[:, 0:keys_of(t)[1]], AX.X))
                    ts(nmax[:, i % 4:i % 4 + 1], smax[:, i % 4:i % 4 + 1], -0.125, None, ALU.mult)\
                        .then_inc(S["nmax_ready"], 1)

                def evacuate(i):
                    dve.wait_ge(S["pt_ps"], NS * l + i + 1)
                    if i >= 2:
                        dve.wait_ge(S["o_ps"], NS * l + i - 1)
                    nk = keys_of(STEPS[i][0])[1]
                    dve.tensor_copy(PRT[:, i % 2, 0:nk], pair(2)[:, 0:nk]).then_inc(S["pt_dve"], 1)

                def normalise(t):
                    dve.wait_ge(S["o_ps"], NS * l + 8 * t + 8)
                    if t:
                        dve.wait_ge(S["ot_ps"], NT * l + t)
                    st.link(dve.reciprocal(prec[:, :], psum_p[:, t % 2, :]))
                    tt(OTOK.rearrange("p (h e) -> p h e", h=8), PS[:, 6, :].rearrange("p (h e) -> p h e", h=8),
                       prec[:, :].unsqueeze(2).to_broadcast([P, 8, 64]), ALU.mult).then_inc(S["o_ready"], 1)

                for i in range(NS + 2):
                    if i < NS:
                        maxima(i)
                    if 1 <= i <= NS and (i - 1) % 2:
                        evacuate(i - 1)
                    if i >= 2 and STEPS[i - 2][1] == 7:
                        normalise(STEPS[i - 2][0])

            def gla(l):
                for ct in range(2):
                    dve.wait_ge(S["cx_mean"], 2 * l + ct + 1)
                    tt(CX[:, ct, :], CX[:, ct, :], pair(ct)[:, 0:NTOK], ALU.subtract).then_inc(S["cx_cent"], 1)
                for i in range(4):
                    dve.wait_ge(S["abs_done"], 4 * l + i + 1)
                    col = (R_ABF if i < 2 else R_ABB) + i % 2
                    st.do(ts(LA[:, i, :], zp(i)[:, 0:NTOK], vec[:, col:col + 1], 0.0, ALU.add, ALU.min))
                st.after(st.n)
                dve.wait_ge(S["ln_done"], l + 1)
                st.link(tt(LA[:, :, :], LA[:, :, :], KK[:, :, :], ALU.subtract))
                for i in range(4):
                    b = QD[:, i, :]
                    st.link(dve.tensor_tensor_scan(b, scan_keep, LA[:, i, :], 0.0, ALU.mult, ALU.add))
                    bch = b.rearrange("p (c s) -> p c s", c=NCH)
                    lch = LA[:, i, :].rearrange("p (c s) -> p c s", c=NCH)
                    kch = KK[:, i, :].rearrange("p (c s) -> p c s", c=NCH)
                    total = bch[:, :, CHUNK - 1:CHUNK].to_broadcast([P, NCH, CHUNK])
                    st.do(dve.tensor_copy(e_last[:, i, :].unsqueeze(2), bch[:, :, CHUNK - 1:CHUNK]))
                    if i < 2:
                        st.do(tt(kch, total, bch, ALU.subtract))
                        st.link(dve.tensor_copy(LA[:, i, :], b))
                    else:
                        st.link(tt(kch, bch, lch, ALU.subtract))
                        st.link(tt(lch, total, kch, ALU.subtract))
                    dve.sem_inc(S["b_ready"], 1)
                for i in range(4):
                    hp = i % 2
                    dve.wait_ge(S["ex_done"], 4 * l + i + 1)
                    st.do(stt(QD[:, i, :], GQ[:, hp, :], 0.125, QD[:, i, :], ALU.mult, ALU.mult))
                    st.do(tt(KD[:, i, :], GK[:, hp, :], KD[:, i, :], ALU.mult))
                    tt(KK[:, i, :], GK[:, hp, :], KK[:, i, :], ALU.mult).then_inc(S["qk_ready"], 1)
                dve.wait_ge(S["el_ready"], l + 1)
                dve.wait_ge(S["st_in"], 16 * 8 * (l + 1))
                for u, (i, ch, nxt) in enumerate(UPD):
                    dve.wait_ge(S["dS_ps"], NUPD * l + u + 1)
                    if u >= 4:
                        dve.wait_ge(S["st_ready"], NUPD * l + u - 3)
                    for hb in range(2):
                        q = slice(64 * hb, 64 * hb + 64)
                        ins = stt(ST[q, i, nxt, q], ST[q, i, ch, q], e_last[q, i, ch:ch + 1],
                                  PS[q, u % 8, q], ALU.mult, ALU.add)
                    ins.then_inc(S["st_ready"], 1)
                for s in range(2 * NT):
                    dve.wait_ge(S["a_ps"], 2 * NT * l + s + 1)
                    if s >= 2:
                        dve.wait_ge(S["og_ps"], 2 * NT * l + s - 1)
                    for hb in range(2):
                        ins = tt(ATM[:, s % 2, hb, :, :],
                                 PS[:, 4 + 2 * (s % 2) + hb, 0:256].rearrange("p (d i) -> p d i", d=2), masks, ALU.mult)
                    ins.then_inc(S["atm_ready"], 1)
                for ct in range(2):
                    dve.wait_ge(S["cx_sd"], 2 * l + ct + 1)
                    st.link(dve.reciprocal(CSQ[:, ct, :], CSQ[:, ct, :]))
                    stt(CX[:, ct, :], CX[:, ct, :], vec[:, R_CNG + ct:R_CNG + ct + 1], CSQ[:, ct, :],
                        ALU.mult, ALU.mult).then_inc(S["cx_ready"], 1)
                for hp in range(2):
                    dve.wait_ge(S["og_sd"], 2 * l + hp + 1)
                    st.link(dve.reciprocal(OSD[:, hp, :], OSD[:, hp, :]))
                    st.link(stt(OG[:, hp, :], OG[:, hp, :], vec[:, R_GLG + hp:R_GLG + hp + 1], OSD[:, hp, :],
                                ALU.mult, ALU.mult))
                    tt(MIX[:, hp, :], OG[:, hp, :], GG[:, hp, :], ALU.mult).then_inc(S["og_done"], 1)

            def out_project(l):
                dve.wait_ge(S["gain2_in"], 16 * (l + 1))
                dve.wait_ge(S["mod2_in"], 32 * (l + 1))
                scale_gain(MOD2, gain2)
                dve.wait_ge(S["gate_in"], 32 * (l + 1))
                for t in range(NT):
                    dve.wait_ge(S["mix_ps"], NT * l + t + 1)
                    tt(TMP, pair(t % 2), MOD1[:, 2, group_of(t), :], ALU.mult).then_inc(S["res_read"], 1)
                    dve.wait_ge(S["res_read"], NT * l + t + 1)
                    tt(X[:, t, :], X[:, t, :], TMP, ALU.add).then_inc(S["res_done"], 1)
                    dve.wait_ge(S["res_done"], NT * l + t + 1)
                dve.wait_ge(S["ss2_done"], l + 1)
                ts(rstd[:, 0:NT], sumsq[:, 1, 0:NT], 1.0 / D, EPS, ALU.mult, ALU.add).then_inc(S["ms2_done"], 1)
                dve.wait_ge(S["sd2_done"], l + 1)
                st.link(dve.reciprocal(rstd[:, 0:NT], rms[:, 0:NT]))

            def normed(l, t):
                if t >= 2:
                    dve.wait_ge(S["h2t_ps"], NT * l + t - 1)
                h, g = H2[:, t % 2, :], group_of(t)
                st.link(stt(h, X[:, t, :], rstd[:, t:t + 1], MOD2[:, 1, g, :], ALU.mult, ALU.mult))
                tt(h, h, MOD2[:, 0, g, :], ALU.add).then_inc(S["h2_ready"], 1)

            def top16(vals, inds, src, spare):
                dve.max(vals[:, 0:8], src)
                dve.drain()
                dve.max_index(inds[:, 0:8], vals[:, 0:8], src)
                dve.match_replace(spare, vals[:, 0:8], src, -3.0e38)
                dve.drain()
                dve.max(vals[:, 8:16], spare)
                dve.drain()
                dve.max_index(inds[:, 8:16], vals[:, 8:16], spare)

            def route(l, head):
                dve.wait_ge(S["sc_now"], head + 1)
                dve.sem_inc(S["dve_turn"], 1)
                for s in range(2):
                    top16(top_v[:, s, :], top_i[:, s, :], SCC[:, s, :], SC2[:, s, :])
                dve.drain().then_inc(S["sc_taken"], 1)
                tt(CAND.rearrange("p (a b) -> p a b", a=16), top_v[:, 0, :].unsqueeze(2).to_broadcast([P, 16, 16]),
                   top_v[:, 1, :].unsqueeze(1).to_broadcast([P, 16, 16]), ALU.add)
                dve.tensor_copy(top_if[:, :, :], top_i[:, :, :])
                dve.drain()
                top16(best[:, :], pos[:, :], CAND, CAND2)
                dve.drain()
                ts(centred[:, :], best[:, :], best[:, 0:1], None, ALU.subtract)
                ts(pos2[:, 0, :], pos[:, :], 4, None, ALU.logical_shift_right)
                ts(pos2[:, 1, :], pos[:, :], 15, None, ALU.bitwise_and)
                dve.drain()
                dve.tensor_copy(pos_f[:, :, :], pos2[:, :, :])
                dve.drain()
                oh = OH.rearrange("p (a b) -> p a b", a=32)
                oh4 = OH.rearrange("p (s a b) -> p s a b", s=2, a=16)
                tt(oh, pos_f[:, :, :].rearrange("p s k -> p (s k)").unsqueeze(2).to_broadcast([P, 32, 16]),
                   iota16.unsqueeze(1).to_broadcast([P, 32, 16]), ALU.is_equal)
                dve.drain()
                tt(oh4, oh4, top_if[:, :, :].unsqueeze(2).to_broadcast([P, 2, 16, 16]), ALU.mult)
                dve.drain()
                dve.reduce_sum(chosen[:, :, :].rearrange("p s k -> p (s k)"), oh, AX.X)
                dve.drain()
                stt(chosen_e[:, :], chosen[:, 0, :], float(NKEYS), chosen[:, 1, :], ALU.mult, ALU.add)
                dve.drain()
                ts(idx_u[:, :], chosen_e[:, :], float(EXPERTS * l), None, ALU.add).then_inc(S["idx_ready"], 1)

            def head_dots(head):
                for k in range(TOPK):
                    if k == 9:
                        dve.wait_ge(S["v_free"], head * TOPK + RING)
                        dve.tensor_copy(idx_v[:, :], idx_u[:, :]).then_inc(S["idxv_ready"], 1)
                    dve.wait_ge(u_in[k % RING], head * 32 + 16 * (k // RING + 1))
                    dve.tensor_tensor_reduce(out=UR[:, k % RING, :], in0=UR[:, k % RING, :], in1=pair(1),
                                             scale=1.0, scalar=0.0, op0=ALU.mult, op1=ALU.add,
                                             accum_out=act_h[:, k:k + 1]).then_inc(S["u_free"], 1)
                dve.wait_ge(S["gelu_done"], head + 1)
                dve.sem_inc(S["dve_turn"], 1)
                dve.reciprocal(grec[:, :], gsum[:, :])
                dve.drain()
                stt(w_h[:, :], gelu_h[:, :], grec[:, 0:1], gexp[:, :], ALU.mult, ALU.mult).then_inc(S["w_ready"], 1)

            def residual(l, t):
                dve.wait_ge(S["acc_out"], NT * l + t + 1)
                st.link(tt(TMP, TMP, MOD2[:, 2, group_of(t), :], ALU.mult))
                tt(X[:, t, :], X[:, t, :], TMP, ALU.add).then_inc(S["y_ready"], 1)

            def peer(l):
                normed(l, 0)
                route(l, HEADS * NT * l)
                if l == 0:
                    dve.sem_inc(S["u_free"], RING)
                for t in range(NT):
                    n = NT * l + t
                    dve.drain()
                    dve.tensor_copy(pair(1), H2[:, t % 2, :])
                    if t + 1 < NT:
                        normed(l, t + 1)
                    dve.drain()
                    with dve.Fori(0, HEADS if t + 1 < NT else HEADS - 1) as i:
                        head_dots(HEADS * n + i)
                        route(l, HEADS * n + 1 + i)
                        dve.drain()
                    if t + 1 == NT:
                        head_dots(HEADS * n + HEADS - 1)
                    if t:
                        residual(l, t - 1)
                residual(l, NT - 1)

            start()
            for l in range(DEPTH):
                for n, stage in enumerate((project, attention, gla, out_project, peer)):
                    stage(l)
                    phase_end(dve, PH * l + n + 1)


def shape_constants():
    t = np.zeros((P, C_END), np.float32)
    p = np.arange(P)
    t[:, C_ID:C_ID + P] = np.eye(P)
    t[:, C_MEAN:C_MEAN + P] = (p[:, None] // 64 == p[None, :] // 64) / 64.0
    low = p % 32 < 16
    t[np.where(low, p + 16, p - 16), C_ROT + p] = np.where(low, -1.0, 1.0)
    for kv in range(2):
        t[kv * 64 + p % 64, C_DUP + P * kv + p] = 1.0
    same = p[:, None] // CHUNK == p[None, :] // CHUNK
    t[:, C_MASK:C_MASK + P] = same & (p[:, None] <= p[None, :])
    t[:, C_MASK + P:C_MASK + 2 * P] = same & (p[:, None] >= p[None, :])
    tok = np.arange(N_SAMPLE)
    freq = np.float32(10000.0) ** (-np.arange(16, dtype=np.float32) / np.float32(16))
    where = np.where((p % 64 < 32)[:, None], (tok // 64)[None, :], (tok % 64)[None, :]).astype(np.float32)
    angle = where * freq[p % 16][:, None]
    t[:, C_COS:C_COS + N_SAMPLE] = np.cos(angle)
    t[:, C_SIN:C_SIN + N_SAMPLE] = np.sin(angle)
    t[:, C_SCAN:C_SCAN + NTOK] = np.arange(NTOK) % CHUNK != 0
    t[:, C_ONE:C_ONE + 2] = 1.0
    t[:, C_IOTA:C_IOTA + 16] = np.arange(16)
    return t


_INS = ['x_prompt', 'x_sample', 'c', 'cache_k', 'cache_v', 'state_gla', 'c_ctx', 'ada_w', 'ada_b', 'norm1_g',
        'norm2_g', 'w_in', 'gla_a_w_f', 'gla_a_b_f', 'gla_a_w_b', 'gla_a_b_b', 'gla_norm_g', 'conv_w', 'conv_b',
        'conv_norm_g', 'conv_norm_b', 'q_norm_g', 'k_norm_g', 'w_out', 'peer_wq', 'peer_keys', 'peer_u', 'peer_v']
_OUTS = [(1, 128, 1024), (1, 512, 1024), (1, 2, 128, 2, 64), (1, 2, 128, 2, 64), (1, 2, 2, 4, 64, 64)]


def kernel(**inputs):
    import numpy as _np
    import concourse.bacc as _bacc
    from concourse import mybir as _mybir
    from concourse.bass_utils import run_bass_kernel_spmd as _run

    nc = _bacc.Bacc("TRN2", target_bir_lowering=False, num_devices=1)
    arrays, args = {}, []
    for name in _INS:
        a = _np.ascontiguousarray(inputs[name])
        arrays[f"in_{name}"] = a
        args.append(nc.dram_tensor(f"in_{name}", a.shape, _mybir.dt.from_np(a.dtype), kind="ExternalInput").ap())
    arrays["in_consts"] = shape_constants()
    args.append(nc.dram_tensor("in_consts", (P, C_END), F32, kind="ExternalInput").ap())
    for i, shape in enumerate(_OUTS):
        args.append(nc.dram_tensor(f"out_{i}", shape, F32, kind="ExternalOutput").ap())
    build(nc, *args)
    r = _run(nc, [arrays], core_ids=[0])
    return tuple(r.results[0][f"out_{i}"] for i in range(len(_OUTS)))
```

```python
import numpy as np
import concourse.bass as bass
from concourse import mybir
from contextlib import ExitStack

F32 = mybir.dt.float32
U32 = mybir.dt.uint32
BF16 = mybir.dt.bfloat16
ALU = mybir.AluOpType
ACT = mybir.ActivationFunctionType
AX = mybir.AxisListType

P = 128
D = 1024
KT = D // P
DEPTH = 2
N_SAMPLE, N_PROMPT = 512, 128
NTOK = N_SAMPLE + N_PROMPT
NT = NTOK // P
NT_S = N_SAMPLE // P
CHUNK = 64
NCH = NTOK // CHUNK
TAPS = 31
PAD = TAPS // 2
EPS = 1e-6
NCOLS = 2336
GQ0, GK0, GV0, GG0, GA0, CV0, CG0, AQ0, AK0, AV0 = 0, 256, 512, 768, 1024, 1056, 1312, 1568, 2080, 2208
HEADS, TOPK, NKEYS = 8, 16, 128
EXPERTS = NKEYS * NKEYS
WRING = 3
RING = 8
DIAGS = 4

C_ID, C_MEAN, C_ROT, C_DUP, C_MASK, C_COS, C_SIN, C_SCAN, C_IOTA, C_ONE = (
    0, 128, 256, 384, 640, 896, 1408, 1920, 2560, 2576)
C_END = 2578
R_CB, R_CNG, R_CNB, R_GLG, R_ABF, R_ABB, R_QG, R_KG, R_END = 62, 64, 66, 68, 70, 72, 74, 75, 76


def group_of(t):
    return 0 if t < NT_S else 1


def build(nc, x_prompt, x_sample, c, cache_k, cache_v, state_gla, c_ctx, ada_w, ada_b, norm1_g, norm2_g,
          w_in, gla_a_w_f, gla_a_b_f, gla_a_w_b, gla_a_b_b, gla_norm_g, conv_w, conv_b,
          conv_norm_g, conv_norm_b, q_norm_g, k_norm_g, w_out, peer_wq, peer_keys, peer_u, peer_v,
          consts, y_prompt, y_sample, new_k, new_v, new_state):
    ctx = ExitStack()
    with ctx:
        def sb(name, shape, dt=F32):
            return ctx.enter_context(nc.sbuf_tensor(name, shape, dt))

        def sem(name):
            return ctx.enter_context(nc.semaphore(name))

        CST = sb("constants", [P, C_END])
        X = sb("residual", [P, NT, D])
        MOD2 = sb("peer_modulation", [P, 3, 2, D])
        ident = CST[:, C_ID:C_ID + P]
        mean_mat = CST[:, C_MEAN:C_MEAN + P]
        rot_mat = CST[:, C_ROT:C_ROT + P]
        masks = CST[:, C_MASK:C_MASK + 256].rearrange("p (a b) -> p a b", a=2)
        cos_t = CST[:, C_COS:C_COS + N_SAMPLE]
        sin_t = CST[:, C_SIN:C_SIN + N_SAMPLE]
        scan_keep = CST[:, C_SCAN:C_SCAN + NTOK]
        iota16 = CST[:, C_IOTA:C_IOTA + 16]

        cond = sb("cond", [P, 2, KT])
        cond_s = sb("cond_silu", [P, KT, 2])
        sumsq = sb("sumsq", [P, 2, 8])
        rms = sb("rms", [P, 8])
        rstd = sb("rstd", [P, 8])
        vec = sb("vec_columns", [P, R_END])
        eps_c = sb("eps_column", [P, 1])
        gla_w = sb("gla_gate_w", [32, 2, 256])
        e_last = sb("gla_chunk_decay", [P, 4, NCH])
        smax = sb("score_max", [P, 4])
        nmax = sb("score_neg_max", [P, 4])
        psum_p = sb("softmax_sum", [P, 2, 8])
        prec = sb("softmax_rec", [P, 8])
        top_v = sb("top_values", [P, 2, 16])
        top_i = sb("top_indices", [P, 2, 16], U32)
        top_if = sb("top_indices_f", [P, 2, 16])
        best = sb("best_scores", [P, 16])
        pos = sb("best_positions", [P, 16], U32)
        pos2 = sb("best_pos_split", [P, 2, 16], U32)
        pos_f = sb("best_pos_f", [P, 2, 16])
        chosen = sb("chosen_pair", [P, 2, 16])
        chosen_e = sb("chosen_expert", [P, 16])
        idx_u = sb("rows_for_u", [P, 16], U32)
        idx_v = sb("rows_for_v", [P, 16], U32)
        centred = sb("centred_scores", [P, 16])
        gexp = sb("gate_exp", [P, 16])
        gsum = sb("gate_sum", [P, 1])
        grec = sb("gate_rec", [P, 1])
        act_h = sb("expert_act", [P, 16])
        gelu_h = sb("expert_gelu", [P, 16])
        w_h = sb("expert_weight", [P, 16])
        zero_l = sb("zero_lhs", [P, P], BF16)
        zero_r = sb("zero_rhs", [P, 512], BF16)
        A = sb("arena", [P, 37680])

        def at(start, n):
            return A[:, start:start + n]

        def at3(start, a, b):
            return A[:, start:start + a * b].rearrange("p (a b) -> p a b", a=a)

        MOD1 = A[:, 0:6144].rearrange("p (r g d) -> p r g d", r=3, g=2)
        wide_slab = [at3(i, KT, 512) for i in (21504, 25600, 6144, 13312)]
        m_row = A[0:2, 29696:31744]
        ada_bias = A[0:2, 31744:33792]
        ada_slab = [at3(35192 + 1152 * i, KT + 1, P) for i in range(2)]
        m_chunk = A[0:2, 37496:37624]
        HT = at3(6144, KT, NTOK)
        hbuf = at3(11264, 2, D)
        w_v = at3(13312, KT, 384)
        win = [at3(16384 + 1024 * i, KT, P) for i in range(WRING)]
        SQ = at(19456, NTOK)
        SD = at(20096, NTOK)
        RT = at(20736, N_SAMPLE)
        CK = at(21248, P)
        KC = at(21376, P)
        CV = at3(21504, 2, NTOK)
        CG = at3(22784, 2, NTOK)
        AQ = at3(24064, 4, NTOK)
        gain1 = at(33144, D)
        AK = at(26624, NTOK)
        GA = A[0:32, 27264:27904]
        GK = at3(27904, 2, NTOK)
        GQ = at3(29184, 2, NTOK)
        GG = at3(30464, 2, NTOK)
        UPW = N_SAMPLE + N_PROMPT + 4 * PAD
        UP = at3(31744, 2, UPW)
        VT = at3(33144, NT, 384)
        vec_rows = A[0:R_END, 24064:24192]
        CX = at3(11264, 2, NTOK)
        CVAL = at(12544, P)
        KOUT = at(12672, P)
        MIX = at3(6144, KT, NTOK)
        KTD = at3(16512, 2, 768)
        PR = at3(18432, 2, NTOK)
        PRT = at3(19712, 2, NTOK)
        OTOK = at(20992, 512)
        LZ = at3(21504, 4, NTOK)
        ST = A[:, 12544:18176].rearrange("p (i s e) -> p i s e", i=4, s=11)
        LA = at3(0, 4, NTOK)
        KK = at3(20736, 4, NTOK)
        QD = at3(18176, 4, NTOK)
        KD = at3(23296, 4, NTOK)
        KKT = A[:, 35064:37624].rearrange("p (i t f) -> p i t f", i=4, t=NT)
        ATM = A[:, 31744:32768].rearrange("p (r h d i) -> p r h d i", r=2, h=2, d=2)
        OG = at3(20736, 2, NTOK)
        OSQ = at3(22016, 2, NTOK)
        OSD = at3(25856, 2, NTOK)
        CSQ = at3(25856, 2, NTOK)
        WOUT = [at3(0, 4, D), at3(12288, 4, D)]
        TMP = at(34168, D)
        gain2 = at(35192, D)
        xsq = at(11264, D)
        UR = at3(0, RING, D)
        VR = at3(8192, RING, D)
        WQ = at3(16384, KT, D)
        H2 = at3(26624, 2, D)
        H2T = at3(28672, KT, P)
        KRAW = at3(32000, HEADS, P)
        QTOK = at(29696, P)
        QT = at(29824, P)
        SCC = at3(29952, 2, NKEYS)
        SC2 = at3(30208, 2, NKEYS)
        CAND = at(30464, 256)
        CAND2 = at(30720, 256)
        OH = at(30976, 512)
        DG = at3(31488, DIAGS, P)
        KEYS = at3(24576, HEADS, 256)

        PS = ctx.enter_context(nc.psum_tensor("ps", [P, 8, 512], F32))
        PSF = PS[:, :, :].rearrange("p b n -> p (b n)")

        def pair(i):
            return PSF[:, 1024 * i:1024 * i + 1024]

        def zp(i):
            return pair((i + 2) % 4)

        S = {n: sem(n) for n in (
            "const_in", "cond_in", "x_in", "adab_in", "gain1_in", "gain2_in", "mod_in", "gate_in", "mod2_in", "vec_in",
            "wv_in", "ck_in", "misc_in", "st_in", "keys_in", "wq_in",
            "cond_ready", "m_ps", "m_row_done", "mod_out",
            "ss_done", "ms_done", "sd_done", "h_ready", "ht_ps", "ht_ready", "vec_ps", "vec_ready", "proj_ps",
            "proj_ev", "vt_ps", "vt_ready", "kc_ps", "kc_ready", "sq_ready", "var_ps", "sd_ready", "n_ready",
            "rot_ps", "rope_done", "kout_ps", "kout_ready", "pad_ready",
            "dup_ps", "dup_ready", "s_ps", "nmax_ready", "p_ready", "pt_ps", "pt_act", "pt_dve", "o_ps", "o_ready",
            "ot_ps", "ot_ready",
            "cx_mean", "cx_cent", "cx_sq", "cx_var", "cx_sd", "cx_ready",
            "z_ps", "z_ready", "conv_done", "ln_done", "b_ready", "ex_done", "el_ready", "qk_ready", "kk_ps",
            "kk_ready", "st_zero", "dS_ps", "st_ready", "a_ps", "atm_ready", "og_ps", "og_sq", "og_var", "og_sd",
            "mix_ps", "res_read", "res_done",
            "keys_zero", "keys_ps", "keys_ready", "ss2_done", "ms2_done", "sd2_done", "h2_ready", "h2t_ps", "h2t_ready",
            "q_ps", "q_ready", "qt_ps", "qt_ready", "sc_ps", "sc_now", "sc_taken", "idx_ready", "idxv_ready", "u_free",
            "v_free", "gelu_done", "w_ready", "diag_ready", "acc_done", "acc_out", "y_ready", "zeros_ready",
            "pool_turn", "dve_turn",
            "out_done", "phase")}
        wide_in = [sem(f"wide_in{i}") for i in range(4)]
        slab_in = [sem(f"slab_in{i}") for i in range(2)]
        win_in = [sem(f"win_in{i}") for i in range(WRING)]
        wout_in = [sem(f"wout_in{i}") for i in range(2)]
        u_in = [sem(f"u_in{i}") for i in range(RING)]
        v_in = [sem(f"v_in{i}") for i in range(RING)]
        step_sem = {e: sem(f"{e}_step") for e in ("dve", "act")}

        class Steps:
            def __init__(self, eng, which):
                self.eng, self.sem, self.n = eng, step_sem[which], 0

            def do(self, ins):
                self.n += 1
                ins.then_inc(self.sem, 1)

            def after(self, n):
                self.eng.wait_ge(self.sem, n)

            def link(self, ins):
                self.do(ins)
                self.after(self.n)

        PH = 3

        def phase_end(eng, n):
            eng.drain().then_inc(S["phase"], 1)
            eng.wait_ge(S["phase"], 4 * n)

        BLOCKS = ([(CG[:, 0, :], P, CG0), (CV[:, 0, :], P, CV0), (CG[:, 1, :], P, CG0 + P), (CV[:, 1, :], P, CV0 + P)]
                  + [(AK, P, AK0)] + [(AQ[:, j, :], P, AQ0 + P * j) for j in range(4)]
                  + [(GA, 32, GA0)]
                  + [(GK[:, j, :], P, GK0 + P * j) for j in range(2)]
                  + [(GQ[:, j, :], P, GQ0 + P * j) for j in range(2)]
                  + [(GG[:, j, :], P, GG0 + P * j) for j in range(2)])
        NB = len(BLOCKS)
        M_BLOCKS = 6 * KT
        WIDE = 4
        LATE = M_BLOCKS - 4 * WIDE
        M_EXPERTS = WIDE + LATE
        scratch = nc.dram_tensor("modulation_rows", (DEPTH, 2, 6 * D), F32, kind="Internal").ap()

        UNITS = [(AK, R_KG)] + [(AQ[:, j, :], R_QG) for j in range(4)]
        NU = len(UNITS)
        STEPS = [(t, h) for t in range(NT) for h in range(8)]
        NS = len(STEPS)

        def keys_of(t):
            return (0, NTOK) if t < NT_S else (NTOK, P)

        def vals_of(t):
            return [VT[:, s, 256:384] for s in range(NT_S)] + [CVAL] if t < NT_S else [VT[:, NT_S, 256:384]]

        def updates():
            out = []
            for n in range(9):
                for i in range(4):
                    if i < 2:
                        ch = n if n < 7 else n + 1
                        out.append((i, ch, 10 if ch == 9 else ch + 1))
                    else:
                        ch = 7 - n if n < 7 else 16 - n
                        out.append((i, ch, 10 if ch == 8 else ch - 1))
            return out

        UPD = updates()
        NUPD = len(UPD)
        EARLY_TAPS = 18
        VBANK = (4, 5, 6)
        SEGS = ((0, N_SAMPLE, 0), (N_SAMPLE, N_PROMPT, N_SAMPLE + 2 * PAD))
        N_OUT = 10
        GROUPS = range(2)

        block = ctx.enter_context(nc.Block())

        @block.sync
        def _(sp):
            def load_slab(l, c0, slot):
                aw = ada_w[l].rearrange("(p k) n -> p k n", p=P)
                sp.dma_start(ada_slab[slot][:, 0:KT, :], aw[:, :, bass.ds(c0, P)]).then_inc(slab_in[slot], 16)
                sp.dma_start(ada_slab[slot][0:1, KT, :], ada_b[l:l + 1, bass.ds(c0, P)]).then_inc(slab_in[slot], 16)

            def store_rows(l, done, c0):
                sp.wait_ge(S["m_row_done"], done)
                sp.dma_start(scratch[l, :, bass.ds(c0, P)], m_chunk).then_inc(S["mod_out"], 16)

            def load_block(l, b):
                _, w, c0 = BLOCKS[b]
                wi = w_in[l].rearrange("(k p) n -> p k n", p=P)
                sp.dma_start(win[b % WRING][:, :, 0:w], wi[:, :, c0:c0 + w]).then_inc(win_in[b % WRING], 16)

            def load_vectors(l):
                for ct in range(2):
                    sp.dma_start(vec_rows[TAPS * ct:TAPS * ct + TAPS, :],
                                 conv_w[l, :, P * ct:P * ct + P]).then_inc(S["vec_in"], 16)
                for r, v in ((R_CB, conv_b[l]), (R_CNG, conv_norm_g[l]), (R_CNB, conv_norm_b[l]),
                             (R_GLG, gla_norm_g[l].rearrange("h e -> (h e)")), (R_ABF, gla_a_b_f[l]),
                             (R_ABB, gla_a_b_b[l])):
                    sp.dma_start(vec_rows[r:r + 2, :], v.rearrange("(a b) -> a b", a=2)).then_inc(S["vec_in"], 16)
                for r, v in ((R_QG, q_norm_g), (R_KG, k_norm_g)):
                    for half in range(2):
                        sp.dma_start(vec_rows[r:r + 1, 64 * half:64 * half + 64],
                                     v[l:l + 1, :]).then_inc(S["vec_in"], 16)
                sp.dma_start(CK, cache_k[0, l].rearrange("s h d -> s (h d)")).then_inc(S["ck_in"], 16)

            def load_rows(l, dst, first, rows, name):
                for g in GROUPS:
                    src = scratch[l, g, D * first:D * (first + rows)].rearrange("(r d) -> r d", r=rows)
                    sp.dma_start(dst[:, :, g, :], src.unsqueeze(0).to_broadcast([P, rows, D])).then_inc(S[name], 16)

            def start():
                for g, v in enumerate((c[0], c_ctx)):
                    sp.dma_start(cond[:, g, :], v.rearrange("(p k) -> p k", p=P)).then_inc(S["cond_in"], 16)
                aw = ada_w[0].rearrange("(p k) n -> p k n", p=P)
                for n in range(WIDE):
                    sp.dma_start(wide_slab[n], aw[:, :, 512 * n:512 * n + 512]).then_inc(wide_in[n], 16)
                sp.dma_start(ada_bias, ada_b[0:1, 0:2 * D].to_broadcast([2, 2 * D])).then_inc(S["adab_in"], 16)
                sp.dma_start(X[:, 0:NT_S, :], x_sample[0].rearrange("(t p) d -> p t d", p=P)).then_inc(S["x_in"], 16)
                sp.dma_start(X[:, NT_S, :], x_prompt[0]).then_inc(S["x_in"], 16)
                sp.dma_start(CST[:, :], consts).then_inc(S["const_in"], 16)
                sp.wait_ge(S["m_row_done"], WIDE)
                sp.dma_start(scratch[0, :, 0:2 * D], m_row).then_inc(S["mod_out"], 16)
                load_vectors(0)
                sp.dma_start(gain1, norm1_g[0:1, :].to_broadcast([P, D])).then_inc(S["gain1_in"], 16)
                sp.wait_ge(S["mod_out"], 16)
                load_rows(0, MOD1[:, 0:2], 0, 2, "mod_in")
                for b in range(WRING):
                    load_block(0, b)

            def project(l):
                if l == 0:
                    for n in range(2):
                        load_slab(0, 512 * WIDE + P * n, n)
                else:
                    sp.wait_ge(S["phase"], 4 * PH * l)
                wi = w_in[l].rearrange("(k p) n -> p k n", p=P)
                sp.dma_start(w_v[:, :, 0:256], wi[:, :, GV0:GV0 + 256]).then_inc(S["wv_in"], 16)
                sp.dma_start(w_v[:, :, 256:384], wi[:, :, AV0:AV0 + P]).then_inc(S["wv_in"], 16)
                for b in range(NB):
                    if b + WRING < NB:
                        sp.wait_ge(S["proj_ps"], NB * l + b + 1)
                        load_block(l, b + WRING)
                    if b == 0:
                        sp.wait_ge(S["ht_ps"], NT * l + NT)
                        sp.dma_start(CVAL, cache_v[0, l].rearrange("s h d -> s (h d)")).then_inc(S["misc_in"], 16)
                        sp.wait_ge(S["zeros_ready"], 1)
                        for dr, w in enumerate((gla_a_w_f, gla_a_w_b)):
                            sp.dma_start(gla_w[16 * dr:16 * dr + 16, dr, :], w[l]).then_inc(S["misc_in"], 16)
                sp.wait_ge(S["kout_ready"], l + 1)
                sp.dma_start(new_k[0, l].rearrange("s h d -> s (h d)"), KOUT).then_inc(S["out_done"], 16)
                sp.wait_ge(S["vt_ready"], NT * (l + 1))
                sp.dma_start(new_v[0, l].rearrange("s h d -> s (h d)"), VT[:, NT_S, 256:384])\
                    .then_inc(S["out_done"], 16)
                if l == 0:
                    for n in range(LATE):
                        store_rows(0, WIDE + n + 1, 512 * WIDE + P * n)
                        if n + 2 < LATE:
                            load_slab(0, 512 * WIDE + P * (n + 2), n % 2)
                    sp.wait_ge(S["mod_out"], 16 * (1 + LATE))
                load_rows(l, MOD1[:, 2:3], 2, 1, "gate_in")
                load_rows(l, MOD2[:, :, :, :], 3, 3, "mod2_in")

            def gla(l):
                sp.wait_ge(S["st_zero"], l + 1)
                for i in range(4):
                    for hb in range(2):
                        q = slice(64 * hb, 64 * hb + 64)
                        sp.dma_start(ST[q, i, 0 if i < 2 else 7, q],
                                     state_gla[0, l, i // 2, 2 * (i % 2) + hb]).then_inc(S["st_in"], 16)
                sp.wait_ge(S["st_ready"], NUPD * (l + 1))
                for i in range(4):
                    for hb in range(2):
                        q = slice(64 * hb, 64 * hb + 64)
                        sp.dma_start(new_state[0, l, i // 2, 2 * (i % 2) + hb],
                                     ST[q, i, 10, q]).then_inc(S["out_done"], 16)

            def out_project(l):
                sp.wait_ge(S["og_ps"], 2 * NT * (l + 1))
                wo = w_out[l].rearrange("(k p) n -> p k n", p=P)
                sp.dma_start(WOUT[0], wo[:, 0:4, :]).then_inc(wout_in[0], 16)
                sp.dma_start(gain2, norm2_g[l:l + 1, :].to_broadcast([P, D])).then_inc(S["gain2_in"], 16)
                for s in range(2):
                    sp.dma_start(KRAW[:, :, 64 * s:64 * s + 64],
                                 peer_keys[l, :, s].rearrange("h k d -> k h d")).then_inc(S["keys_in"], 16)
                sp.wait_ge(S["out_done"], 16 * N_OUT * (l + 1))
                sp.wait_ge(S["phase"], 4 * (PH * l + 2))
                sp.dma_start(WOUT[1], wo[:, 4:8, :]).then_inc(wout_in[1], 16)
                sp.dma_start(WQ, peer_wq[l].rearrange("(k p) n -> p k n", p=P)).then_inc(S["wq_in"], 16)

            def peer(l):
                if l + 1 == DEPTH:
                    return
                sp.wait_ge(S["res_done"], NT * (l + 1))
                for n in range(2):
                    load_slab(l + 1, P * n, n)
                with sp.Fori(0, M_BLOCKS // 2 - 1) as i:
                    for j in range(2):
                        store_rows(l + 1, M_EXPERTS + 2 * i + j + 1, i * (2 * P) + P * j)
                        load_slab(l + 1, i * (2 * P) + P * (j + 2), j)
                for n in (M_BLOCKS - 2, M_BLOCKS - 1):
                    store_rows(l + 1, M_EXPERTS + n + 1, P * n)
                sp.wait_ge(S["keys_ready"], l + 1)
                sp.dma_start(gain1, norm1_g[l + 1:l + 2, :].to_broadcast([P, D])).then_inc(S["gain1_in"], 16)
                sp.wait_ge(S["q_ps"], HEADS * NT * (l + 1))
                for b in range(WRING):
                    load_block(l + 1, b)
                load_vectors(l + 1)
                sp.wait_ge(S["mod_out"], 16 * (1 + LATE + M_BLOCKS))
                sp.wait_ge(S["u_free"], RING + TOPK * HEADS * NT * (l + 1))
                load_rows(l + 1, MOD1[:, 0:2], 0, 2, "mod_in")

            start()
            for l in range(DEPTH):
                for stage in (project, gla, out_project, peer):
                    stage(l)
            for t in range(NT):
                sp.wait_ge(S["y_ready"], NT * (DEPTH - 1) + t + 1)
                dst = y_sample[0, P * t:P * t + P, :] if t < NT_S else y_prompt[0]
                sp.dma_start(dst, X[:, t, :]).then_inc(S["out_done"], 16)
            sp.wait_ge(S["out_done"], 16 * (N_OUT * DEPTH + NT))

        @block.gpsimd
        def _(pool):
            u_rows = peer_u.rearrange("l e d -> (l e) d")
            v_rows = peer_v.rearrange("l e d -> (l e) d")
            pool.memset(gla_w[:, :, :], 0.0)
            pool.memset(zero_l[:, :], 0.0)
            pool.memset(zero_r[:, :], 0.0).then_inc(S["zeros_ready"], 1)
            for l in range(DEPTH):
                if l == 0:
                    pool.wait_ge(S["m_row_done"], WIDE)
                pool.memset(UP[:, :, :], 0.0)
                pool.wait_ge(S["vec_ready"], l + 1)
                pool.wait_ge(S["ht_ps"], NT * l + NT)
                pool.drain().then_inc(S["pad_ready"], 1)
                pool.wait_ge(S["proj_ev"], NB * l + 2)
                for o, n, q in SEGS:
                    pool.tensor_tensor(UP[:, 0, q + PAD:q + PAD + n], CV[:, 0, o:o + n], CG[:, 0, o:o + n], ALU.mult)
                for j in range(TAPS):
                    pool.drain()
                    w = vec[:, j:j + 1]
                    for o, n, q in SEGS:
                        src = UP[:, 0, q + j:q + j + n]
                        if j == 0:
                            pool.tensor_scalar(CX[:, 0, o:o + n], src, w, vec[:, R_CB:R_CB + 1], ALU.mult, ALU.add)
                        else:
                            pool.tensor_scalar(CV[:, 0, o:o + n], src, w, None, ALU.mult)
                    if j:
                        pool.drain()
                        pool.tensor_tensor(CX[:, 0, :], CX[:, 0, :], CV[:, 0, :], ALU.add)
                pool.drain().then_inc(S["conv_done"], 1)
                phase_end(pool, PH * l + 1)
                pool.wait_ge(S["out_done"], 16 * (N_OUT * l + 2))
                pool.memset(ST[:, :, :, :], 0.0).then_inc(S["st_zero"], 1)
                phase_end(pool, PH * l + 2)
                pool.memset(KEYS[:, :, :], 0.0).then_inc(S["keys_zero"], 1)
                pool.wait_ge(S["mix_ps"], NT * (l + 1))
                pool.wait_ge(S["res_done"], NT * (l + 1))
                pool.wait_ge(S["ss2_done"], 2 * (l + 1))
                with pool.Fori(0, NT * HEADS) as i:
                    head = NT * HEADS * l + i
                    pool.wait_ge(S["idx_ready"], head + 1)
                    pool.sem_inc(S["pool_turn"], 1)
                    for k in range(TOPK):
                        pool.wait_ge(S["u_free"], head * TOPK + k + 1)
                        pool.sem_inc(S["pool_turn"], 1)
                        pool.indirect_dma_start(UR[:, k % RING, :], None, u_rows,
                                                bass.IndirectOffsetOnAxis(ap=idx_u[:, k:k + 1], axis=0))\
                            .then_inc(u_in[k % RING], 16)
                    pool.wait_ge(S["idxv_ready"], head + 1)
                    pool.sem_inc(S["pool_turn"], 1)
                    for k in range(TOPK):
                        pool.wait_ge(S["v_free"], head * TOPK + k + 1)
                        pool.sem_inc(S["pool_turn"], 1)
                        pool.indirect_dma_start(VR[:, k % RING, :], None, v_rows,
                                                bass.IndirectOffsetOnAxis(ap=idx_v[:, k:k + 1], axis=0))\
                            .then_inc(v_in[k % RING], 16)
                phase_end(pool, PH * l + 3)

        @block.tensor
        def _(pe):
            def mm(out, lhsT, rhs, start=True, stop=True):
                return pe.matmul(out, lhsT, rhs, start=start, stop=stop)

            def wide(out, lhsT, rhs, start=True, stop=True):
                mm(out[:, 0:512], lhsT, rhs[:, 0:512], start, stop)
                return mm(out[:, 512:NTOK], lhsT, rhs[:, 512:NTOK], start, stop)

            def start():
                pe.wait_ge(S["cond_ready"], 2)
                for n in range(WIDE):
                    pe.wait_ge(wide_in[n], 16)
                    if n >= 2:
                        pe.wait_ge(S["m_row_done"], n - 1)
                    for k in range(KT):
                        m = mm(PS[0:2, n % 2, :], cond_s[:, k, :], wide_slab[n][:, k, :], k == 0, k == KT - 1)
                    m.then_inc(S["m_ps"], 1)
                pe.wait_ge(S["m_row_done"], WIDE)
                pe.wait_ge(S["const_in"], 16)

            def mod_block(bank, slot, loads, done):
                pe.wait_ge(slab_in[slot], loads)
                pe.wait_ge(S["m_row_done"], done)
                for k in range(KT):
                    mm(PS[0:2, bank, 0:P], cond_s[:, k, :], ada_slab[slot][:, k, :], k == 0, False)
                mm(PS[0:2, bank, 0:P], CST[0:1, C_ONE:C_ONE + 2], ada_slab[slot][0:1, KT, :], False, True)\
                    .then_inc(S["m_ps"], 1)

            def project(l):
                pe.wait_ge(S["vec_in"], 16 * 12 * (l + 1))
                pe.transpose(PS[:, 4, 0:R_END], vec_rows, CST[0:R_END, C_ID:C_ID + R_END]).then_inc(S["vec_ps"], 1)
                pe.wait_ge(S["ck_in"], 16 * (l + 1))
                pe.transpose(PS[:, 5, 0:P], CK, ident).then_inc(S["kc_ps"], 1)
                for t in range(NT):
                    pe.wait_ge(S["h_ready"], NT * l + t + 1)
                    if t >= 2:
                        pe.wait_ge(S["ht_ready"], NT * l + t - 1)
                    for k in range(KT):
                        m = pe.transpose(pair(t % 2)[:, P * k:P * k + P], hbuf[:, t % 2, P * k:P * k + P], ident)
                    m.then_inc(S["ht_ps"], 1)
                pe.wait_ge(S["ht_ready"], NT * l + NT)
                pe.wait_ge(S["vec_ready"], l + 1)
                pe.wait_ge(S["kc_ready"], l + 1)

                def variance(u):
                    pe.wait_ge(S["sq_ready"], NU * l + u + 1)
                    if u:
                        pe.wait_ge(S["sd_ready"], NU * l + u)
                    wide(pair(0), mean_mat, SQ).then_inc(S["var_ps"], 1)

                def rotated(u):
                    pe.wait_ge(S["n_ready"], NU * l + u + 1)
                    if u:
                        pe.wait_ge(S["rope_done"], NU * l + u)
                    mm(PS[:, 2, :], rot_mat, UNITS[u][0][:, 0:N_SAMPLE]).then_inc(S["rot_ps"], 1)

                for b, (_, w, _c) in enumerate(BLOCKS):
                    pe.wait_ge(win_in[b % WRING], 16 * (len(range(b % WRING, NB, WRING)) * l + b // WRING + 1))
                    if b >= 2:
                        pe.wait_ge(S["proj_ev"], NB * l + b - 1)
                    for k in range(KT):
                        m = wide(pair(2 + b % 2)[0:w], win[b % WRING][:, k, 0:w], HT[:, k, :], k == 0, k == KT - 1)
                    m.then_inc(S["proj_ps"], 1)
                    if 0 <= b - 5 < NU:
                        variance(b - 5)
                    if 0 <= b - 7 < NU:
                        rotated(b - 7)
                    if 11 <= b < 15:
                        i = b - 11
                        if i == 0:
                            pe.wait_ge(S["misc_in"], 48 * (l + 1))
                            pe.wait_ge(S["sd_ready"], NU * (l + 1))
                            pe.wait_ge(S["proj_ev"], NB * l + 10)
                        else:
                            pe.wait_ge(S["z_ready"], 4 * l + i)
                        wide(pair(0), gla_w[:, i // 2, P * (i % 2):P * (i % 2) + P], GA).then_inc(S["z_ps"], 1)
                    if b == 13:
                        pe.wait_ge(S["rope_done"], NU * (l + 1))
                        pe.transpose(PS[:, 2, 0:P], AK[:, N_SAMPLE:NTOK], ident).then_inc(S["kout_ps"], 1)

            def attention(l):
                def scores(i):
                    t, h = STEPS[i]
                    if i >= 2:
                        pe.wait_ge(S["p_ready"], NS * l + i - 1)
                    q = slice(64 * (h % 2), 64 * (h % 2) + 64)
                    k0, nk = keys_of(t)
                    for a in range(0, nk, 512):
                        b = min(nk, a + 512)
                        m = mm(pair(i % 2)[:, a:b], AQ[q, h // 2, P * t:P * t + P], KTD[q, h // 4, k0 + a:k0 + b])
                    m.then_inc(S["s_ps"], 1)

                def evacuated(i):
                    pe.wait_ge(S["pt_dve" if i % 2 else "pt_act"], NS // 2 * l + i // 2 + 1)

                def transposes(i):
                    pe.wait_ge(S["p_ready"], NS * l + i + 1)
                    if i >= 1:
                        evacuated(i - 1)
                    for s in range(keys_of(STEPS[i][0])[1] // P):
                        m = pe.transpose(pair(2)[:, P * s:P * s + P], PR[:, i % 2, P * s:P * s + P], ident)
                    m.then_inc(S["pt_ps"], 1)

                def values(i):
                    t, h = STEPS[i]
                    evacuated(i)
                    if h == 0 and t:
                        pe.wait_ge(S["o_ready"], NT * l + t)
                    v = vals_of(t)
                    for s, vt in enumerate(v):
                        m = mm(PS[:, 6, 64 * h:64 * h + 64], PRT[:, i % 2, P * s:P * s + P],
                               vt[:, 64 * (h // 4):64 * (h // 4) + 64], s == 0, s == len(v) - 1)
                    m.then_inc(S["o_ps"], 1)

                def out_transposes(t):
                    pe.wait_ge(S["o_ready"], NT * l + t + 1)
                    if l == 0:
                        pe.wait_ge(S["m_row_done"], WIDE + min(LATE, 8 * t + 11))
                    if t:
                        pe.wait_ge(S["ot_ready"], NT * l + t)
                    for j in range(4):
                        m = pe.transpose(PS[:, 7, P * j:P * j + P], OTOK[:, P * j:P * j + P], ident)
                    m.then_inc(S["ot_ps"], 1)

                pe.wait_ge(S["rope_done"], NU * (l + 1))
                pe.wait_ge(S["z_ready"], 4 * (l + 1))
                pe.wait_ge(S["kout_ready"], l + 1)
                for kv in range(2):
                    dup = CST[:, C_DUP + P * kv:C_DUP + P * kv + P]
                    o = pair(kv)
                    mm(o[:, 0:512], dup, AK[:, 0:512])
                    mm(o[:, 512:640], dup, KC)
                    mm(o[:, 640:768], dup, AK[:, N_SAMPLE:NTOK]).then_inc(S["dup_ps"], 1)

                def values_projection(t):
                    if t >= 3:
                        pe.wait_ge(S["vt_ready"], NT * l + t - 2)
                    for k in range(KT):
                        m = mm(PS[:, VBANK[t % 3], 0:384], HT[:, k, P * t:P * t + P], w_v[:, k, :], k == 0, k == KT - 1)
                    m.then_inc(S["vt_ps"], 1)

                pe.wait_ge(S["wv_in"], 32 * (l + 1))
                pe.wait_ge(S["proj_ev"], NB * (l + 1))
                for t in range(NT - 2):
                    values_projection(t)
                pe.wait_ge(S["dup_ready"], 2 * (l + 1))
                pe.wait_ge(S["misc_in"], 48 * (l + 1))
                for i in range(NS + 4):
                    if i < NS:
                        scores(i)
                    if i < 2:
                        values_projection(NT - 2 + i)
                    if i == 2:
                        pe.wait_ge(S["vt_ready"], NT * (l + 1))
                    if 2 <= i < NS + 2:
                        transposes(i - 2)
                    if l == 0 and 0 <= i - 1 < LATE:
                        if i >= 12 and i % 8 == 4:
                            pe.wait_ge(S["ot_ready"], (i - 12) // 8 + 1)
                        mod_block(7, (i - 1) % 2, 32 * ((i + 1) // 2), WIDE + i - 1)
                    if 3 <= i < NS + 3:
                        values(i - 3)
                    if i >= 11 and i % 8 == 3:
                        out_transposes((i - 11) // 8)

            def gla_out(l, s):
                hp, t = s // NT, s % NT
                pe.wait_ge(S["atm_ready"], 2 * NT * l + s + 1)
                o = pair(hp)
                for n, (dr, ch) in enumerate(((0, 2 * t), (0, 2 * t + 1), (1, 2 * t), (1, 2 * t + 1))):
                    i = 2 * dr + hp
                    cols = slice(64 * ch, 64 * ch + 64)
                    mm(o[:, cols], ST[:, i, ch, :], QD[:, i, cols], n == 0, False)
                for hb in range(2):
                    head = 2 * hp + hb
                    for dr in range(2):
                        m = mm(o[64 * hb:64 * hb + 64, P * t:P * t + P], VT[:, t, 64 * head:64 * head + 64],
                               ATM[:, s % 2, hb, dr, :], False, dr == 1)
                m.then_inc(S["og_ps"], 1)

            def gla(l):
                for ct in range(2):
                    wide(pair(ct), mean_mat, CX[:, ct, :]).then_inc(S["cx_mean"], 1)
                for ct in range(2):
                    pe.wait_ge(S["cx_sq"], 2 * l + ct + 1)
                    wide(zp(ct), mean_mat, CSQ[:, ct, :]).then_inc(S["cx_var"], 1)
                for i in range(4):
                    if i < 2:
                        pe.wait_ge(S["cx_sd"], 2 * l + i + 1)
                    pe.wait_ge(S["qk_ready"], 4 * l + i + 1)
                    for t in range(NT):
                        m = pe.transpose(zp(i)[:, P * t:P * t + P], KK[:, i, P * t:P * t + P], ident)
                    m.then_inc(S["kk_ps"], 1)
                pe.wait_ge(S["kk_ready"], 4 * l + 4)
                for u, (i, ch, _n) in enumerate(UPD):
                    if u >= 8:
                        pe.wait_ge(S["st_ready"], NUPD * l + u - 7)
                    q = slice(64 * (ch % 2), 64 * (ch % 2) + 64)
                    mm(PS[:, u % 8, 0:P], KKT[q, i, ch // 2, :],
                       VT[q, ch // 2, P * (i % 2):P * (i % 2) + P]).then_inc(S["dS_ps"], 1)
                pe.wait_ge(S["st_ready"], NUPD * (l + 1))
                for s in range(2 * NT):
                    hp, t = s // NT, s % NT
                    if s >= 2:
                        pe.wait_ge(S["atm_ready"], 2 * NT * l + s - 1)
                    cols = slice(P * t, P * t + P)
                    for hb in range(2):
                        q = slice(64 * hb, 64 * hb + 64)
                        for dr in range(2):
                            i = 2 * dr + hp
                            m = mm(PS[:, 4 + 2 * (s % 2) + hb, P * dr:P * dr + P], KD[q, i, cols], QD[q, i, cols])
                    m.then_inc(S["a_ps"], 1)
                    if s >= 1:
                        gla_out(l, s - 1)
                gla_out(l, 2 * NT - 1)
                for hp in range(2):
                    pe.wait_ge(S["og_sq"], 2 * l + hp + 1)
                    wide(pair(hp), mean_mat, OSQ[:, hp, :]).then_inc(S["og_var"], 1)

            def tile_transposes(l, t):
                n = NT * l + t
                pe.wait_ge(S["h2_ready"], n + 1)
                if t:
                    pe.wait_ge(S["sc_now"], HEADS * n)
                    if l == 0:
                        pe.wait_ge(S["m_row_done"], M_EXPERTS + 12 * t)
                for k in range(KT):
                    m = pe.transpose(pair(2)[:, P * k:P * k + P], H2[:, t % 2, P * k:P * k + P], ident)
                m.then_inc(S["h2t_ps"], 1)
                pe.wait_ge(S["h2t_ready"], n + 1)

            def query(g, h):
                if not isinstance(g, int) or g:
                    pe.wait_ge(S["q_ready"], g)
                for k in range(KT):
                    m = mm(PS[:, 6, 0:P], H2T[:, k, :], WQ[:, k, bass.ds(h * P, P)], k == 0, k == KT - 1)
                m.then_inc(S["q_ps"], 1)

            def query_transpose(g):
                pe.wait_ge(S["q_ready"], g + 1)
                pe.transpose(PS[:, 7, 0:P], QTOK, ident).then_inc(S["qt_ps"], 1)

            def key_scores(g, h):
                pe.wait_ge(S["qt_ready"], g + 1)
                mm(PS[:, 4, 0:256], QT, KEYS[:, :, :].rearrange("p h k -> p (h k)")[:, bass.ds(h * 256, 256)])\
                    .then_inc(S["sc_ps"], 1)

            def out_project(l):
                def mix(t, half):
                    if t >= 2 and half == 0:
                        pe.wait_ge(S["res_read"], NT * l + t - 1)
                    if t == 0:
                        pe.wait_ge(wout_in[half], 16 * (l + 1))
                    for k in range(4):
                        for hf in range(2):
                            m = mm(pair(t % 2)[:, 512 * hf:512 * hf + 512], MIX[:, 4 * half + k, P * t:P * t + P],
                                   WOUT[half][:, k, 512 * hf:512 * hf + 512], half + k == 0, half == 1 and k == 3)
                    if half:
                        m.then_inc(S["mix_ps"], 1)

                g = HEADS * NT * l
                for t in (0, 1):
                    mix(t, 0)
                    mix(t, 1)
                pe.wait_ge(S["keys_in"], 32 * (l + 1))
                for h in range(HEADS):
                    m = pe.transpose(pair(2)[:, P * h:P * h + P], KRAW[:, h, :], ident)
                m.then_inc(S["keys_ps"], 1)
                pe.wait_ge(S["keys_ready"], l + 1)
                tile_transposes(l, 0)
                pe.wait_ge(S["wq_in"], 16 * (l + 1))
                query(g, 0)
                mix(2, 0)
                query_transpose(g)
                mix(2, 1)
                key_scores(g, 0)
                mix(3, 0)
                query(g + 1, 1)
                mix(3, 1)
                query_transpose(g + 1)
                mix(4, 0)
                pe.wait_ge(S["sc_now"], g + 1)
                key_scores(g + 1, 1)
                mix(4, 1)

            def head_sum(head, ahead, block=None):
                for k in range(TOPK):
                    if block is not None and k in (4, 14):
                        j = k // 10
                        mod_block(5, j, 32 * LATE // 2 + 16 * block + 32, M_EXPERTS + block + j)
                    if ahead is not None:
                        if k == 0:
                            query(head + 2, ahead)
                        if k == 5:
                            query_transpose(head + 2)
                        if k == 10:
                            key_scores(head + 2, ahead)
                    pe.wait_ge(v_in[k % RING], head * 32 + 16 * (k // RING + 1))
                    pe.wait_ge(S["diag_ready"], head * TOPK + k + 1)
                    for cc in range(2):
                        m = mm(PS[:, cc, :], DG[:, k % DIAGS, :], VR[:, k % RING, 512 * cc:512 * cc + 512],
                               False, False)
                    m.then_inc(S["v_free"], 1)

            def peer(l):
                pe.wait_ge(S["res_read"], NT * (l + 1))
                if l == 0:
                    pe.wait_ge(S["zeros_ready"], 1)
                    pe.sem_inc(S["v_free"], RING)
                for t in range(NT):
                    n = NT * l + t
                    if n:
                        pe.wait_ge(S["acc_out"], n)
                    for cc in range(2):
                        mm(PS[:, cc, :], zero_l[:, :], zero_r[:, :], True, False)
                    with pe.Fori(0, HEADS - 2) as i:
                        head_sum(HEADS * n + i, i + 2, 12 * t + i * 2 if l == 0 and t < 4 else None)
                    if t + 1 < NT:
                        tile_transposes(l, t + 1)
                        with pe.Fori(0, 2) as i:
                            head_sum(HEADS * n + HEADS - 2 + i, i)
                    else:
                        with pe.Fori(0, 2) as i:
                            head_sum(HEADS * n + HEADS - 2 + i, None)
                    for cc in range(2):
                        m = mm(PS[:, cc, :], zero_l[:, :], zero_r[:, :], False, True)
                    m.then_inc(S["acc_done"], 1)

            start()
            for l in range(DEPTH):
                project(l)
                attention(l)
                phase_end(pe, PH * l + 1)
                gla(l)
                phase_end(pe, PH * l + 2)
                out_project(l)
                peer(l)
                phase_end(pe, PH * l + 3)

        @block.scalar
        def _(act):
            st = Steps(act, "act")

            def start():
                act.wait_ge(S["cond_in"], 32)
                for group in GROUPS:
                    act.activation(cond_s[:, :, group], cond[:, group, :], ACT.Silu).then_inc(S["cond_ready"], 1)
                act.wait_ge(S["x_in"], 32)

            def mod_rows(bank, done, stored):
                act.wait_ge(S["m_ps"], done + 1)
                act.wait_ge(S["mod_out"], stored)
                act.activation(m_chunk, PS[0:2, bank, 0:P], ACT.Copy).then_inc(S["m_row_done"], 1)

            def project(l):
                for t in range(NT):
                    st.link(act.activation(hbuf[:, t % 2, :], X[:, t, :], ACT.Square, accum_out=sumsq[:, 0, t:t + 1]))
                act.sem_inc(S["ss_done"], 1)
                act.wait_ge(S["ms_done"], l + 1)
                act.activation(rms[:, 0:NT], rstd[:, 0:NT], ACT.Sqrt).then_inc(S["sd_done"], 1)
                act.wait_ge(S["vec_ps"], l + 1)
                act.activation(vec[:, :], PS[:, 4, 0:R_END], ACT.Copy).then_inc(S["vec_ready"], 1)
                act.wait_ge(S["kc_ps"], l + 1)
                act.activation(KC, PS[:, 5, 0:P], ACT.Copy).then_inc(S["kc_ready"], 1)
                for t in range(NT):
                    act.wait_ge(S["ht_ps"], NT * l + t + 1)
                    act.activation(HT[:, :, P * t:P * t + P], pair(t % 2).rearrange("p (k n) -> p k n", k=KT),
                                   ACT.Copy).then_inc(S["ht_ready"], 1)

                def square(u):
                    if u:
                        act.wait_ge(S["var_ps"], NU * l + u)
                    act.wait_ge(S["proj_ev"], NB * l + 4 + u + 1)
                    act.activation(SQ, UNITS[u][0], ACT.Square).then_inc(S["sq_ready"], 1)

                def deviation(u):
                    act.wait_ge(S["var_ps"], NU * l + u + 1)
                    if u:
                        act.wait_ge(S["n_ready"], NU * l + u)
                    act.activation(SD, pair(0)[:, 0:NTOK], ACT.Sqrt, bias=eps_c[:, 0:1]).then_inc(S["sd_ready"], 1)

                for b, (dst, w, _c) in enumerate(BLOCKS):
                    act.wait_ge(S["proj_ps"], NB * l + b + 1)
                    f = ACT.Sigmoid if b in (0, 2) else ACT.Silu if b >= NB - 2 else ACT.Copy
                    act.activation(dst, pair(2 + b % 2)[0:w, 0:NTOK], f).then_inc(S["proj_ev"], 1)
                    if 0 <= b - 6 < NU:
                        deviation(b - 6)
                    if 0 <= b - 4 < NU:
                        square(b - 4)
                    if b >= 12:
                        i = b - 12
                        col = (R_ABF if i < 2 else R_ABB) + i % 2
                        act.wait_ge(S["z_ps"], 4 * l + i + 1)
                        act.activation(LA[:, i, :], pair(0)[:, 0:NTOK], ACT.Identity, bias=vec[:, col:col + 1])\
                            .then_inc(S["z_ready"], 1)
                    if b == 14:
                        act.wait_ge(S["kout_ps"], l + 1)
                        act.activation(KOUT, PS[:, 2, 0:P], ACT.Copy).then_inc(S["kout_ready"], 1)

            def attention(l):
                def softmax(i):
                    t, h = STEPS[i]
                    act.wait_ge(S["nmax_ready"], NS * l + i + 1)
                    if i >= 2:
                        act.wait_ge(S["pt_ps"], NS * l + i - 1)
                    if h == 0 and t >= 2:
                        act.wait_ge(S["o_ready"], NT * l + t - 1)
                    nk = keys_of(t)[1]
                    act.activation(PR[:, i % 2, 0:nk], pair(i % 2)[:, 0:nk], ACT.Exp, bias=nmax[:, i % 4:i % 4 + 1],
                                   scale=0.125, accum_out=psum_p[:, t % 2, h:h + 1]).then_inc(S["p_ready"], 1)

                def evacuate(i):
                    act.wait_ge(S["pt_ps"], NS * l + i + 1)
                    if i >= 2:
                        act.wait_ge(S["o_ps"], NS * l + i - 1)
                    nk = keys_of(STEPS[i][0])[1]
                    act.activation(PRT[:, i % 2, 0:nk], pair(2)[:, 0:nk], ACT.Copy).then_inc(S["pt_act"], 1)

                def out_evacuate(t):
                    act.wait_ge(S["ot_ps"], NT * l + t + 1)
                    act.activation(MIX[:, 4:8, P * t:P * t + P], PS[:, 7, :].rearrange("p (j n) -> p j n", j=4),
                                   ACT.Copy).then_inc(S["ot_ready"], 1)

                for kv in range(2):
                    act.wait_ge(S["dup_ps"], 2 * l + kv + 1)
                    act.activation(KTD[:, kv, :], pair(kv)[:, 0:768], ACT.Copy).then_inc(S["dup_ready"], 1)

                def values_out(t):
                    act.wait_ge(S["vt_ps"], NT * l + t + 1)
                    act.activation(VT[:, t, :], PS[:, VBANK[t % 3], 0:384], ACT.Copy).then_inc(S["vt_ready"], 1)

                for t in range(NT - 2):
                    values_out(t)
                act.wait_ge(S["z_ready"], 4 * (l + 1))
                for i in range(NS + 5):
                    if i == 8:
                        act.wait_ge(S["conv_done"], 2 * (l + 1))
                    if 8 <= i < 12:
                        st.link(act.activation(LZ[:, i - 8, :], LA[:, i - 8, :], ACT.Abs))
                    if 12 <= i < 16:
                        st.link(act.activation(LZ[:, i - 12, :], LZ[:, i - 12, :], ACT.Exp, scale=-1.0))
                    if i == NS + 2:
                        act.activation(LZ[:, :, :], LZ[:, :, :], ACT.Ln, bias=1.0).then_inc(S["ln_done"], 1)
                    if i < NS:
                        softmax(i)
                    if i < 2:
                        values_out(NT - 2 + i)
                    if 2 <= i < NS + 2 and i % 2 == 0:
                        evacuate(i - 2)
                    if i >= 12 and i % 8 == 4:
                        out_evacuate((i - 12) // 8)
                    if l == 0 and 0 <= i - 1 < LATE:
                        mod_rows(7, WIDE + i - 1, 16 * i)

            def gla(l):
                for ct in range(2):
                    act.wait_ge(S["cx_cent"], 2 * l + ct + 1)
                    act.activation(CSQ[:, ct, :], CX[:, ct, :], ACT.Square).then_inc(S["cx_sq"], 1)
                for ct in range(2):
                    act.wait_ge(S["cx_var"], 2 * l + ct + 1)
                    act.activation(CSQ[:, ct, :], zp(ct)[:, 0:NTOK], ACT.Sqrt, bias=eps_c[:, 0:1])\
                        .then_inc(S["cx_sd"], 1)
                for i in range(4):
                    act.wait_ge(S["b_ready"], 4 * l + i + 1)
                    act.activation(QD[:, i, :], LA[:, i, :], ACT.Exp, scale=1 / 16)
                    act.activation(KD[:, i, :], LA[:, i, :], ACT.Exp, scale=-1 / 16)
                    act.activation(KK[:, i, :], KK[:, i, :], ACT.Exp, scale=1 / 16).then_inc(S["ex_done"], 1)
                act.activation(e_last[:, :, :], e_last[:, :, :], ACT.Exp, scale=1 / 16).then_inc(S["el_ready"], 1)
                act.wait_ge(S["mod_out"], 16 * (1 + LATE))
                for i in range(4):
                    act.wait_ge(S["kk_ps"], 4 * l + i + 1)
                    act.activation(KKT[:, i, :, :], zp(i)[:, 0:NTOK].rearrange("p (t f) -> p t f", t=NT), ACT.Copy)\
                        .then_inc(S["kk_ready"], 1)
                for ct in range(2):
                    act.wait_ge(S["cx_ready"], 2 * l + ct + 1)
                    act.activation(MIX[:, 2 + ct, :], CX[:, ct, :], ACT.Silu, bias=vec[:, R_CNB + ct:R_CNB + ct + 1])
                for hp in range(2):
                    act.wait_ge(S["og_ps"], 2 * NT * l + NT * (hp + 1))
                    act.activation(OG[:, hp, :], pair(hp)[:, 0:NTOK], ACT.Copy)
                    act.activation(OSQ[:, hp, :], pair(hp)[:, 0:NTOK], ACT.Square).then_inc(S["og_sq"], 1)
                for hp in range(2):
                    act.wait_ge(S["og_var"], 2 * l + hp + 1)
                    act.activation(OSD[:, hp, :], pair(hp)[:, 0:NTOK], ACT.Sqrt, bias=eps_c[:, 0:1])\
                        .then_inc(S["og_sd"], 1)

            def query_out(g):
                act.wait_ge(S["q_ps"], g + 1)
                act.activation(QTOK, PS[:, 6, 0:P], ACT.Copy).then_inc(S["q_ready"], 1)

            def query_transpose_out(g):
                act.wait_ge(S["qt_ps"], g + 1)
                act.activation(QT, PS[:, 7, 0:P], ACT.Copy).then_inc(S["qt_ready"], 1)

            def scores_out(g):
                act.wait_ge(S["sc_ps"], g + 1)
                if not isinstance(g, int) or g:
                    act.wait_ge(S["sc_taken"], g)
                act.activation(SCC[:, :, :].rearrange("p a b -> p (a b)"), PS[:, 4, 0:256], ACT.Copy)\
                    .then_inc(S["sc_now"], 1)

            def head_weights(head, ahead, block=None):
                act.wait_ge(S["idx_ready"], head + 1)
                act.activation(gexp[:, :], centred[:, :], ACT.Exp, accum_out=gsum[:, 0:1])
                act.wait_ge(S["u_free"], head * TOPK + TOPK + RING)
                act.activation(gelu_h[:, :], act_h[:, :], ACT.Gelu).then_inc(S["gelu_done"], 1)
                act.wait_ge(S["w_ready"], head + 1)
                for k in range(TOPK):
                    if ahead:
                        if k == 2:
                            query_out(head + 2)
                        if k == 7:
                            query_transpose_out(head + 2)
                        if k == 12:
                            scores_out(head + 2)
                    if block is not None and k in (6, 15):
                        mod_rows(5, M_EXPERTS + block + k // 10, 16 * (1 + LATE) + block * 16 + 16 * (k // 10))
                    act.wait_ge(S["v_free"], head * TOPK + k + 1 + RING - DIAGS)
                    act.activation(DG[:, k % DIAGS, :], ident, ACT.Copy, scale=w_h[:, k:k + 1])\
                        .then_inc(S["diag_ready"], 1)

            def tile_out(l, t):
                act.wait_ge(S["h2t_ps"], NT * l + t + 1)
                act.activation(H2T[:, :, :], pair(2).rearrange("p (k n) -> p k n", k=KT), ACT.Copy)\
                    .then_inc(S["h2t_ready"], 1)

            def out_project(l):
                def square(t):
                    act.wait_ge(S["res_done"], NT * l + t + 1)
                    st.link(act.activation(xsq, X[:, t, :], ACT.Square, accum_out=sumsq[:, 1, t:t + 1]))

                def deviation(first, last, part):
                    act.sem_inc(S["ss2_done"], 1)
                    act.wait_ge(S["ms2_done"], 2 * l + part + 1)
                    act.activation(rms[:, first:last], rstd[:, first:last], ACT.Sqrt).then_inc(S["sd2_done"], 1)

                act.wait_ge(S["out_done"], 16 * N_OUT * (l + 1))
                g = HEADS * NT * l
                square(0)
                deviation(0, 1, 0)
                act.wait_ge(S["keys_ps"], l + 1)
                act.wait_ge(S["keys_zero"], l + 1)
                kv = pair(2).rearrange("p (h k) -> p h k", h=HEADS)
                act.activation(KEYS[0:64, :, 0:128], kv[0:64], ACT.Copy)
                act.activation(KEYS[64:128, :, 128:256], kv[64:128], ACT.Copy).then_inc(S["keys_ready"], 1)
                tile_out(l, 0)
                query_out(g)
                square(1)
                query_transpose_out(g)
                scores_out(g)
                square(2)
                query_out(g + 1)
                query_transpose_out(g + 1)
                scores_out(g + 1)
                for t in (3, 4):
                    square(t)
                deviation(1, NT, 1)

            def peer(l):
                for t in range(NT):
                    n = NT * l + t
                    with act.Fori(0, HEADS - 2) as i:
                        head_weights(HEADS * n + i, True, 12 * t + i * 2 if l == 0 and t < 4 else None)
                    if t + 1 < NT:
                        tile_out(l, t + 1)
                    with act.Fori(0, 2) as i:
                        head_weights(HEADS * n + HEADS - 2 + i, t + 1 < NT)
                    act.wait_ge(S["acc_done"], n + 1)
                    if n:
                        act.wait_ge(S["y_ready"], n)
                    act.activation(TMP, pair(0), ACT.Copy).then_inc(S["acc_out"], 1)

            start()
            for l in range(DEPTH):
                project(l)
                attention(l)
                phase_end(act, PH * l + 1)
                gla(l)
                phase_end(act, PH * l + 2)
                out_project(l)
                peer(l)
                phase_end(act, PH * l + 3)

        @block.vector
        def _(dve):
            st = Steps(dve, "dve")
            tt, stt, ts = dve.tensor_tensor, dve.scalar_tensor_tensor, dve.tensor_scalar

            def start():
                dve.memset(eps_c[:, :], EPS)
                dve.wait_ge(S["adab_in"], 16)
                for n in range(WIDE):
                    dve.wait_ge(S["m_ps"], n + 1)
                    w = slice(512 * n, 512 * n + 512)
                    tt(m_row[:, w], PS[0:2, n % 2, :], ada_bias[:, w], ALU.add).then_inc(S["m_row_done"], 1)

            def scale_gain(mod, gain):
                for g in GROUPS:
                    st.do(stt(mod[:, 1, g, :], mod[:, 1, g, :], 1.0, gain, ALU.add, ALU.mult))
                st.after(st.n)

            def project(l):
                dve.wait_ge(S["ss_done"], l + 1)
                ts(rstd[:, 0:NT], sumsq[:, 0, 0:NT], 1.0 / D, EPS, ALU.mult, ALU.add).then_inc(S["ms_done"], 1)
                dve.wait_ge(S["sd_done"], l + 1)
                st.link(dve.reciprocal(rstd[:, 0:NT], rms[:, 0:NT]))
                dve.wait_ge(S["gain1_in"], 16 * (l + 1))
                dve.wait_ge(S["mod_in"], 32 * (l + 1))
                scale_gain(MOD1, gain1)
                for t in range(NT):
                    if t >= 2:
                        dve.wait_ge(S["ht_ps"], NT * l + t - 1)
                    g = group_of(t)
                    st.link(stt(hbuf[:, t % 2, :], X[:, t, :], rstd[:, t:t + 1], MOD1[:, 1, g, :], ALU.mult, ALU.mult))
                    tt(hbuf[:, t % 2, :], hbuf[:, t % 2, :], MOD1[:, 0, g, :], ALU.add).then_inc(S["h_ready"], 1)

                def convolve(first, last):
                    for j in range(first, last):
                        w = vec[:, TAPS + j:TAPS + j + 1]
                        for o, n, q in SEGS:
                            st.after(st.n - 1)
                            src, dst = UP[:, 1, q + j:q + j + n], CX[:, 1, o:o + n]
                            if j == 0:
                                st.do(ts(dst, src, w, vec[:, R_CB + 1:R_CB + 2], ALU.mult, ALU.add))
                            else:
                                st.do(stt(dst, src, w, dst, ALU.mult, ALU.add))

                dve.wait_ge(S["pad_ready"], l + 1)
                dve.wait_ge(S["ht_ps"], NT * (l + 1))
                dve.wait_ge(S["proj_ev"], NB * l + 4)
                for o, n, q in SEGS:
                    st.do(tt(UP[:, 1, q + PAD:q + PAD + n], CV[:, 1, o:o + n], CG[:, 1, o:o + n], ALU.mult))
                convolve(0, EARLY_TAPS)
                for u, (src, g) in enumerate(UNITS):
                    dve.wait_ge(S["sd_ready"], NU * l + u + 1)
                    st.link(dve.reciprocal(SD, SD))
                    stt(src, src, vec[:, g:g + 1], SD, ALU.mult, ALU.mult).then_inc(S["n_ready"], 1)
                    dve.wait_ge(S["rot_ps"], NU * l + u + 1)
                    s5 = src[:, 0:N_SAMPLE]
                    st.do(tt(RT, PS[:, 2, :], sin_t, ALU.mult))
                    st.link(tt(s5, s5, cos_t, ALU.mult))
                    tt(s5, s5, RT, ALU.add).then_inc(S["rope_done"], 1)
                    dve.wait_ge(S["rope_done"], NU * l + u + 1)
                convolve(EARLY_TAPS, TAPS)
                dve.drain().then_inc(S["conv_done"], 1)

            def attention(l):
                def maxima(i):
                    t, h = STEPS[i]
                    dve.wait_ge(S["s_ps"], NS * l + i + 1)
                    if i >= 4:
                        dve.wait_ge(S["p_ready"], NS * l + i - 3)
                    st.link(dve.reduce_max(smax[:, i % 4:i % 4 + 1], pair(i % 2)[:, 0:keys_of(t)[1]], AX.X))
                    ts(nmax[:, i % 4:i % 4 + 1], smax[:, i % 4:i % 4 + 1], -0.125, None, ALU.mult)\
                        .then_inc(S["nmax_ready"], 1)

                def evacuate(i):
                    dve.wait_ge(S["pt_ps"], NS * l + i + 1)
                    if i >= 2:
                        dve.wait_ge(S["o_ps"], NS * l + i - 1)
                    nk = keys_of(STEPS[i][0])[1]
                    dve.tensor_copy(PRT[:, i % 2, 0:nk], pair(2)[:, 0:nk]).then_inc(S["pt_dve"], 1)

                def normalise(t):
                    dve.wait_ge(S["o_ps"], NS * l + 8 * t + 8)
                    if t:
                        dve.wait_ge(S["ot_ps"], NT * l + t)
                    st.link(dve.reciprocal(prec[:, :], psum_p[:, t % 2, :]))
                    tt(OTOK.rearrange("p (h e) -> p h e", h=8), PS[:, 6, :].rearrange("p (h e) -> p h e", h=8),
                       prec[:, :].unsqueeze(2).to_broadcast([P, 8, 64]), ALU.mult).then_inc(S["o_ready"], 1)

                for i in range(NS + 3):
                    if i < NS:
                        maxima(i)
                    if 2 <= i < NS + 2 and i % 2:
                        evacuate(i - 2)
                    if i >= 10 and i % 8 == 2:
                        normalise((i - 10) // 8)

            def gla(l):
                for i in range(4):
                    dve.wait_ge(S["ln_done"], l + 1)
                    st.do(stt(LA[:, i, :], LA[:, i, :], 0.0, LZ[:, i, :], ALU.min, ALU.subtract))
                st.after(st.n)
                for ct in range(2):
                    dve.wait_ge(S["cx_mean"], 2 * l + ct + 1)
                    tt(CX[:, ct, :], CX[:, ct, :], pair(ct)[:, 0:NTOK], ALU.subtract).then_inc(S["cx_cent"], 1)
                for i in range(4):
                    b = QD[:, i, :]
                    st.link(dve.tensor_tensor_scan(b, scan_keep, LA[:, i, :], 0.0, ALU.mult, ALU.add))
                    bch = b.rearrange("p (c s) -> p c s", c=NCH)
                    lch = LA[:, i, :].rearrange("p (c s) -> p c s", c=NCH)
                    kch = KK[:, i, :].rearrange("p (c s) -> p c s", c=NCH)
                    total = bch[:, :, CHUNK - 1:CHUNK].to_broadcast([P, NCH, CHUNK])
                    st.do(dve.tensor_copy(e_last[:, i, :].unsqueeze(2), bch[:, :, CHUNK - 1:CHUNK]))
                    if i < 2:
                        st.do(tt(kch, total, bch, ALU.subtract))
                        st.link(dve.tensor_copy(LA[:, i, :], b))
                    else:
                        st.link(tt(kch, bch, lch, ALU.subtract))
                        st.link(tt(lch, total, kch, ALU.subtract))
                    dve.sem_inc(S["b_ready"], 1)
                for ct in range(2):
                    dve.wait_ge(S["cx_sd"], 2 * l + ct + 1)
                    st.link(dve.reciprocal(CSQ[:, ct, :], CSQ[:, ct, :]))
                    stt(CX[:, ct, :], CX[:, ct, :], vec[:, R_CNG + ct:R_CNG + ct + 1], CSQ[:, ct, :],
                        ALU.mult, ALU.mult).then_inc(S["cx_ready"], 1)
                for i in range(4):
                    hp = i % 2
                    dve.wait_ge(S["ex_done"], 4 * l + i + 1)
                    st.do(stt(QD[:, i, :], GQ[:, hp, :], 0.125, QD[:, i, :], ALU.mult, ALU.mult))
                    st.do(tt(KD[:, i, :], GK[:, hp, :], KD[:, i, :], ALU.mult))
                    tt(KK[:, i, :], GK[:, hp, :], KK[:, i, :], ALU.mult).then_inc(S["qk_ready"], 1)
                dve.wait_ge(S["el_ready"], l + 1)
                dve.wait_ge(S["st_in"], 16 * 8 * (l + 1))
                for u, (i, ch, nxt) in enumerate(UPD):
                    dve.wait_ge(S["dS_ps"], NUPD * l + u + 1)
                    if u >= 4:
                        dve.wait_ge(S["st_ready"], NUPD * l + u - 3)
                    for hb in range(2):
                        q = slice(64 * hb, 64 * hb + 64)
                        ins = stt(ST[q, i, nxt, q], ST[q, i, ch, q], e_last[q, i, ch:ch + 1],
                                  PS[q, u % 8, q], ALU.mult, ALU.add)
                    ins.then_inc(S["st_ready"], 1)
                for s in range(2 * NT):
                    dve.wait_ge(S["a_ps"], 2 * NT * l + s + 1)
                    if s >= 2:
                        dve.wait_ge(S["og_ps"], 2 * NT * l + s - 1)
                    for hb in range(2):
                        ins = tt(ATM[:, s % 2, hb, :, :],
                                 PS[:, 4 + 2 * (s % 2) + hb, 0:256].rearrange("p (d i) -> p d i", d=2), masks, ALU.mult)
                    ins.then_inc(S["atm_ready"], 1)
                for hp in range(2):
                    dve.wait_ge(S["og_sd"], 2 * l + hp + 1)
                    st.link(dve.reciprocal(OSD[:, hp, :], OSD[:, hp, :]))
                    st.link(stt(OG[:, hp, :], OG[:, hp, :], vec[:, R_GLG + hp:R_GLG + hp + 1], OSD[:, hp, :],
                                ALU.mult, ALU.mult))
                    tt(MIX[:, hp, :], OG[:, hp, :], GG[:, hp, :], ALU.mult)

            def normed(l, t):
                if t >= 2:
                    dve.wait_ge(S["h2t_ps"], NT * l + t - 1)
                h, g = H2[:, t % 2, :], group_of(t)
                st.link(stt(h, X[:, t, :], rstd[:, t:t + 1], MOD2[:, 1, g, :], ALU.mult, ALU.mult))
                tt(h, h, MOD2[:, 0, g, :], ALU.add).then_inc(S["h2_ready"], 1)

            def top16(vals, inds, src, spare):
                dve.max(vals[:, 0:8], src)
                dve.drain()
                dve.max_index(inds[:, 0:8], vals[:, 0:8], src)
                dve.match_replace(spare, vals[:, 0:8], src, -3.0e38)
                dve.drain()
                dve.max(vals[:, 8:16], spare)
                dve.drain()
                dve.max_index(inds[:, 8:16], vals[:, 8:16], spare)

            def route(l, head):
                dve.wait_ge(S["sc_now"], head + 1)
                dve.sem_inc(S["dve_turn"], 1)
                for s in range(2):
                    top16(top_v[:, s, :], top_i[:, s, :], SCC[:, s, :], SC2[:, s, :])
                dve.drain().then_inc(S["sc_taken"], 1)
                tt(CAND.rearrange("p (a b) -> p a b", a=16), top_v[:, 0, :].unsqueeze(2).to_broadcast([P, 16, 16]),
                   top_v[:, 1, :].unsqueeze(1).to_broadcast([P, 16, 16]), ALU.add)
                dve.tensor_copy(top_if[:, :, :], top_i[:, :, :])
                dve.drain()
                top16(best[:, :], pos[:, :], CAND, CAND2)
                dve.drain()
                ts(centred[:, :], best[:, :], best[:, 0:1], None, ALU.subtract)
                ts(pos2[:, 0, :], pos[:, :], 4, None, ALU.logical_shift_right)
                ts(pos2[:, 1, :], pos[:, :], 15, None, ALU.bitwise_and)
                dve.drain()
                dve.tensor_copy(pos_f[:, :, :], pos2[:, :, :])
                dve.drain()
                oh = OH.rearrange("p (a b) -> p a b", a=32)
                oh4 = OH.rearrange("p (s a b) -> p s a b", s=2, a=16)
                tt(oh, pos_f[:, :, :].rearrange("p s k -> p (s k)").unsqueeze(2).to_broadcast([P, 32, 16]),
                   iota16.unsqueeze(1).to_broadcast([P, 32, 16]), ALU.is_equal)
                dve.drain()
                tt(oh4, oh4, top_if[:, :, :].unsqueeze(2).to_broadcast([P, 2, 16, 16]), ALU.mult)
                dve.drain()
                dve.reduce_sum(chosen[:, :, :].rearrange("p s k -> p (s k)"), oh, AX.X)
                dve.drain()
                stt(chosen_e[:, :], chosen[:, 0, :], float(NKEYS), chosen[:, 1, :], ALU.mult, ALU.add)
                dve.drain()
                ts(idx_u[:, :], chosen_e[:, :], float(EXPERTS * l), None, ALU.add).then_inc(S["idx_ready"], 1)

            def head_dots(head):
                for k in range(TOPK):
                    if k == 9:
                        dve.wait_ge(S["v_free"], head * TOPK + RING)
                        dve.tensor_copy(idx_v[:, :], idx_u[:, :]).then_inc(S["idxv_ready"], 1)
                    dve.wait_ge(u_in[k % RING], head * 32 + 16 * (k // RING + 1))
                    dve.tensor_tensor_reduce(out=UR[:, k % RING, :], in0=UR[:, k % RING, :], in1=pair(1),
                                             scale=1.0, scalar=0.0, op0=ALU.mult, op1=ALU.add,
                                             accum_out=act_h[:, k:k + 1]).then_inc(S["u_free"], 1)
                dve.wait_ge(S["gelu_done"], head + 1)
                dve.sem_inc(S["dve_turn"], 1)
                dve.reciprocal(grec[:, :], gsum[:, :])
                dve.drain()
                stt(w_h[:, :], gelu_h[:, :], grec[:, 0:1], gexp[:, :], ALU.mult, ALU.mult).then_inc(S["w_ready"], 1)

            def residual(l, t):
                dve.wait_ge(S["acc_out"], NT * l + t + 1)
                st.link(tt(TMP, TMP, MOD2[:, 2, group_of(t), :], ALU.mult))
                tt(X[:, t, :], X[:, t, :], TMP, ALU.add).then_inc(S["y_ready"], 1)

            def out_project(l):
                def gated_residual(t):
                    dve.wait_ge(S["mix_ps"], NT * l + t + 1)
                    tt(TMP, pair(t % 2), MOD1[:, 2, group_of(t), :], ALU.mult).then_inc(S["res_read"], 1)
                    dve.wait_ge(S["res_read"], NT * l + t + 1)
                    tt(X[:, t, :], X[:, t, :], TMP, ALU.add).then_inc(S["res_done"], 1)
                    dve.wait_ge(S["res_done"], NT * l + t + 1)

                def reciprocal_rms(first, last, part):
                    dve.wait_ge(S["ss2_done"], 2 * l + part + 1)
                    ts(rstd[:, first:last], sumsq[:, 1, first:last], 1.0 / D, EPS, ALU.mult, ALU.add)\
                        .then_inc(S["ms2_done"], 1)
                    dve.wait_ge(S["sd2_done"], 2 * l + part + 1)
                    st.link(dve.reciprocal(rstd[:, first:last], rms[:, first:last]))

                dve.wait_ge(S["gain2_in"], 16 * (l + 1))
                dve.wait_ge(S["mod2_in"], 32 * (l + 1))
                scale_gain(MOD2, gain2)
                dve.wait_ge(S["gate_in"], 32 * (l + 1))
                gated_residual(0)
                reciprocal_rms(0, 1, 0)
                normed(l, 0)
                gated_residual(1)
                gated_residual(2)
                route(l, HEADS * NT * l)
                for t in (3, 4):
                    gated_residual(t)
                reciprocal_rms(1, NT, 1)

            def peer(l):
                if l == 0:
                    dve.sem_inc(S["u_free"], RING)
                for t in range(NT):
                    n = NT * l + t
                    dve.drain()
                    dve.tensor_copy(pair(1), H2[:, t % 2, :])
                    if t + 1 < NT:
                        normed(l, t + 1)
                    dve.drain()
                    with dve.Fori(0, HEADS if t + 1 < NT else HEADS - 1) as i:
                        head_dots(HEADS * n + i)
                        route(l, HEADS * n + 1 + i)
                        dve.drain()
                    if t + 1 == NT:
                        head_dots(HEADS * n + HEADS - 1)
                    if t:
                        residual(l, t - 1)
                residual(l, NT - 1)

            start()
            for l in range(DEPTH):
                project(l)
                attention(l)
                phase_end(dve, PH * l + 1)
                gla(l)
                phase_end(dve, PH * l + 2)
                out_project(l)
                peer(l)
                phase_end(dve, PH * l + 3)


def shape_constants():
    t = np.zeros((P, C_END), np.float32)
    p = np.arange(P)
    t[:, C_ID:C_ID + P] = np.eye(P)
    t[:, C_MEAN:C_MEAN + P] = (p[:, None] // 64 == p[None, :] // 64) / 64.0
    low = p % 32 < 16
    t[np.where(low, p + 16, p - 16), C_ROT + p] = np.where(low, -1.0, 1.0)
    for kv in range(2):
        t[kv * 64 + p % 64, C_DUP + P * kv + p] = 1.0
    same = p[:, None] // CHUNK == p[None, :] // CHUNK
    t[:, C_MASK:C_MASK + P] = same & (p[:, None] <= p[None, :])
    t[:, C_MASK + P:C_MASK + 2 * P] = same & (p[:, None] >= p[None, :])
    tok = np.arange(N_SAMPLE)
    freq = np.float32(10000.0) ** (-np.arange(16, dtype=np.float32) / np.float32(16))
    where = np.where((p % 64 < 32)[:, None], (tok // 64)[None, :], (tok % 64)[None, :]).astype(np.float32)
    angle = where * freq[p % 16][:, None]
    t[:, C_COS:C_COS + N_SAMPLE] = np.cos(angle)
    t[:, C_SIN:C_SIN + N_SAMPLE] = np.sin(angle)
    t[:, C_SCAN:C_SCAN + NTOK] = np.arange(NTOK) % CHUNK != 0
    t[:, C_ONE:C_ONE + 2] = 1.0
    t[:, C_IOTA:C_IOTA + 16] = np.arange(16)
    return t


_INS = ['x_prompt', 'x_sample', 'c', 'cache_k', 'cache_v', 'state_gla', 'c_ctx', 'ada_w', 'ada_b', 'norm1_g',
        'norm2_g', 'w_in', 'gla_a_w_f', 'gla_a_b_f', 'gla_a_w_b', 'gla_a_b_b', 'gla_norm_g', 'conv_w', 'conv_b',
        'conv_norm_g', 'conv_norm_b', 'q_norm_g', 'k_norm_g', 'w_out', 'peer_wq', 'peer_keys', 'peer_u', 'peer_v']
_OUTS = [(1, 128, 1024), (1, 512, 1024), (1, 2, 128, 2, 64), (1, 2, 128, 2, 64), (1, 2, 2, 4, 64, 64)]


def kernel(**inputs):
    import numpy as _np
    import concourse.bacc as _bacc
    from concourse import mybir as _mybir
    from concourse.bass_utils import run_bass_kernel_spmd as _run

    nc = _bacc.Bacc("TRN2", target_bir_lowering=False, num_devices=1)
    arrays, args = {}, []
    for name in _INS:
        a = _np.ascontiguousarray(inputs[name])
        arrays[f"in_{name}"] = a
        args.append(nc.dram_tensor(f"in_{name}", a.shape, _mybir.dt.from_np(a.dtype), kind="ExternalInput").ap())
    arrays["in_consts"] = shape_constants()
    args.append(nc.dram_tensor("in_consts", (P, C_END), F32, kind="ExternalInput").ap())
    for i, shape in enumerate(_OUTS):
        args.append(nc.dram_tensor(f"out_{i}", shape, F32, kind="ExternalOutput").ap())
    build(nc, *args)
    r = _run(nc, [arrays], core_ids=[0])
    return tuple(r.results[0][f"out_{i}"] for i in range(len(_OUTS)))
```
